# Optimizing a Trainium2 kernel written in Bass

```python
import jax
import jax.numpy as jnp
from jax import lax
import numpy as np

D_MODEL = 1024
BATCH = 1
SEQ = 512
DEPTH = 2
DEC_BATCH = 8
DEC_SEQ = 4
PAST_LEN = 2048
PAGE_SIZE = 128

HEAD_DIM = 64
NSA_W = D_MODEL // 2
GM_W = D_MODEL // 4
POOL_W = D_MODEL // 4
MIX_W = NSA_W + GM_W + POOL_W
N_HEADS = NSA_W // HEAD_DIM
N_KV_HEADS = 2
GROUP = N_HEADS // N_KV_HEADS
CMP_STRIDE = 16
CMP_LEN = 2 * CMP_STRIDE
CMP_HID = HEAD_DIM
SLC_BLOCK = 64
SLC_TOPK = 16
WINDOW = 512
WIN_QB = 128
SLC_QC = 32
FORCE_SCORE = 1.0e4
ROPE_THETA = 10000.0
SCALE = HEAD_DIM ** -0.5
GM_HEADS = GM_W // HEAD_DIM
GM_CHUNK = 128
POOL_GROUPS = 4
POOL_GW = POOL_W // POOL_GROUPS
POOL_WINDOWS = (2, 4, 8, 16)
POOL_HIST = max(POOL_WINDOWS) - 1
D_FF = 256 * ((8 * D_MODEL // 3 + 255) // 256)
ALPHA = (2 * DEPTH) ** 0.25
BETA = (8 * DEPTH) ** -0.25
LN_EPS = 1e-5
Q_W = N_HEADS * HEAD_DIM
KV_W = 2 * N_KV_HEADS * HEAD_DIM
GATE_W = 3 * N_HEADS
SPLITS = [Q_W, Q_W + KV_W, Q_W + 2 * KV_W, Q_W + 3 * KV_W, Q_W + 3 * KV_W + GATE_W, Q_W + 3 * KV_W + GATE_W + 2 * GM_W]
N_IN = SPLITS[-1] + POOL_W

kernel_name = 'nsa_gmlp_pool_hybrid_step'

def _ln(x, g, b):
    xf = x.astype(jnp.float32)
    mu = jnp.mean(xf, -1, keepdims=True)
    var = jnp.mean(jnp.square(xf - mu), -1, keepdims=True)
    return ((xf - mu) * lax.rsqrt(var + LN_EPS) * g + b).astype(x.dtype)

def _swiglu(x, w_in, w_out):
    gate, up = jnp.split(x @ w_in, 2, axis=-1)
    return (jax.nn.silu(gate) * up) @ w_out

def _rope(x, pos):
    half = HEAD_DIM // 2
    inv = ROPE_THETA ** (-jnp.arange(half, dtype=jnp.float32) / half)
    ang = pos.astype(jnp.float32)[:, None] * inv[None, :]
    cos = jnp.cos(ang)[None, :, None, :]
    sin = jnp.sin(ang)[None, :, None, :]
    xf = x.astype(jnp.float32)
    x1, x2 = xf[..., :half], xf[..., half:]
    return jnp.concatenate([x1 * cos - x2 * sin, x1 * sin + x2 * cos], -1).astype(x.dtype)

def _masked_softmax(s, mask):
    s = jnp.where(mask, s.astype(jnp.float32), -1e30)
    return jnp.where(mask, jax.nn.softmax(s, axis=-1), 0.0)

def _attend(q, k, v, mask):
    s = jnp.einsum('btkgd,bskd->bkgts', q, k) * SCALE
    p = _masked_softmax(s, mask)
    return jnp.einsum('bkgts,bskd->btkgd', p.astype(v.dtype), v)

def _win_mask(qpos, kpos):
    d = qpos[:, None] - kpos[None, :]
    return (d >= 0) & (d <= WINDOW) & (kpos[None, :] >= 0)

def _pad_seq(x, mult):
    pad = (-x.shape[1]) % mult
    return jnp.pad(x, [(0, 0), (0, pad)] + [(0, 0)] * (x.ndim - 2))

def _compress(x, pe, w1, w2):
    B, L, K, D = x.shape
    sub = x.reshape(B, L // CMP_STRIDE, CMP_STRIDE, K, D)
    first = jnp.einsum('bnjkd,jde->bnke', sub, w1[:CMP_STRIDE])
    second = jnp.einsum('bnjkd,jde->bnke', sub, w1[CMP_STRIDE:])
    pe_term = jnp.einsum('jd,jde->e', pe, w1)
    hid = jax.nn.gelu(first[:, :-1] + second[:, 1:] + pe_term)
    return jnp.einsum('bnke,ed->bnkd', hid, w2)

def _sel_map(nc, ns):
    c0 = CMP_STRIDE * np.arange(nc)[:, None]
    s0 = SLC_BLOCK * np.arange(ns)[None, :]
    ov = np.clip(np.minimum(c0 + CMP_LEN, s0 + SLC_BLOCK) - np.maximum(c0, s0), 0, None) / CMP_LEN
    return jnp.asarray(ov, dtype=jnp.float32)

def _nsa_keys(k_c, v_c, k_s, v_s, pe, w1, w2):
    B, L = k_c.shape[:2]
    kc = _compress(k_c, pe[0], w1[0], w2[0])
    vc = _compress(v_c, pe[1], w1[1], w2[1])
    nc = kc.shape[1]
    cmp_end = CMP_STRIDE * jnp.arange(nc) + (CMP_LEN - 1)
    ns = L // SLC_BLOCK
    ksb = k_s.reshape(B, ns, SLC_BLOCK, N_KV_HEADS, HEAD_DIM).transpose(0, 3, 1, 2, 4)
    vsb = v_s.reshape(B, ns, SLC_BLOCK, N_KV_HEADS, HEAD_DIM).transpose(0, 3, 1, 2, 4)
    return (kc, vc, cmp_end, ksb, vsb, _sel_map(nc, ns))

def _cmp_slc_attend(q, qpos, kc, vc, cmp_end, ksb, vsb, sel_map):
    B, Tq = q.shape[:2]
    s = jnp.einsum('btkgd,bckd->bkgtc', q, kc) * SCALE
    p = _masked_softmax(s, cmp_end[None, :] <= qpos[:, None])
    o_c = jnp.einsum('bkgtc,bckd->btkgd', p.astype(vc.dtype), vc)
    imp = jnp.einsum('bkgtc,cs->bkts', p, sel_map)
    ns = ksb.shape[2]
    blk = jnp.arange(ns)[None, :]
    cur = (qpos // SLC_BLOCK)[:, None]
    forced = (blk == 0) | (blk == cur) | (blk == cur - 1)
    score = jnp.where(forced, FORCE_SCORE, jnp.where(blk <= cur, imp, -1.0))
    n_sel = min(SLC_TOPK, ns)
    _, idx = lax.top_k(score, n_sel)
    bi = jnp.arange(B)[:, None, None, None]
    ki = jnp.arange(N_KV_HEADS)[None, :, None, None]
    kg = ksb[bi, ki, idx].reshape(B, N_KV_HEADS, Tq, n_sel * SLC_BLOCK, HEAD_DIM)
    vg = vsb[bi, ki, idx].reshape(B, N_KV_HEADS, Tq, n_sel * SLC_BLOCK, HEAD_DIM)
    kpos = (idx[..., None] * SLC_BLOCK + jnp.arange(SLC_BLOCK)).reshape(B, N_KV_HEADS, Tq, n_sel * SLC_BLOCK)
    mask = kpos <= qpos[None, None, :, None]
    s2 = jnp.einsum('btkgd,bktnd->bkgtn', q, kg) * SCALE
    p2 = _masked_softmax(s2, mask[:, :, None])
    o_s = jnp.einsum('bkgtn,bktnd->btkgd', p2.astype(vg.dtype), vg)
    return o_c, o_s

def _cmp_slc_prompt(q, keys):
    B, T = q.shape[:2]
    nq = T // SLC_QC
    qc = jnp.moveaxis(q.reshape(B, nq, SLC_QC, N_KV_HEADS, GROUP, HEAD_DIM), 1, 0)
    qpos = jnp.arange(T).reshape(nq, SLC_QC)
    o_c, o_s = lax.map(lambda a: _cmp_slc_attend(a[0], a[1], *keys), (qc, qpos))
    back = lambda o: jnp.moveaxis(o, 0, 1).reshape(B, T, N_KV_HEADS, GROUP, HEAD_DIM)
    return back(o_c), back(o_s)

def _window_prompt(q, k, v):
    B, T = q.shape[:2]
    nb = T // WIN_QB
    span = WINDOW + WIN_QB
    padw = [(0, 0), (WINDOW, 0), (0, 0), (0, 0)]
    kp = jnp.pad(k, padw)
    vp = jnp.pad(v, padw)
    qb = jnp.moveaxis(q.reshape(B, nb, WIN_QB, N_KV_HEADS, GROUP, HEAD_DIM), 1, 0)

    def block(args):
        qi, i = args
        start = i * WIN_QB
        ks = lax.dynamic_slice_in_dim(kp, start, span, axis=1)
        vs = lax.dynamic_slice_in_dim(vp, start, span, axis=1)
        qpos = start + jnp.arange(WIN_QB)
        kpos = start - WINDOW + jnp.arange(span)
        return _attend(qi, ks, vs, _win_mask(qpos, kpos))

    o = lax.map(block, (qb, jnp.arange(nb)))
    return jnp.moveaxis(o, 0, 1).reshape(B, T, N_KV_HEADS, GROUP, HEAD_DIM)

def _gmlp(u, v, ws, bias):
    B, n = v.shape[:2]
    c = min(n, GM_CHUNK)
    vc = v.reshape(B, n // c, c, GM_HEADS, HEAD_DIM)
    wm = jnp.tril(ws[:, :c, :c])
    s = jnp.einsum('hts,bnshd->bnthd', wm, vc) + bias[:, :c].T[None, None, :, :, None]
    return u * s.reshape(B, n, GM_W)

def _pool(z_ext, pos0, pw, ps):
    n = z_ext.shape[1] - POOL_HIST
    zf = z_ext.astype(jnp.float32)
    cs = jnp.concatenate([jnp.zeros_like(zf[:, :1]), jnp.cumsum(zf, axis=1)], axis=1)
    pos = pos0 + jnp.arange(n)
    cur = zf[:, POOL_HIST:]
    outs = []
    for g, w in enumerate(POOL_WINDOWS):
        sl = slice(g * POOL_GW, (g + 1) * POOL_GW)
        wsum = cs[:, POOL_HIST + 1:POOL_HIST + 1 + n, sl] - cs[:, POOL_HIST + 1 - w:POOL_HIST + 1 - w + n, sl]
        cnt = jnp.minimum(w, pos + 1).astype(jnp.float32)[None, :, None]
        d = (wsum / cnt - cur[..., sl]).astype(z_ext.dtype)
        outs.append(jnp.einsum('btc,ce->bte', d, pw[g]))
    return jnp.concatenate(outs, -1) * ps

def _project(h, w_in, pos):
    B, T = h.shape[:2]
    q, kvc, kvs, kvw, gt, uv, p = jnp.split(h @ w_in, SPLITS, axis=-1)
    q = _rope(q.reshape(B, T, N_HEADS, HEAD_DIM), pos).reshape(B, T, N_KV_HEADS, GROUP, HEAD_DIM)

    def kv(t):
        t = t.reshape(B, T, 2, N_KV_HEADS, HEAD_DIM)
        return _rope(t[:, :, 0], pos), t[:, :, 1]

    gates = jax.nn.sigmoid(gt).reshape(B, T, N_HEADS, 3)
    gu, gv = jnp.split(jax.nn.gelu(uv), 2, axis=-1)
    return q, kv(kvc), kv(kvs), kv(kvw), gates, gu, gv, p

def _gate_merge(gates, o_c, o_s, o_w):
    B, T = gates.shape[:2]
    f = lambda o: o.reshape(B, T, N_HEADS, HEAD_DIM)
    o = gates[..., 0:1] * f(o_c) + gates[..., 1:2] * f(o_s) + gates[..., 2:3] * f(o_w)
    return o.reshape(B, T, NSA_W)

def _mixer_prompt(h, P):
    w_in, w_o, pe, w1, w2, gmg, gmb, ws, gb, pw, ps = P
    B, T = h.shape[:2]
    pos = jnp.arange(T)
    q, (kc_, vc_), (ks_, vs_), (kw_, vw_), gates, gu, gv, p = _project(h, w_in, pos)
    gv = _ln(gv, gmg, gmb)
    keys = _nsa_keys(_pad_seq(kc_, SLC_BLOCK), _pad_seq(vc_, SLC_BLOCK), _pad_seq(ks_, SLC_BLOCK), _pad_seq(vs_, SLC_BLOCK), pe, w1, w2)
    o_c, o_s = _cmp_slc_prompt(q, keys)
    o_w = _window_prompt(q, kw_, vw_)
    o_nsa = _gate_merge(gates, o_c, o_s, o_w)
    o_gm = _gmlp(gu, gv, ws, gb)
    z_ext = jnp.concatenate([jnp.zeros((B, POOL_HIST, POOL_W), p.dtype), p], axis=1)
    o_pool = _pool(z_ext, 0, pw, ps)
    y = jnp.concatenate([o_nsa, o_gm, o_pool], -1) @ w_o
    wb = min(WINDOW, T)
    new = (jnp.stack([kc_, vc_], 2), jnp.stack([ks_, vs_], 2),
           jnp.stack([kw_[:, T - wb:], vw_[:, T - wb:]], 2), p[:, T - POOL_HIST:])
    return y, new

def _mixer_sample(h, pool_c, pool_s, win_buf, pool_buf, page_table, P):
    w_in, w_o, pe, w1, w2, gmg, gmb, ws, gb, pw, ps = P
    B, T = h.shape[:2]
    pos = PAST_LEN + jnp.arange(T)
    q, (kc_, vc_), (ks_, vs_), (kw_, vw_), gates, gu, gv, p = _project(h, w_in, pos)
    gv = _ln(gv, gmg, gmb)

    def full(pool_kv, k_new, v_new):
        past = pool_kv[page_table].reshape(B, -1, 2, N_KV_HEADS, HEAD_DIM)
        k = _pad_seq(jnp.concatenate([past[:, :, 0], k_new], axis=1), SLC_BLOCK)
        v = _pad_seq(jnp.concatenate([past[:, :, 1], v_new], axis=1), SLC_BLOCK)
        return k, v

    kfc, vfc = full(pool_c, kc_, vc_)
    kfs, vfs = full(pool_s, ks_, vs_)
    keys = _nsa_keys(kfc, vfc, kfs, vfs, pe, w1, w2)
    o_c, o_s = _cmp_slc_attend(q, pos, *keys)
    kwb = jnp.concatenate([win_buf[:, :, 0], kw_], axis=1)
    vwb = jnp.concatenate([win_buf[:, :, 1], vw_], axis=1)
    wb = win_buf.shape[1]
    kpos = PAST_LEN - wb + jnp.arange(wb + T)
    o_w = _attend(q, kwb, vwb, _win_mask(pos, kpos))
    o_nsa = _gate_merge(gates, o_c, o_s, o_w)
    o_gm = _gmlp(gu, gv, ws, gb)
    z_ext = jnp.concatenate([pool_buf, p], axis=1)
    o_pool = _pool(z_ext, PAST_LEN, pw, ps)
    y = jnp.concatenate([o_nsa, o_gm, o_pool], -1) @ w_o
    new = (jnp.stack([kc_, vc_], 2), jnp.stack([ks_, vs_], 2),
           jnp.stack([kwb[:, T:], vwb[:, T:]], 2), z_ext[:, T:], gv)
    return y, new

def _layer(x, f_in, f_out, g, b, mixer):
    x = _ln(ALPHA * x + 0.5 * _swiglu(x, f_in[0], f_out[0]), g[0], b[0])
    m, new = mixer(x)
    x = _ln(ALPHA * x + m, g[1], b[1])
    x = _ln(ALPHA * x + 0.5 * _swiglu(x, f_in[1], f_out[1]), g[2], b[2])
    return x, new

def setup_inputs(seed: int = 0) -> dict:
    key = jax.random.key(seed)
    ks = jax.random.split(key, 24)

    def nrm(i, shape, scale):
        return scale * jax.random.normal(ks[i], shape, jnp.float32)

    n_pages = PAST_LEN // PAGE_SIZE
    n_phys = (DEC_BATCH * n_pages * 5) // 4
    w_buf = min(WINDOW, PAST_LEN)
    kv_page = (DEPTH, n_phys, PAGE_SIZE, 2, N_KV_HEADS, HEAD_DIM)
    perm = jax.random.permutation(ks[5], n_phys)
    page_table = perm[:DEC_BATCH * n_pages].reshape(DEC_BATCH, n_pages).astype(jnp.int32)
    return {
        'x_prompt': nrm(0, (BATCH, SEQ, D_MODEL), 1.0),
        'x_sample': nrm(1, (DEC_BATCH, DEC_SEQ, D_MODEL), 1.0),
        'cache_kv_cmp': nrm(2, kv_page, 1.0),
        'cache_kv_slc': nrm(3, kv_page, 1.0),
        'state_kv_win': nrm(4, (DEPTH, DEC_BATCH, w_buf, 2, N_KV_HEADS, HEAD_DIM), 1.0),
        'state_pool': nrm(6, (DEPTH, DEC_BATCH, POOL_HIST, POOL_W), 1.0),
        'page_table': page_table,
        'ln_g': 1.0 + nrm(7, (DEPTH, 3, D_MODEL), 0.02),
        'ln_b': nrm(8, (DEPTH, 3, D_MODEL), 0.02),
        'ffn_w_in': nrm(9, (DEPTH, 2, D_MODEL, 2 * D_FF), D_MODEL ** -0.5),
        'ffn_w_out': nrm(10, (DEPTH, 2, D_FF, D_MODEL), BETA * D_FF ** -0.5),
        'w_in': nrm(11, (DEPTH, D_MODEL, N_IN), D_MODEL ** -0.5),
        'w_o': nrm(12, (DEPTH, MIX_W, D_MODEL), BETA * MIX_W ** -0.5),
        'cmp_pe': nrm(13, (DEPTH, 2, CMP_LEN, HEAD_DIM), 0.1),
        'cmp_w1': nrm(14, (DEPTH, 2, CMP_LEN, HEAD_DIM, CMP_HID), (CMP_LEN * HEAD_DIM) ** -0.5),
        'cmp_w2': nrm(15, (DEPTH, 2, CMP_HID, HEAD_DIM), CMP_HID ** -0.5),
        'gm_ln_g': 1.0 + nrm(16, (DEPTH, GM_W), 0.02),
        'gm_ln_b': nrm(17, (DEPTH, GM_W), 0.02),
        'gm_ws': nrm(18, (DEPTH, GM_HEADS, GM_CHUNK, GM_CHUNK), GM_CHUNK ** -0.5),
        'gm_b': 1.0 + nrm(19, (DEPTH, GM_HEADS, GM_CHUNK), 0.02),
        'pool_w': nrm(20, (DEPTH, POOL_GROUPS, POOL_GW, POOL_GW), POOL_GW ** -0.5),
        'pool_scale': 1.0 + nrm(21, (DEPTH, POOL_W), 0.02),
    }

def reference(x_prompt, x_sample, cache_kv_cmp, cache_kv_slc, state_kv_win, state_pool, page_table,
              ln_g, ln_b, ffn_w_in, ffn_w_out, w_in, w_o, cmp_pe, cmp_w1, cmp_w2,
              gm_ln_g, gm_ln_b, gm_ws, gm_b, pool_w, pool_scale):
    xp, xs = x_prompt, x_sample
    new_p, new_s = [], []
    for l in range(DEPTH):
        P = (w_in[l], w_o[l], cmp_pe[l], cmp_w1[l], cmp_w2[l], gm_ln_g[l], gm_ln_b[l],
             gm_ws[l], gm_b[l], pool_w[l], pool_scale[l])
        xp, st_p = _layer(xp, ffn_w_in[l], ffn_w_out[l], ln_g[l], ln_b[l],
                          lambda h: _mixer_prompt(h, P))
        xs, st_s = _layer(xs, ffn_w_in[l], ffn_w_out[l], ln_g[l], ln_b[l],
                          lambda h: _mixer_sample(h, cache_kv_cmp[l], cache_kv_slc[l], state_kv_win[l],
                                                  state_pool[l], page_table, P))
        new_p.append(st_p)
        new_s.append(st_s)
    stk = lambda lst, i: jnp.stack([t[i] for t in lst])
    return (xp, xs, stk(new_p, 0), stk(new_s, 0), stk(new_p, 1), stk(new_s, 1),
            stk(new_p, 2), stk(new_s, 2), stk(new_p, 3), stk(new_s, 3), stk(new_s, 4))


_drawn_inputs = setup_inputs


def setup_inputs(seed=0):
    import zlib

    import numpy as np

    out = dict(_drawn_inputs(seed))
    spreads = {}
    factors = {'cache_kv_cmp': 3.897,
     'cache_kv_slc': 5.48,
     'cmp_pe': 6.58,
     'gm_ln_g': 21.806,
     'gm_ln_b': 23.248,
     'gm_b': 8.0,
     'pool_scale': 8.0}
    for name, (base, spread) in spreads.items():
        noise = np.random.default_rng([zlib.crc32(name.encode()), seed]).standard_normal(out[name].shape)
        drawn = base * np.exp(spread * noise) if base else spread * noise
        out[name] = jnp.asarray(drawn.astype(out[name].dtype))
    for name, factor in factors.items():
        out[name] = (out[name] * factor).astype(out[name].dtype)
    return out
```

```python
import numpy as np
import concourse.bass as bass
from concourse import mybir
from contextlib import ExitStack

F32 = mybir.dt.float32
BF16 = mybir.dt.bfloat16
I32 = mybir.dt.int32
ACT = mybir.ActivationFunctionType
ALU = mybir.AluOpType
X = mybir.AxisListType.X
ds = bass.ds

P = 128
DEPTH, D, DFF = 2, 1024, 2816
TP, B, TS = 512, 8, 4
NS = B * TS
T = TP + NS
TH = T // 2
KD, KF = D // P, DFF // P
PAST, PAGE, NPG = 2048, 128, 16
HD, SCALE = 64, 64 ** -0.5
ALPHA = (2 * DEPTH) ** 0.25
EPS, NEG = 1e-5, -1e30
CW, NCH = 352, 6
PJW = CW * NCH
C_KV, C_GT, C_U, C_V, C_P = 512, 1280, 1304, 1560, 1816
NT = TP // P
ROWS = [P] * NT + [NS]
NPHYS = B * NPG * 5 // 4
LOT = 8
NW = 4
NC_S, NC_P = PAST // 16 - 1, TP // 16 - 1
NTOP = 13
WINS = (2, 4, 8, 16)
NWI, NWO, NCR = 50, 22, 18
CR_DMAS = 4 * NPG + 1 + 2 * 2 * NPG + 2 * 2 * NPG

CONST = {}
_at = 0
for _n, _w in (("cos", 5 * 32), ("sin", 5 * 32), ("ident", P), ("ones", P), ("cadd", 4 * 31),
               ("wadd", 32), ("nadd", 256), ("selmap", 32), ("band", 4 * 143), ("band0", 4 * 16),
               ("bandh", 4 * 32), ("bandn", 4 * 32), ("tril", P), ("trils", 32), ("idx", 30), ("eps", 1)):
    CONST[_n] = (_at, _w)
    _at += _w
NCONST = _at
PAR = {}
_at = 0
for _n, _w in (("ln", 48), ("gmgb", 512), ("ws", 512), ("gmb", 4), ("wss", 128), ("gmbs", 4), ("pw", 256),
               ("ps", 4), ("w2", 128), ("pe", 32), ("hist", 256)):
    PAR[_n] = (_at, _w)
    _at += _w
NPAR = _at


def at(l, per_layer, n):
    return l * per_layer + n


def build(nc, x_in, wi, wo, cmp_t, slc_k, slc_v, win_k, win_v, win_rows, hist_rows, table, par, consts, tri,
          o_x, o_cmp_p, o_cmp_s, o_slc_p, o_slc_s, o_win_p, o_win_s, o_pool_p, o_pool_s, o_gv):
    ctx = ExitStack()
    sb = lambda n, s, d=F32: ctx.enter_context(nc.sbuf_tensor(n, s, d))
    sem = lambda n: ctx.enter_context(nc.semaphore(n))
    with ctx:
        x = sb("x", [P, KD, T])
        R = sb("R", [P, KD * T])
        WI = sb("WI", [P, 2, 16, P])
        WO = sb("WO", [P, 2, KF * P])
        H = sb("H", [P, KF * T])
        CR = sb("CR", [P, 2, 4096])
        qT = sb("qT", [P, 4, TP])
        kT = sb("kT", [P, 2, TP])
        knew = sb("knew", [P, 2, NS])
        Qblk = sb("Qblk", [P, B, 2, TS, 4])
        kcT = sb("kcT", [P, B, NC_S])
        vc = sb("vc", [P, B, P])
        hidb = sb("hidb", [HD, 4, 2, P])
        OT = sb("OT", [P, 3, 4, NS])
        Z = sb("Z", [P, 3264])
        C = sb("C", [P, NCONST])
        PR = sb("PR", [P, NPAR])
        TRI = sb("TRI", [P, 2, P], BF16)
        peb = sb("peb", [HD, 2])
        sm = sb("sm", [P, 192])
        pt_sb = sb("pt_sb", [1, B * NPG], I32)
        PS = ctx.enter_context(nc.psum_tensor("PS", [P, 8, 512], F32))

        cat = R[:, :].rearrange("p (k t) -> p k t", k=KD)
        h = H[:, :].rearrange("p (k t) -> p k t", k=KF)
        pj = H[:, 0:5 * PJW].rearrange("p (t c) -> p t c", t=5)
        T9 = H[:, 5 * PJW:5 * PJW + 1024].rearrange("p (c h n) -> p c h n", c=2, h=2)
        kcTp = H[:, 5 * PJW + 1024:5 * PJW + 1024 + NC_P]
        vcp = H[0:32, 5 * PJW + 1056:5 * PJW + 1056 + P]
        sil = Z[:, 0:2 * T].rearrange("p (a h t) -> p a h t", a=2, h=2)
        sq = Z[:, 0:T]
        mu, rs = Z[:, 2 * T:3 * T], Z[:, 3 * T:4 * T]
        ysum, qsum = Z[:, 4 * T:5 * T], Z[:, 5 * T:6 * T]
        pbuf = Z[:, 0:1024].rearrange("p (a n) -> p a n", a=2)
        ptbuf = Z[:, 1024:2048].rearrange("p (a n) -> p a n", a=2)
        Madd = Z[:, 2048:3072].rearrange("p (c r) -> p c r", c=NPG)
        colx, diag, rden = Z[:, 0:256], Z[:, 256:512], Z[:, 512:768]
        snew = Z[0:NS, 768:1024]
        selb = Z[:, 1024:1280]
        stmp = Z[:, 1280:1792]
        den, nmx = sm[:, 0:64], sm[:, 64:128]
        w8 = sm[:, 128:136]
        s2 = sm[:, 136:144]
        gst = sm[:, 144:174].rearrange("p (t s) -> p t s", t=5)
        gmv = sm[:, 174:184].rearrange("p (t s) -> p t s", t=5)
        grs = sm[:, 184:189]

        def cst(n, rows=P):
            a, w = CONST[n]
            return C[0:rows, a:a + w]

        def prm(n, rows=P):
            a, w = PAR[n]
            return PR[0:rows, a:a + w]

        ident = cst("ident")
        ones = cst("ones")
        cos = cst("cos").rearrange("p (t d) -> p t d", t=5)
        sin = cst("sin").rearrange("p (t d) -> p t d", t=5)
        lnp = prm("ln").rearrange("p (s a k) -> p s a k", s=3, a=2)
        w1 = WI[:, 0, :, :]
        expand = WI[0:32, 1, :, :]
        w2 = prm("w2", HD).rearrange("p (c d) -> p c d", c=2)

        x_loaded, par_loaded, tab_loaded = sem("x_loaded"), sem("par_loaded"), sem("tab_loaded")
        con_loaded = sem("con_loaded")
        wi_full = [sem("wi_full0"), sem("wi_full1")]
        wo_full = [sem("wo_full0"), sem("wo_full1")]
        cr_full = [sem("cr_full0"), sem("cr_full1")]
        wi_done, wo_done, cr_freed = sem("wi_done"), sem("wo_done"), sem("cr_freed")
        sil_ready, gu_freed = sem("sil_ready"), sem("gu_freed")
        y_ready, y_added, sq_ready = sem("y_ready"), sem("y_added"), sem("sq_ready")
        sums_ready, stats_ready, var_ready, std_ready = (sem("sums_ready"), sem("stats_ready"), sem("var_ready"),
                                                         sem("std_ready"))
        xn_ready, x_ready = sem("xn_ready"), sem("x_ready")
        pj_ready, pj_freed, acts_done = sem("pj_ready"), sem("pj_freed"), sem("acts_done")
        rope_ready, gvar_ready, gstd_ready, gv_ready = (sem("rope_ready"), sem("gvar_ready"), sem("gstd_ready"),
                                                        sem("gv_ready"))
        tr_ready, tr_freed = sem("tr_ready"), sem("tr_freed")
        pe_ready, peb_ready = sem("pe_ready"), sem("peb_ready")
        cm_ready, cm_freed, hp_ready, hid_ready = sem("cm_ready"), sem("cm_freed"), sem("hp_ready"), sem("hid_ready")
        w2_ready, kc_ready = sem("w2_ready"), sem("kc_ready")
        sm_pe, sm_dve, sm_act, sm_toact = sem("sm_pe"), sem("sm_dve"), sem("sm_act"), sem("sm_toact")
        sk_ready, sk_freed = sem("sk_ready"), sem("sk_freed")
        cp_pe, cp_dve, cp_act, cp_toact = sem("cp_pe"), sem("cp_dve"), sem("cp_act"), sem("cp_toact")
        sc_ready, nm_ready, p_ready, pt_ready = sem("sc_ready"), sem("nm_ready"), sem("p_ready"), sem("pt_ready")
        ptc_ready, pv_done, o_freed = sem("ptc_ready"), sem("pv_done"), sem("o_freed")
        gm_ready, gm_done = sem("gm_ready"), sem("gm_done")
        pd_ready, pd_done, pl_ready, pl_done = sem("pd_ready"), sem("pd_done"), sem("pl_ready"), sem("pl_done")
        ct_ready, ct_done = sem("ct_ready"), sem("ct_done")
        stored, out_stored = sem("stored"), sem("out_stored")
        set_up = sem("set_up")
        waited = sem("waited")

        def own(eng):
            eng.sem_inc(waited, 1)

        NST = 14

        block = ctx.enter_context(nc.Block())

        @block.sync
        def _(sp):
            def load_wi(l, s, p):
                sp.wait_ge(wi_done, at(l, NWI, s + 1))
                sp.dma_start(WI[:, p, :, :], wi[ds(l * NWI + s, 1), :, :].rearrange("o p (k n) -> p (o k) n", k=16)
                             ).then_inc(wi_full[p], 16)

            def load_wo(l, s, p):
                sp.wait_ge(wo_done, at(l, NWO, s + 1))
                sp.dma_start(WO[:, p, :], wo[ds(l * NWO + s, 1), :, :].rearrange("o p n -> p (o n)")
                             ).then_inc(wo_full[p], 16)

            def ffn_in(l, bi):
                with sp.Fori(0, KF // 2) as i:
                    for p in range(2):
                        load_wi(l, bi + 2 * i + p, p)

            def ffn_out(l, bo):
                with sp.Fori(0, KD // 2) as i:
                    for p in range(2):
                        load_wo(l, bo + 2 * i + p, p)

            def load_pages(l, first, n, src, p, width):
                with sp.Fori(0, n // LOT) as g:
                    pages = nc.values_load_multi_w_load_instructions(
                        pt_sb[0:1, ds(first + LOT * g, LOT)], engines=[mybir.EngineType.SP],
                        min_val=0, max_val=NPHYS - 1)[1]
                    for j, page in enumerate(pages):
                        sp.dma_start(CR[:, p, ds((LOT * g + j) * width, width)],
                                     src[ds(l * NPHYS + page, 1), :, :].rearrange("o p n -> p (o n)")
                                     ).then_inc(cr_full[p], 16)

            sp.dma_start(pt_sb[:, :], table).then_inc(tab_loaded, 16)
            sp.dma_start(C[:, :], consts).then_inc(con_loaded, 16)
            sp.dma_start(TRI[:, :, :], tri).then_inc(con_loaded, 16)
            sp.dma_start(x[:, :, :], x_in).then_inc(x_loaded, 16)
            sp.wait_ge(tab_loaded, 16)
            own(sp)
            with sp.Fori(0, DEPTH) as l:
                ffn_in(l, 0)
                load_wi(l, KF, 0)
                load_wi(l, KF + 1, 1)
                with sp.Fori(0, B // 2) as i:
                    for p in range(2):
                        b = 2 * i + p
                        load_wo(l, b, p)
                        sp.wait_ge(cr_freed, at(l, NCR, b + 1))
                        own(sp)
                        load_pages(l, b * NPG, NPG, cmp_t, p, 256)
                with sp.Fori(0, NCH // 2) as i:
                    for p in range(2):
                        load_wo(l, KD + 2 * i + p, p)
                for p, src in ((0, win_k), (1, win_v)):
                    sp.wait_ge(cr_freed, at(l, NCR, B + p + 1))
                    sp.dma_start(CR[:, p, :], src[ds(l, 1), :, :].rearrange("o p n -> p (o n)")
                                 ).then_inc(cr_full[p], 16)
                for first, src in ((B + 2, slc_k), (B + 6, slc_v)):
                    with sp.Fori(0, B // 4) as i:
                        for p in range(2):
                            sp.wait_ge(cr_freed, at(l, NCR, first + 1 + 2 * i + p))
                            own(sp)
                            load_pages(l, (2 * i + p) * 2 * NPG, 2 * NPG, src, p, 128)
                with sp.Fori(0, 2) as i:
                    for p in range(2):
                        load_wi(l, KF + 2 + 2 * i + p, p)
                ffn_in(l, KF + 6)
                ffn_out(l, KD + NCH)
            sp.wait_ge(x_ready, 24 * DEPTH + 1)
            sp.dma_start(o_x, x[:, :, :]).then_inc(out_stored, 16)
            sp.wait_ge(out_stored, 16)

        @block.gpsimd
        def _(pool):
            nc.gpsimd.memset(Qblk[:, :, :, :, :], 0.0)
            nc.gpsimd.memset(gmv[:, :, :], 1.0)
            nc.gpsimd.memset(vc[:, :, :], 0.0)
            pool.drain().then_inc(set_up, 1)
            with pool.Fori(0, DEPTH) as l:
                pool.wait_ge(x_ready, at(l, 24, 1))
                own(pool)
                pool.dma_start(PR[:, :], par[ds(l, 1), :, :].rearrange("o p n -> p (o n)")).then_inc(par_loaded, 16)
                pool.wait_ge(pj_freed, at(l, 30, 30 + 5))
                own(pool)
                lw = lambda t, n: t[ds(l, 1)].rearrange(n)
                pool.dma_start(lw(o_pool_p, "o s n -> (o s) n"), pj[P - 15:P, NT - 1, C_P:C_P + 256]).then_inc(stored, 16)
                ops = lw(o_pool_s, "o b s n -> (o b) s n")
                pool.dma_start(ops[:, 0:11, :], lw(hist_rows, "o b s n -> (o b) s n")[:, 4:15, :]).then_inc(stored, 16)
                pool.dma_start(lw(o_pool_s, "o b s n -> (o b) s n")[:, 11:15, :],
                               pj[0:NS, NT, C_P:C_P + 256]).then_inc(stored, 16)
                ows = lw(o_win_s, "o b s n -> (o b) s n")
                pool.dma_start(ows[:, 0:508, :], lw(win_rows, "o b s n -> (o b) s n")[:, 4:512, :]).then_inc(stored, 16)
                pool.wait_ge(rope_ready, at(l, 5, 5))
                own(pool)
                for i, (op, os) in enumerate(((o_cmp_p, o_cmp_s), (o_slc_p, o_slc_s), (o_win_p, None))):
                    c0 = C_KV + 256 * i
                    pool.dma_start(op[ds(l, 1)].rearrange("o (t p) n -> p (o t) n", p=P),
                                   pj[:, 0:NT, c0:c0 + 256]).then_inc(stored, 16)
                    if os is not None:
                        pool.dma_start(lw(os, "o s n -> (o s) n"), pj[0:NS, NT, c0:c0 + 256]).then_inc(stored, 16)
                    else:
                        pool.dma_start(ows[:, 508:512, :], pj[0:NS, NT, c0:c0 + 256]).then_inc(stored, 16)
                pool.wait_ge(gv_ready, at(l, 1, 1))
                own(pool)
                pool.dma_start(lw(o_gv, "o s n -> (o s) n"), pj[0:NS, NT, C_V:C_V + 256]).then_inc(stored, 16)
            pool.wait_ge(stored, 16 * 11 * DEPTH)

        @block.tensor
        def _(pe):
            def mm(out, lhsT, rhs, start, stop):
                return nc.tensor.matmul(out, lhsT, rhs, start=start, stop=stop, skip_group_check=True)

            def ffn_in(l, f, bi, x_at):
                pe.wait_ge(x_ready, at(l, 24, x_at + 1))
                own(pe)
                with pe.Fori(0, KF // 2) as i:
                    for p in range(2):
                        pe.wait_ge(wi_full[p], 16 * (at(l, NWI // 2, bi // 2 + 1) + i))
                        pe.wait_ge(gu_freed, at(l, 44, 22 * f + p + 1) + 2 * i)
                        for side in range(2):
                            for k in range(KD):
                                for a in range(2):
                                    last = mm(PS[:, 4 * p + 2 * side + a, 0:TH], WI[:, p, 8 * side + k, :],
                                              x[:, k, a * TH:(a + 1) * TH], k == 0, k == KD - 1)
                        last.then_inc(wi_done, 1)

            def ffn_out(l, f, bo, y0, beside=None):
                pe.wait_ge(gu_freed, at(l, 44, 22 * (f + 1) + 2))
                own(pe)
                with pe.Fori(0, KD // 2) as i:
                    for p in range(2):
                        pe.wait_ge(wo_full[p], 16 * (at(l, NWO // 2, bo // 2 + 1) + i))
                        pe.wait_ge(y_added, at(l, 24, y0 + p + 1) + 2 * i)
                        if beside:
                            beside(i, p, 0)
                        for k in range(KF):
                            for a in range(2):
                                last = mm(PS[:, 2 * p + a, 0:TH], WO[:, p, k * P:(k + 1) * P],
                                          h[:, k, a * TH:(a + 1) * TH], k == 0, k == KF - 1)
                        last.then_inc(wo_done, 1)
                        if beside:
                            beside(i, p, 1)

            def ln_stats(l, s):
                pe.wait_ge(sums_ready, at(l, 3, s + 1))
                for i, src in enumerate((ysum, qsum)):
                    for a in range(2):
                        last = mm(PS[:, 4 + 2 * i + a, 0:TH], ones, src[:, a * TH:(a + 1) * TH], True, True)
                last.then_inc(stats_ready, 1)

            def project(l):
                pe.wait_ge(x_ready, at(l, 24, 8 + 1))
                own(pe)
                with pe.Fori(0, NCH // 2) as i:
                    for p in range(2):
                        pe.wait_ge(wo_full[p], 16 * (at(l, NWO // 2, KD // 2 + 1) + i))
                        for t in range(5):
                            pe.wait_ge(pj_freed, at(l, 30, 5 * p + t + 1) + 10 * i)
                            for k in range(KD):
                                last = mm(PS[0:ROWS[t], t, 0:CW], x[:, k, t * P:t * P + ROWS[t]],
                                          WO[:, p, k * CW:(k + 1) * CW], k == 0, k == KD - 1)
                            last.then_inc(pj_ready, 1)
                        pe.drain().then_inc(wo_done, 1)

            def rows_to_cols(l):
                pe.wait_ge(rope_ready, at(l, 5, 5))
                for u in range(10):
                    pe.wait_ge(tr_freed, at(l, 10, u + 1))
                    if u >= 8:
                        own(pe)
                    bank = PS[:, 5 + u % 2, :]
                    if u < 8:
                        for t in range(NT):
                            if u < 4:
                                src = pj[:, t, u * P:(u + 1) * P]
                            else:
                                c0 = (C_KV + 256, C_KV + 512, C_KV, C_KV + 128)[u - 4]
                                src = pj[:, t, c0:c0 + P]
                            last = nc.tensor.transpose(bank[:, t * P:(t + 1) * P], src, ident)
                    elif u == 8:
                        for g in range(4):
                            last = nc.tensor.transpose(bank[:, g * NS:(g + 1) * NS], pj[0:NS, NT, g * P:(g + 1) * P],
                                                       ident[0:NS, 0:NS])
                    else:
                        for i in range(2):
                            last = nc.tensor.transpose(bank[:, i * NS:(i + 1) * NS],
                                                       pj[0:NS, NT, C_KV + 256 * (i + 1):C_KV + 256 * (i + 1) + P],
                                                       ident[0:NS, 0:NS])
                    last.then_inc(tr_ready, 1)

            def hidden(v, prompt=False):
                for j in range(8):
                    for kv in range(2 if prompt else 1):
                        if prompt:
                            out = PS[:, 4 + v % 2, kv * 32:kv * 32 + 32]
                            src = T9[:, v, kv, :].rearrange("p (n j) -> p n j", j=8)[:, :, j]
                        else:
                            out = PS[:, 4 + v % 2, 0:256]
                            o = v % 2 * P + j * 16
                            src = CR[:, v // 2, :].rearrange("p (g n) -> p g n", g=NPG)[:, :, o:o + 16]
                        last = mm(out, w1[:, 8 * (v % 2) + j, :], src, j == 0 and kv == 0, j == 7)
                last.then_inc(cm_ready, 1)

            def compressed(base, v, n):
                c, hb = v % 2, hidb[:, 2 + v % 2, :, :]
                pe.wait_ge(hid_ready, base + v + 2)
                pe.wait_ge(kc_ready, base + v + 1)
                own(pe)
                if c == 0:
                    last = mm(PS[0:HD, 6, 0:2 * n], w2[:, 0, :], hb[:, :, 0:n], True, True)
                else:
                    for kv in range(2):
                        last = mm(PS[0:n, 7, kv * HD:(kv + 1) * HD], hb[:, kv, 0:n], w2[:, 1, :], True, True)
                last.then_inc(w2_ready, 1)

            def compress_pe(l):
                pe.wait_ge(wi_full[0], 16 * at(l, NWI // 2, KF // 2 + 1))
                pe.wait_ge(par_loaded, 16 * at(l, 1, 1))
                pe.wait_ge(gu_freed, at(l, 44, 22 + 2))
                pev = prm("pe").rearrange("p (c a j) -> p c a j", c=2, a=2)
                for c in range(2):
                    for a in range(2):
                        for j in range(8):
                            last = mm(PS[0:HD, 7, c:c + 1], w1[:, 8 * c + j, a * HD:(a + 1) * HD],
                                      pev[:, c, a, j:j + 1], (a, j) == (0, 0), (a, j) == (1, 7))
                last.then_inc(pe_ready, 1)
                pe.wait_ge(peb_ready, at(l, 1, 1))

            def compress_beside(l):
                def beside(i, p, after):
                    base = at(l, 18, 0) + 4 * i
                    if not after:
                        pe.wait_ge(cr_full[p], 16 * (at(l, CR_DMAS, NPG) + NPG * i))
                    for v in (2 * p, 2 * p + 1):
                        if after:
                            compressed(base, v, NC_S)
                        else:
                            pe.wait_ge(cm_freed, base + v + 1)
                            hidden(v)
                    if not after:
                        pe.drain().then_inc(cr_freed, 1)
                return beside

            def compress_prompt(l):
                base = at(l, 18, 16)
                pe.wait_ge(tr_freed, at(l, 10, 10 + 2))
                for v in range(2):
                    pe.wait_ge(cm_freed, base + v + 1)
                    hidden(v, True)
                pe.drain().then_inc(wi_done, 1)
                for v in range(2):
                    compressed(base, v, NC_P)

            def sample_softmax_and_pv(l, s0, d0, state_pv, br):
                pe.wait_ge(sm_dve, at(l, 18, d0))
                for a in range(2):
                    last = nc.tensor.transpose(PS[:, 0, a * P:(a + 1) * P], colx[:, a * P:(a + 1) * P], ident)
                last.then_inc(sm_pe, 1)
                pe.wait_ge(sm_dve, at(l, 18, d0 + 1))
                mm(PS[:, 1, 0:256], ones, diag, True, True).then_inc(sm_pe, 1)
                pe.wait_ge(sm_dve, at(l, 18, d0 + 2))
                mm(PS[:, 0, 0:256], ones, colx, True, True).then_inc(sm_pe, 1)
                mm(PS[:, 2, 0:256], pj[0:NS, NT, C_KV + 256 * (br + 1) + P:C_KV + 256 * (br + 1) + 2 * P], snew,
                   True, False)
                state_pv()

            def sample_attention(l):
                pe.wait_ge(kc_ready, at(l, 18, 18 + 2))
                for b in range(B):
                    last = mm(PS[0:NC_S, 0, b * 32:(b + 1) * 32], kcT[:, b, :], Qblk[:, b, :, :, :], True, True)
                last.then_inc(sm_pe, 1)
                pe.wait_ge(sm_dve, at(l, 18, 1))
                for a in range(2):
                    last = nc.tensor.transpose(PS[:, 1, a * NC_S:(a + 1) * NC_S], R[0:NC_S, a * P:(a + 1) * P],
                                               ident[0:NC_S, 0:NC_S])
                last.then_inc(sm_pe, 1)
                pe.wait_ge(sm_dve, at(l, 18, 2))
                for a in range(2):
                    last = nc.tensor.transpose(PS[0:NC_S, 0, a * P:(a + 1) * P],
                                               R[:, 256 + a * NC_S:256 + (a + 1) * NC_S], ident)
                last.then_inc(sm_pe, 1)
                pe.wait_ge(sm_dve, at(l, 18, 3))
                mm(PS[0:64, 1, 0:32], R[0:NC_S, 768:832], cst("selmap", NC_S), True, True)
                for b in range(B):
                    last = mm(PS[:, 2, b * 32:(b + 1) * 32], vc[0:NC_S, b, :], R[0:NC_S, 512 + b * 32:544 + b * 32],
                              b == 0, True)
                last.then_inc(sm_pe, 1)
                pe.wait_ge(sm_dve, at(l, 18, 4))
                own(pe)
                nc.tensor.transpose(PS[0:32, 1, 0:64], R[0:64, 832:864], ident[0:64, 0:64]).then_inc(sm_pe, 1)
                pe.wait_ge(sm_dve, at(l, 18, 5))
                pe.wait_ge(wi_full[1], 16 * at(l, NWI // 2, KF // 2 + 1))
                for c in range(NPG):
                    last = mm(PS[:, 3 + c // 8, c % 8 * 64:c % 8 * 64 + 64], expand[:, c, :], R[0:32, 864:928],
                              c % 8 == 0, True)
                last.then_inc(sm_pe, 1)
                pe.drain().then_inc(wi_done, 1)
                pe.wait_ge(cr_full[0], 16 * at(l, CR_DMAS, 4 * NPG + 1))
                for b in range(B):
                    for c in range(NW):
                        last = mm(PS[:, 5 + b // 4, (b % 4 * NW + c) * 32:(b % 4 * NW + c + 1) * 32],
                                  CR[:, 0, b * 512 + c * P:b * 512 + (c + 1) * P], Qblk[:, b, :, :, :],
                                  b % 4 == 0 and c == 0, True)
                last.then_inc(cr_freed, 1)
                mm(PS[0:NS, 7, 0:256], knew[:, 1, :], Qblk[:, :, :, :, :], True, True).then_inc(sm_pe, 1)

                def win_pv():
                    pe.wait_ge(cr_full[1], 16 * at(l, CR_DMAS, 4 * NPG + 1))
                    pw = R[:, 0:1024].rearrange("p (c r) -> p c r", c=NW)
                    for b in range(B):
                        for c in range(NW):
                            last = mm(PS[:, 2, b * 32:(b + 1) * 32], CR[:, 1, (b * NW + c) * P:(b * NW + c + 1) * P],
                                      pw[:, c, b * 32:(b + 1) * 32], False, b == B - 1 and c == NW - 1)
                    last.then_inc(sm_pe, 1)
                    pe.drain().then_inc(cr_freed, 1)

                sample_softmax_and_pv(l, 8, 7, win_pv, 1)
                with pe.Fori(0, 2) as i:
                    for p in range(2):
                        pe.wait_ge(cr_full[p], 16 * (at(l, CR_DMAS, 6 * NPG + 1) + 2 * NPG * i))
                        for q in range(2):
                            v = 2 * p + q
                            pe.wait_ge(sk_freed, at(l, 8, v + 1) + 4 * i)
                            for c in range(NPG):
                                last = mm(PS[:, 5 + q, c * 32:(c + 1) * 32],
                                          CR[:, p, (q * NPG + c) * P:(q * NPG + c + 1) * P],
                                          Qblk[:, ds(4 * i + v, 1), :, :, :], c == 0, True)
                            last.then_inc(sk_ready, 1)
                        pe.drain().then_inc(cr_freed, 1)
                mm(PS[0:NS, 7, 0:256], knew[:, 0, :], Qblk[:, :, :, :, :], True, True).then_inc(sm_pe, 1)

                def slc_pv():
                    ps = R[:, 0:4096].rearrange("p (c r) -> p c r", c=NPG)
                    with pe.Fori(0, 2) as i:
                        for p in range(2):
                            pe.wait_ge(cr_full[p], 16 * (at(l, CR_DMAS, 10 * NPG + 1) + 2 * NPG * i))
                            for q in range(2):
                                for c in range(NPG):
                                    r = ds((4 * i + 2 * p + q) * 32, 32)
                                    last = mm(PS[:, 2, r], CR[:, p, (q * NPG + c) * P:(q * NPG + c + 1) * P],
                                              ps[:, c, r], False, c == NPG - 1)
                            last.then_inc(cr_freed, 1)
                    mm(PS[:, 2, 0:256], pj[0:NS, NT, C_KV + 256 + P:C_KV + 256 + 2 * P], snew, False, True)\
                        .then_inc(sm_pe, 1)

                pe.wait_ge(sm_dve, at(l, 18, 11))
                pe.wait_ge(sm_dve, at(l, 18, 12))
                for a in range(2):
                    last = nc.tensor.transpose(PS[:, 0, a * P:(a + 1) * P], colx[:, a * P:(a + 1) * P], ident)
                last.then_inc(sm_pe, 1)
                pe.wait_ge(sm_dve, at(l, 18, 13))
                mm(PS[:, 1, 0:256], ones, diag, True, True).then_inc(sm_pe, 1)
                pe.wait_ge(sm_dve, at(l, 18, 14))
                mm(PS[:, 0, 0:256], ones, colx, True, True).then_inc(sm_pe, 1)
                mm(PS[:, 2, 0:256], ident, R[:, 4096:4352], True, False)
                slc_pv()
                pe.wait_ge(sm_dve, at(l, 18, 15))
                for br in range(3):
                    for g in range(4):
                        last = nc.tensor.transpose(PS[0:NS, 3 + br, g * P:(g + 1) * P], OT[:, br, g, :], ident)
                last.then_inc(sm_pe, 1)

            def prompt_compressed(l):
                pe.wait_ge(sm_dve, at(l, 18, 18))
                for t in range(NT):
                    for hh in range(8):
                        g, kv = hh // 2, hh % 2
                        last = mm(PS[:, 4 * kv + t, g * NC_P:(g + 1) * NC_P],
                                  qT[kv * HD:kv * HD + HD, g, t * P:(t + 1) * P],
                                  kcTp[kv * HD:kv * HD + HD, :], g == 0, True)
                last.then_inc(cp_pe, 1)
                for t in range(NT):
                    pe.wait_ge(cp_dve, at(l, 9, 1 + 2 * t))
                    for hh in range(8):
                        o = 512 + t * 248 + (hh % 2 * 4 + hh // 2) * NC_P
                        last = nc.tensor.transpose(PS[0:NC_P, 4 + hh // 4, hh % 4 * P:(hh % 4 + 1) * P],
                                                   R[:, o:o + NC_P], ident)
                    last.then_inc(cp_pe, 1)
                    pe.wait_ge(cp_dve, at(l, 9, 2 + 2 * t))
                    for hh in range(8):
                        kv = hh % 2
                        last = mm(PS[:, 6, hh * HD:(hh + 1) * HD], R[0:NC_P, 1536 + hh * P:1536 + (hh + 1) * P],
                                  vcp[0:NC_P, kv * HD:kv * HD + HD], hh == 0, True)
                    last.then_inc(cp_pe, 1)

            def prompt_attention(l):
                def unit(u):
                    g8, hh = u // 8, u % 8
                    return g8 // 2, g8 % 2, hh % 2, hh // 2

                def scores(u):
                    t, br, kv, g = unit(u)
                    n = (t + 1) * P
                    if u >= 3:
                        pe.wait_ge(p_ready, at(l, 64, u - 2))
                    r = slice(kv * HD, kv * HD + HD)
                    mm(PS[:, u % 3, 0:n], qT[r, g, t * P:(t + 1) * P], kT[r, br, 0:n], True, False)
                    mm(PS[:, u % 3, n - P:n], TRI[:, 1, :], TRI[:, 0, :], False, True).then_inc(sc_ready, 1)

                def turn(u):
                    t, br, kv, g = unit(u)
                    pe.wait_ge(p_ready, at(l, 64, u + 1))
                    if u >= 2:
                        pe.wait_ge(ptc_ready, at(l, 64, u - 1))
                    for c in range(t + 1):
                        last = nc.tensor.transpose(PS[:, 3 + u % 2, c * P:(c + 1) * P],
                                                   pbuf[:, u % 2, c * P:(c + 1) * P], ident)
                    last.then_inc(pt_ready, 1)

                def times_v(u):
                    t, br, kv, g = unit(u)
                    g8, hh = u // 8, u % 8
                    pe.wait_ge(ptc_ready, at(l, 64, u + 1))
                    if hh == 0 and g8 >= 2:
                        pe.wait_ge(o_freed, at(l, 8, g8 - 1))
                    c0 = C_KV + 256 * (br + 1) + P + kv * HD
                    for c in range(t + 1):
                        last = mm(PS[:, 5 + g8 % 2, hh * HD:(hh + 1) * HD], ptbuf[:, u % 2, c * P:(c + 1) * P],
                                  pj[:, c, c0:c0 + HD], hh == 0 and c == 0, c == t)
                    last.then_inc(pv_done, 1)

                pe.wait_ge(cp_dve, at(l, 9, 9))
                for u in range(64 + 2):
                    if u < 64:
                        scores(u)
                    if 1 <= u <= 64:
                        turn(u - 1)
                    if u >= 2:
                        times_v(u - 2)

            def gating(l):
                pe.wait_ge(gv_ready, at(l, 1, 1))
                for t in range(5):
                    r = ROWS[t]
                    w = (prm("ws") if t < NT else prm("wss", NS)).rearrange("p (h t) -> p h t", h=4)
                    for hh in range(4):
                        last = mm(PS[0:r, t % 2, hh * HD:(hh + 1) * HD] if t < 2 else
                                  PS[0:r, (0, 1, 2, 3, 4)[t], hh * HD:(hh + 1) * HD], w[:, hh, :],
                                  pj[0:r, t, C_V + hh * HD:C_V + (hh + 1) * HD], hh == 0, True)
                    last.then_inc(gm_ready, 1)

            def pooling(l):
                band = cst("band").rearrange("p (g t) -> p g t", g=4)
                band0 = cst("band0").rearrange("p (g t) -> p g t", g=4)
                bandh = cst("bandh", 120).rearrange("p (g t) -> p g t", g=4)
                bandn = cst("bandn", NS).rearrange("p (g t) -> p g t", g=4)
                for g in range(4):
                    c0 = C_P + g * HD
                    if g >= 1:
                        pe.wait_ge(pd_done, at(l, 4, g))
                    for t in range(NT):
                        z = pj[:, t, c0:c0 + HD]
                        if t == 0:
                            mm(PS[0:HD, 5, 0:16], z, band0[:, g, :], True, False)
                            mm(PS[0:HD, 5, 16:P], z, band[:, g, 16:P], False, False)
                        else:
                            mm(PS[0:HD, 5, t * P:(t + 1) * P], z, band[:, g, 0:P], False, False)
                            mm(PS[0:HD, 5, t * P:t * P + 15], pj[:, t - 1, c0:c0 + HD], band[:, g, P:P + 15],
                               False, t == NT - 1)
                    mm(PS[0:HD, 6, 0:NS], pj[0:NS, NT, c0:c0 + HD], bandn[:, g, :], True, False)
                    mm(PS[0:HD, 6, 0:NS], prm("hist", 120)[:, g * HD:(g + 1) * HD], bandh[:, g, :], False, True)\
                        .then_inc(pd_ready, 1)
                    pe.wait_ge(pd_done, at(l, 4, g + 1))
                    if g >= 1:
                        pe.wait_ge(pl_done, at(l, 4, g))
                        own(pe)
                    pw = prm("pw", HD).rearrange("p (g e) -> p g e", g=4)
                    if g == 0:
                        pe.wait_ge(gm_done, at(l, 5, 5))
                        own(pe)
                    for a in range(2):
                        last = mm(PS[0:HD, (7, 4)[a], 0:TH], pw[:, g, :], Z[0:HD, a * TH:(a + 1) * TH], True, True)
                    last.then_inc(pl_ready, 1)

            def turn_rows(l):
                for k in range(6):
                    if k >= 2:
                        pe.wait_ge(ct_done, at(l, 6, k - 1))
                    c0 = k * P if k < 4 else C_U + (k - 4) * P
                    for t in range(NT):
                        nc.tensor.transpose(PS[:, 2 * (k % 2), t * P:(t + 1) * P], pj[:, t, c0:c0 + P], ident)
                    nc.tensor.transpose(PS[:, 2 * (k % 2) + 1, 0:NS], pj[0:NS, NT, c0:c0 + P], ident[0:NS, 0:NS])\
                        .then_inc(ct_ready, 1)

            def mixer_out(l):
                pe.wait_ge(ct_done, at(l, 6, 6))
                pe.wait_ge(pl_done, at(l, 4, 4))
                own(pe)
                with pe.Fori(0, 2) as i:
                    for p in range(2):
                        pe.wait_ge(wi_full[p], 16 * (at(l, NWI // 2, (KF + 2) // 2 + 1) + i))
                        for q in range(2):
                            pe.wait_ge(y_added, at(l, 24, 8 + 2 * p + q + 1) + 4 * i)
                            for k in range(KD):
                                for a in range(2):
                                    last = mm(PS[:, 2 * q + a, 0:TH], WI[:, p, 8 * q + k, :],
                                              cat[:, k, a * TH:(a + 1) * TH], k == 0, k == KD - 1)
                            last.then_inc(y_ready, 1)
                        pe.drain().then_inc(wi_done, 1)

            pe.sem_inc(wi_done, 2)
            pe.sem_inc(w2_ready, 2)
            pe.sem_inc(wo_done, 2)
            pe.sem_inc(cr_freed, 2)
            pe.wait_ge(con_loaded, 32)
            pe.wait_ge(x_loaded, 16)
            pe.wait_ge(set_up, 1)
            own(pe)
            with pe.Fori(0, DEPTH) as l:
                ffn_in(l, 0, 0, 0)
                compress_pe(l)
                ffn_out(l, 0, 0, 0, compress_beside(l))
                ln_stats(l, 0)
                project(l)
                rows_to_cols(l)
                compress_prompt(l)
                sample_attention(l)
                prompt_compressed(l)
                prompt_attention(l)
                pe.wait_ge(o_freed, at(l, 8, 8))
                gating(l)
                pooling(l)
                turn_rows(l)
                mixer_out(l)
                ln_stats(l, 1)
                ffn_in(l, 1, KF + 6, 16)
                ffn_out(l, 1, KD + NCH, 16)
                ln_stats(l, 2)

        @block.scalar
        def _(act):
            def af(out, in_, func, **kw):
                return nc.scalar.activation(out, in_, func, **kw)

            def ffn_in(l, f):
                with act.Fori(0, KF // 2) as i:
                    for p in range(2):
                        act.wait_ge(wi_done, at(l, NWI, (KF + 6) * f + p + 3) + 2 * i)
                        act.wait_ge(gu_freed, at(l, 44, 22 * f + p + 1) + 2 * i)
                        af(sil[:, p, :, :], PS[:, 4 * p:4 * p + 2, 0:TH], ACT.Silu).then_inc(sil_ready, 1)

            def squares(l, s, beside=None):
                with act.Fori(0, KD // 2) as i:
                    for p in range(2):
                        if beside:
                            beside(i, p)
                        act.wait_ge(y_added, at(l, 24, 8 * s + p + 3) + 2 * i)
                        af(sq, x[:, ds(2 * i + p, 1), :].rearrange("p o t -> p (o t)"), ACT.Square)\
                            .then_inc(sq_ready, 1)

            def ln(l, s):
                act.wait_ge(var_ready, at(l, 3, s + 1))
                af(rs, rs, ACT.Sqrt, bias=cst("eps")).then_inc(std_ready, 1)
                act.wait_ge(par_loaded, 16 * at(l, 1, 1))
                for k in range(KD):
                    act.wait_ge(xn_ready, at(l, 24, 8 * s + k + 1))
                    af(x[:, k, :], x[:, k, :], ACT.Identity, bias=lnp[:, s, 1, k:k + 1],
                       scale=lnp[:, s, 0, k:k + 1]).then_inc(x_ready, 1)

            def project(l):
                with act.Fori(0, NCH // 2) as i:
                    for p in range(2):
                        for t in range(5):
                            r = ROWS[t]
                            act.wait_ge(pj_ready, at(l, 30, 5 * p + t + 1) + 10 * i)
                            af(pj[0:r, t, ds(2 * CW * i + CW * p, CW)], PS[0:r, t, 0:CW], ACT.Copy)\
                                .then_inc(pj_freed, 1)
                act.drain()
                for r, ts in ((P, slice(0, NT)), (NS, slice(NT, 5))):
                    af(pj[0:r, ts, C_GT:C_GT + 24], pj[0:r, ts, C_GT:C_GT + 24], ACT.Sigmoid)
                for r, ts in ((P, slice(0, NT)), (NS, slice(NT, 5))):
                    last = af(pj[0:r, ts, C_U:C_U + 512], pj[0:r, ts, C_U:C_U + 512], ACT.Gelu_apprx_tanh)
                last.then_inc(acts_done, 1)

            def gelu(base, v, n):
                act.wait_ge(hp_ready, base + v + 1)
                act.wait_ge(w2_ready, base + v + 1)
                af(hidb[:, 2 + v % 2, :, 0:n], hidb[:, 0, :, 0:n], ACT.Gelu_apprx_tanh,
                   bias=peb[:, v % 2:v % 2 + 1]).then_inc(hid_ready, 1)

            def compress_pe(l):
                act.wait_ge(pe_ready, at(l, 1, 1))
                af(peb[:, :], PS[0:HD, 7, 0:2], ACT.Copy)
                act.drain().then_inc(peb_ready, 1)

            def compress_beside(l):
                def beside(i, p):
                    for v in (2 * p, 2 * p + 1):
                        gelu(at(l, 18, 0) + 4 * i, v, NC_S)
                return beside

            def sample_attention(l):
                act.wait_ge(sm_toact, at(l, 4, 1))
                for a in range(2):
                    last = af(R[:, 256 + a * NC_S:256 + (a + 1) * NC_S], PS[:, 1, a * NC_S:(a + 1) * NC_S], ACT.Exp,
                              bias=s2[:, 2 + a:3 + a], scale=SCALE, accum_out=s2[:, 4 + a:5 + a])
                last.then_inc(sm_act, 1)
                act.wait_ge(sm_toact, at(l, 4, 2))
                af(R[:, 0:1024], R[:, 0:1024], ACT.Exp, scale=SCALE)
                af(snew, snew, ACT.Exp, scale=SCALE).then_inc(sm_act, 1)
                act.wait_ge(sm_toact, at(l, 4, 3))
                af(R[:, 0:4096], R[:, 0:4096], ACT.Exp, scale=SCALE)
                af(snew, snew, ACT.Exp, scale=SCALE).then_inc(sm_act, 1)
                act.wait_ge(sm_toact, at(l, 4, 4))
                af(R[:, 512:512 + 992], R[:, 512:512 + 992], ACT.Exp, scale=SCALE).then_inc(sm_act, 1)

            def prompt_attention(l):
                for u in range(64):
                    n = (u // 16 + 1) * P
                    act.wait_ge(nm_ready, at(l, 64, u + 1))
                    if u >= 2:
                        act.wait_ge(pt_ready, at(l, 64, u - 1))
                    af(pbuf[:, u % 2, 0:n], PS[:, u % 3, 0:n], ACT.Exp, bias=nmx[:, u:u + 1], scale=SCALE,
                       accum_out=den[:, u:u + 1]).then_inc(p_ready, 1)

            def pooling(l):
                for g in range(4):
                    act.wait_ge(pl_ready, at(l, 4, g + 1))
                    for a in range(2):
                        last = af(cat[g % 2 * HD:g % 2 * HD + HD, 6 + g // 2, a * TH:(a + 1) * TH],
                                  PS[0:HD, (7, 4)[a], 0:TH], ACT.Copy, scale=prm("ps", HD)[:, g:g + 1])
                    last.then_inc(pl_done, 1)

            act.sem_inc(hid_ready, 1)
            act.sem_inc(x_ready, 1)
            with act.Fori(0, DEPTH) as l:
                ffn_in(l, 0)
                compress_pe(l)
                squares(l, 0, compress_beside(l))
                ln(l, 0)
                project(l)
                act.wait_ge(gvar_ready, at(l, 1, 1))
                act.wait_ge(con_loaded, 32)
                af(grs, gmv[:, :, 1], ACT.Sqrt, bias=cst("eps")).then_inc(gstd_ready, 1)
                for v in range(2):
                    gelu(at(l, 18, 16), v, NC_P)
                sample_attention(l)
                prompt_attention(l)
                pooling(l)
                squares(l, 1)
                ln(l, 1)
                ffn_in(l, 1)
                squares(l, 2)
                ln(l, 2)

        @block.vector
        def _(dve):
            V = nc.vector

            def settle():
                dve.drain()

            def tt(out, a, b, op):
                return V.tensor_tensor(out, a, b, op)

            def ffn_in(l, f):
                with dve.Fori(0, KF // 2) as i:
                    for p in range(2):
                        dve.wait_ge(sil_ready, at(l, 44, 22 * f + p + 1) + 2 * i)
                        V.scalar_tensor_tensor(h[:, ds(2 * i + p, 1), :].rearrange("p o (a t) -> p (o a) t", a=2),
                                               sil[:, p, :, :], 0.5, PS[:, 4 * p + 2:4 * p + 4, 0:TH],
                                               ALU.mult, ALU.mult).then_inc(gu_freed, 1)

            def add_y(l, s, beside=None):
                V.memset(ysum, 0.0)
                V.memset(qsum, 0.0)
                settle()
                with dve.Fori(0, KD // 2) as i:
                    for p in range(2):
                        if beside:
                            beside(i, p, 0)
                        if s == 1:
                            dve.wait_ge(y_ready, at(l, KD, p + 1) + 2 * i)
                        else:
                            dve.wait_ge(wo_done, at(l, NWO, (KD + NCH) * (s // 2) + p + 3) + 2 * i)
                        xk = x[:, ds(2 * i + p, 1), :].rearrange("p o t -> p (o t)")
                        V.scalar_tensor_tensor(xk.rearrange("p (a t) -> p a t", a=2),
                                               xk.rearrange("p (a t) -> p a t", a=2), ALPHA,
                                               PS[:, 2 * p:2 * p + 2, 0:TH], ALU.mult, ALU.add)
                        dve.drain().then_inc(y_added, 1)
                        tt(ysum, ysum, xk, ALU.add)
                        dve.wait_ge(sq_ready, at(l, 24, 8 * s + p + 1) + 2 * i)
                        tt(qsum, qsum, sq, ALU.add)
                        if beside:
                            beside(i, p, 1)
                        settle()
                dve.sem_inc(sums_ready, 1)

            def ln(l, s):
                h2 = lambda a: a.rearrange("p (a t) -> p a t", a=2)
                dve.wait_ge(stats_ready, at(l, 3, s + 1))
                V.tensor_scalar(h2(mu), PS[:, 4:6, 0:TH], 1.0 / D, None, ALU.mult)
                settle()
                tt(rs, mu, mu, ALU.mult)
                settle()
                V.scalar_tensor_tensor(h2(rs), PS[:, 6:8, 0:TH], 1.0 / D, h2(rs), ALU.mult, ALU.subtract)\
                    .then_inc(var_ready, 1)
                dve.wait_ge(std_ready, at(l, 3, s + 1))
                V.reciprocal(rs, rs)
                for k in range(KD):
                    tt(x[:, k, :], x[:, k, :], mu, ALU.subtract)
                    settle()
                    tt(x[:, k, :], x[:, k, :], rs, ALU.mult).then_inc(xn_ready, 1)

            def rope(l):
                dve.wait_ge(pj_freed, at(l, 30, 30 + 5))
                for t in range(5):
                    r = ROWS[t]
                    ta, tb = R[0:r, 0:896], R[0:r, 896:1792]
                    q = pj[0:r, t, 0:512].rearrange("p (n a d) -> p n a d", n=8, a=2)
                    ks = [pj[0:r, t, C_KV + 256 * i:C_KV + 256 * i + P].rearrange("p (n a d) -> p n a d", n=2, a=2)
                          for i in range(3)]
                    parts = [(q, 0, 8)] + [(ks[i], 512 + P * i, 2) for i in range(3)]
                    if t:
                        settle()
                    for src, o, n in parts:
                        for tab, buf in ((cos, ta), (sin, tb)):
                            cs = tab[0:r, t, :].rearrange("p (o d) -> p o d", o=1).to_broadcast([r, 2 * n, 32])
                            tt(buf[:, o:o + n * HD].rearrange("p (m d) -> p m d", d=32),
                               src.rearrange("p n a d -> p (n a) d"), cs, ALU.mult)
                    settle()
                    for src, o, n in parts:
                        a = ta[:, o:o + n * HD].rearrange("p (n a d) -> p n a d", n=n, a=2)
                        b = tb[:, o:o + n * HD].rearrange("p (n a d) -> p n a d", n=n, a=2)
                        tt(src[:, :, 0, :], a[:, :, 0, :], b[:, :, 1, :], ALU.subtract)
                        last = tt(src[:, :, 1, :], a[:, :, 1, :], b[:, :, 0, :], ALU.add)
                    last.then_inc(rope_ready, 1)

            def gv_norm(l):
                dve.wait_ge(par_loaded, 16 * at(l, 1, 1))
                ws = prm("ws").rearrange("p (h t) -> p h t", h=4)
                wss = prm("wss", NS).rearrange("p (h t) -> p h t", h=4)
                for hh in range(4):
                    tt(ws[:, hh, :], ws[:, hh, :], cst("tril"), ALU.mult)
                    tt(wss[:, hh, :], wss[:, hh, :], cst("trils", NS), ALU.mult)
                dve.wait_ge(acts_done, at(l, 1, 1))
                for t in range(5):
                    V.bn_stats(gst[0:ROWS[t], t, :], pj[0:ROWS[t], t, C_V:C_V + 256])
                settle()
                for t in range(5):
                    V.bn_aggr(gmv[0:ROWS[t], t, :], gst[0:ROWS[t], t, :])
                settle()
                dve.sem_inc(gvar_ready, 1)
                dve.wait_ge(gstd_ready, at(l, 1, 1))
                V.reciprocal(grs, grs)
                settle()
                for t in range(5):
                    r = ROWS[t]
                    v = pj[0:r, t, C_V:C_V + 256]
                    V.tensor_scalar(v, v, gmv[0:r, t, 0:1], grs[0:r, t:t + 1], ALU.subtract, ALU.mult)
                settle()
                for op, o in ((ALU.mult, 0), (ALU.add, 256)):
                    for t in range(5):
                        r = ROWS[t]
                        v = pj[0:r, t, C_V:C_V + 256]
                        tt(v, v, prm("gmgb", r)[:, o:o + 256], op)
                    settle()
                dve.sem_inc(gv_ready, 1)

            def rows_to_cols(l):
                for u in range(10):
                    dve.wait_ge(tr_ready, at(l, 10, u + 1))
                    bank = PS[:, 5 + u % 2, :]
                    if u < 4:
                        last = V.tensor_copy(qT[:, u, :], bank)
                    elif u < 6:
                        last = V.tensor_copy(kT[:, u - 4, :], bank)
                    elif u < 8:
                        for kv in range(2):
                            for j in range(2):
                                last = V.tensor_copy(T9[j * HD:(j + 1) * HD, u - 6, kv, :],
                                                     bank[kv * HD:(kv + 1) * HD, :]
                                                     .rearrange("p (n j) -> p n j", j=2)[:, :, j])
                    elif u == 8:
                        for kv in range(2):
                            s = slice(kv * HD, (kv + 1) * HD)
                            last = V.tensor_copy(Qblk[s, :, kv, :, :],
                                                 bank[s, 0:P].rearrange("p (g b t) -> p b t g", g=4, b=B))
                    else:
                        last = V.tensor_copy(knew[:, :, :], bank[:, 0:2 * NS].rearrange("p (a n) -> p a n", a=2))
                    last.then_inc(tr_freed, 1)

            def hidden_sum(base, v, n, pages):
                dve.wait_ge(cm_ready, base + v + 1)
                dve.wait_ge(hid_ready, base + v + 1)
                for half in range(2):
                    s = PS[half * HD:(half + 1) * HD, 4 + v % 2, 0:2 * n]
                    if pages:
                        for kv in range(2):
                            V.tensor_copy(hidb[:, half, kv, 0:n].rearrange("p (g n) -> p g n", g=NPG),
                                          s.rearrange("p (g h n) -> p h g n", g=NPG, h=2)[:, kv, :, :])
                    else:
                        V.tensor_copy(hidb[:, half, :, 0:n], s.rearrange("p (h n) -> p h n", h=2))
                dve.drain().then_inc(cm_freed, 1)
                tt(hidb[:, 0, :, 0:n - 1], hidb[:, 0, :, 0:n - 1], hidb[:, 1, :, 1:n], ALU.add)\
                    .then_inc(hp_ready, 1)

            def compressed(base, v, n, b):
                dve.wait_ge(w2_ready, base + v + 3)
                if v % 2 == 0:
                    for kv in range(2):
                        s = slice(kv * HD, (kv + 1) * HD)
                        out = kcTp[s, :] if b is None else kcT[s, ds(b, 1), :].rearrange("p o n -> p (o n)")
                        last = V.tensor_copy(out, PS[0:HD, 6, kv * n:(kv + 1) * n])
                else:
                    out = vcp[0:n, :] if b is None else vc[0:n, ds(b, 1), :].rearrange("p o n -> p (o n)")
                    last = V.tensor_copy(out, PS[0:n, 7, 0:P])
                last.then_inc(kc_ready, 1)

            def compress_beside(l):
                def beside(i, p, after):
                    for v in (2 * p, 2 * p + 1):
                        if after:
                            compressed(at(l, 18, 0) + 4 * i, v, NC_S, 2 * i + p)
                        else:
                            hidden_sum(at(l, 18, 0) + 4 * i, v, P, True)
                return beside

            def compress_prompt(l):
                for v in range(2):
                    hidden_sum(at(l, 18, 16), v, 32, False)
                for v in range(2):
                    compressed(at(l, 18, 16), v, NC_P, None)

            def take_out(br, scaled):
                for kv in range(2):
                    s = slice(kv * HD, (kv + 1) * HD)
                    for b in range(1):
                        src = PS[s, 2, 0:256].rearrange("p (b h r) -> p b h r", b=B, h=2)[:, :, kv, :]
                        dst = OT[s, br, :, :].rearrange("p g (b t) -> p b t g", b=B)
                        if scaled:
                            rd = rden[s, :].rearrange("p (b h r) -> p b h r", b=B, h=2)[:, :, kv, :]
                            last = tt(dst, src.rearrange("p b (t g) -> p b t g", g=4),
                                      rd.rearrange("p b (t g) -> p b t g", g=4), ALU.mult)
                        else:
                            last = V.tensor_copy(dst, src.rearrange("p b (t g) -> p b t g", g=4))
                return last

            def chunk_softmax(l, n, s0, t0):
                sc = R[:, 0:n * 256].rearrange("p (c r) -> p r c", c=n)
                V.tensor_reduce(colx, sc, X, ALU.max)
                settle()
                tt(colx[0:NS, :], colx[0:NS, :], snew, ALU.max).then_inc(sm_dve, 1)
                dve.wait_ge(sm_pe, at(l, 17, s0 + 1))
                V.tensor_reduce(s2[:, 0:2], PS[:, 0, 0:256].rearrange("p (a n) -> p a n", a=2), X, ALU.max)
                settle()
                for a in range(2):
                    last = V.tensor_scalar(diag[:, a * P:(a + 1) * P], ident, s2[:, a:a + 1], None, ALU.mult)
                last.then_inc(sm_dve, 1)
                dve.wait_ge(sm_pe, at(l, 17, s0 + 2))
                V.tensor_copy(rden, PS[:, 1, 0:256])
                settle()
                sr = R[:, 0:n * 256].rearrange("p (c r) -> p c r", c=n)
                tt(sr, sr, rden.rearrange("p (o r) -> p o r", o=1).to_broadcast([P, n, 256]), ALU.subtract)
                tt(snew, snew, rden[0:NS, :], ALU.subtract)
                settle()
                dve.sem_inc(sm_toact, 1)
                dve.wait_ge(sm_act, at(l, 4, t0))
                V.tensor_reduce(colx, sc, X, ALU.add)
                settle()
                tt(colx[0:NS, :], colx[0:NS, :], snew, ALU.add).then_inc(sm_dve, 1)
                dve.wait_ge(sm_pe, at(l, 17, s0 + 3))
                V.reciprocal(rden, PS[:, 0, 0:256])
                settle()

            def sample_attention(l):
                dve.wait_ge(sm_pe, at(l, 17, 1))
                V.tensor_copy(R[0:NC_S, 0:256], PS[0:NC_S, 0, 0:256]).then_inc(sm_dve, 1)
                dve.wait_ge(sm_pe, at(l, 17, 2))
                V.tensor_reduce(s2[:, 0:2], PS[:, 1, 0:2 * NC_S].rearrange("p (a n) -> p a n", a=2), X, ALU.max)
                settle()
                V.tensor_scalar(s2[:, 2:4], s2[:, 0:2], -SCALE, None, ALU.mult).then_inc(sm_toact, 1)
                dve.wait_ge(sm_act, at(l, 4, 1))
                V.reciprocal(s2[:, 6:8], s2[:, 4:6])
                settle()
                for a in range(2):
                    pr = R[:, 256 + a * NC_S:256 + (a + 1) * NC_S]
                    last = V.tensor_scalar(pr, pr, s2[:, 6 + a:7 + a], None, ALU.mult)
                last.then_inc(sm_dve, 1)
                dve.wait_ge(sm_pe, at(l, 17, 3))
                V.tensor_copy(R[0:NC_S, 512:768], PS[0:NC_S, 0, 0:256])
                settle()
                V.tensor_reduce(R[0:NC_S, 768:832], R[0:NC_S, 512:768].rearrange("p (r g) -> p r g", g=4), X, ALU.add)\
                    .then_inc(sm_dve, 1)
                dve.wait_ge(sm_pe, at(l, 17, 4))
                take_out(0, False)
                imp = R[0:64, 928:960]
                V.tensor_copy(imp, PS[0:64, 1, 0:32])
                settle()
                g3 = R[0:64, 1024:1924].rearrange("p (j i) -> p j i", i=30)
                e3 = R[0:64, 1924:2824].rearrange("p (j i) -> p j i", i=30)
                row = lambda a: a.rearrange("p (o i) -> p o i", o=1).to_broadcast([64, 30, 30])
                col = lambda a: a.rearrange("p (j o) -> p j o", o=1).to_broadcast([64, 30, 30])
                ix = cst("idx", 64)
                cnt, cnt2 = R[0:64, 960:990], R[0:64, 990:1020]
                sel = R[0:64, 832:864]
                tt(g3, row(imp[:, 1:31]), col(imp[:, 1:31]), ALU.is_equal)
                tt(e3, row(ix), col(ix), ALU.is_lt)
                settle()
                tt(e3, e3, g3, ALU.mult)
                settle()
                tt(g3, row(imp[:, 1:31]), col(imp[:, 1:31]), ALU.is_gt)
                settle()
                tt(g3, g3, e3, ALU.add)
                V.memset(sel, 1.0)
                settle()
                V.tensor_reduce(cnt, g3, X, ALU.add)
                settle()
                V.tensor_scalar(sel[:, 1:31], cnt, NTOP - 0.5, None, ALU.is_lt).then_inc(sm_dve, 1)
                dve.wait_ge(sm_pe, at(l, 17, 5))
                V.tensor_copy(R[0:32, 864:928], PS[0:32, 1, 0:64]).then_inc(sm_dve, 1)
                dve.wait_ge(sm_pe, at(l, 17, 6))
                V.tensor_scalar(Madd.rearrange("p (a c) r -> p a (c r)", a=2), PS[:, 3:5, :], 1.0, -NEG,
                                ALU.subtract, ALU.mult)
                settle()
                dve.wait_ge(sm_pe, at(l, 17, 7))
                sw = R[:, 0:1024].rearrange("p (c b r) -> p c b r", c=NW, b=B)
                for a in range(2):
                    V.tensor_copy(sw[:, :, 4 * a:4 * a + 4, :],
                                  PS[:, 5 + a, :].rearrange("p (b c r) -> p c b r", b=4, c=NW))
                tt(snew, PS[0:NS, 7, 0:256], cst("nadd", NS), ALU.add)
                settle()
                tt(sw[:, 0, :, :], sw[:, 0, :, :],
                   cst("wadd").rearrange("p (o r) -> p o r", o=1).to_broadcast([P, B, 32]), ALU.add)
                settle()
                dve.sem_inc(sm_dve, 1)
                chunk_softmax(l, NW, 7, 2)
                dve.sem_inc(sm_dve, 1)
                dve.wait_ge(sm_pe, at(l, 17, 11))
                take_out(2, True)
                settle()
                dve.sem_inc(sm_dve, 1)
                with dve.Fori(0, 4) as i:
                    for q in range(2):
                        dve.wait_ge(sk_ready, at(l, 8, q + 1) + 2 * i)
                        b = 2 * i + q
                        mb = Madd[:, :, ds(b * 8, 8)].rearrange("p c (r o) -> p c r o", o=1)\
                            .to_broadcast([P, NPG, 8, 4])
                        tt(R[:, 0:4096].rearrange("p (c r g) -> p c r g", c=NPG, g=4)[:, :, ds(b * 8, 8), :],
                           PS[:, 5 + q, :].rearrange("p (c r g) -> p c r g", c=NPG, g=4), mb, ALU.add)\
                            .then_inc(sk_freed, 1)
                V.memset(R[:, 4096:4352], 0.0)
                dve.wait_ge(sm_pe, at(l, 17, 12))
                tt(snew, PS[0:NS, 7, 0:256], cst("nadd", NS), ALU.add)
                settle()
                chunk_softmax(l, NPG, 12, 3)
                dve.wait_ge(sm_pe, at(l, 17, 16))
                take_out(1, True)
                settle()
                dve.sem_inc(sm_dve, 1)
                dve.wait_ge(sm_pe, at(l, 17, 17))
                merge(NS, NT, lambda br: PS[0:NS, 3 + br, :].rearrange("p (g h d) -> p g h d", g=4, h=2),
                      Z[0:NS, 0:512])
                settle()
                dve.sem_inc(sm_dve, 3)

            def gate(r, t, br):
                return pj[0:r, t, C_GT:C_GT + 24].rearrange("p (h g b) -> p g h b", h=2, g=4)[:, :, :, br:br + 1]\
                    .to_broadcast([r, 4, 2, HD])

            def merge(r, t, src, tmp):
                out = pj[0:r, t, 0:512].rearrange("p (g h d) -> p g h d", g=4, h=2)
                t4 = tmp.rearrange("p (g h d) -> p g h d", g=4, h=2)
                for br in range(3):
                    tt(out if br == 0 else t4, src(br), gate(r, t, br), ALU.mult)
                    settle()
                    if br:
                        tt(out, out, t4, ALU.add)
                        settle()

            def prompt_compressed(l):
                dve.wait_ge(cp_pe, at(l, 9, 1))
                for t in range(NT):
                    for kv in range(2):
                        o = 512 + t * 248 + kv * 124
                        tt(R[:, o:o + 124].rearrange("p (h n) -> p h n", h=4),
                           PS[:, 4 * kv + t, 0:124].rearrange("p (h n) -> p h n", h=4),
                           cst("cadd")[:, t * 31:(t + 1) * 31].rearrange("p (o n) -> p o n", o=1)
                           .to_broadcast([P, 4, NC_P]), ALU.add)
                settle()
                sc = R[:, 512:512 + 992].rearrange("p (u n) -> p u n", u=32)
                m32 = Z[:, 0:32]
                mb = lambda: m32.rearrange("p (u o) -> p u o", o=1).to_broadcast([P, 32, NC_P])
                V.tensor_reduce(m32, sc, X, ALU.max)
                settle()
                tt(sc, sc, mb(), ALU.subtract)
                settle()
                dve.sem_inc(sm_toact, 1)
                dve.wait_ge(sm_act, at(l, 4, 4))
                V.tensor_reduce(m32, sc, X, ALU.add)
                settle()
                V.reciprocal(m32, m32)
                for t in range(NT):
                    s3 = R[:, 512 + t * 248:512 + (t + 1) * 248].rearrange("p (h n) -> p h n", h=8)
                    V.scalar_tensor_tensor(s3, cst("cadd")[:, t * 31:(t + 1) * 31].rearrange("p (o n) -> p o n", o=1)
                                           .to_broadcast([P, 8, NC_P]), -1.0, s3, ALU.is_ge, ALU.mult)
                settle()
                tt(sc, sc, mb(), ALU.mult).then_inc(cp_dve, 1)
                for t in range(NT):
                    dve.wait_ge(cp_pe, at(l, 9, 2 + 2 * t))
                    V.tensor_copy(R[0:NC_P, 1536:2560].rearrange("p (a n) -> p a n", a=2), PS[0:NC_P, 4:6, :])\
                        .then_inc(cp_dve, 1)
                    dve.wait_ge(cp_pe, at(l, 9, 3 + 2 * t))
                    tt(pj[:, t, 0:512].rearrange("p (g h d) -> p g h d", g=4, h=2),
                       PS[:, 6, :].rearrange("p (g h d) -> p g h d", g=4, h=2), gate(P, t, 0), ALU.mult)\
                        .then_inc(cp_dve, 1)

            def prompt_attention(l):
                def maxima(u):
                    n = (u // 16 + 1) * P
                    dve.wait_ge(sc_ready, at(l, 64, u + 1))
                    V.tensor_reduce(s2[:, u % 2:u % 2 + 1], PS[:, u % 3, 0:n], X, ALU.max)
                    settle()
                    V.tensor_scalar(nmx[:, u:u + 1], s2[:, u % 2:u % 2 + 1], -SCALE, None, ALU.mult)\
                        .then_inc(nm_ready, 1)

                def turned(u):
                    n = (u // 16 + 1) * P
                    dve.wait_ge(pt_ready, at(l, 64, u + 1))
                    if u >= 2:
                        dve.wait_ge(pv_done, at(l, 64, u - 1))
                    V.tensor_copy(ptbuf[:, u % 2, 0:n], PS[:, 3 + u % 2, 0:n]).then_inc(ptc_ready, 1)

                def merged(g8):
                    t, br = g8 // 2, g8 % 2
                    dve.wait_ge(pv_done, at(l, 64, 8 * g8 + 8))
                    V.reciprocal(w8, den[:, 8 * g8:8 * g8 + 8])
                    settle()
                    gt = pj[:, t, C_GT:C_GT + 24].rearrange("p (h g b) -> p g h b", h=2, g=4)[:, :, :, br + 1]
                    w42 = w8.rearrange("p (g h) -> p g h", g=4)
                    tt(w42, w42, gt, ALU.mult)
                    settle()
                    tmp = R[:, 0:512].rearrange("p (h d) -> p h d", h=8)
                    tt(tmp, PS[:, 5 + g8 % 2, :].rearrange("p (h d) -> p h d", h=8),
                       w8.rearrange("p (h o) -> p h o", o=1).to_broadcast([P, 8, HD]), ALU.mult)
                    settle()
                    tt(pj[:, t, 0:512], pj[:, t, 0:512], R[:, 0:512], ALU.add).then_inc(o_freed, 1)

                for u in range(64 + 2):
                    if u < 64:
                        maxima(u)
                    if 1 <= u <= 64:
                        turned(u - 1)
                    if u >= 2 and (u - 2) % 8 == 7:
                        merged((u - 2) // 8)

            def gating(l):
                for t in range(5):
                    r = ROWS[t]
                    dve.wait_ge(gm_ready, at(l, 5, t + 1))
                    b = (prm("gmb") if t < NT else prm("gmbs", NS)).rearrange("p (h o) -> p h o", o=1)\
                        .to_broadcast([r, 4, HD])
                    tmp = Z[0:r, 1088:1344].rearrange("p (h d) -> p h d", h=4)
                    tt(tmp, PS[0:r, t, 0:256].rearrange("p (h d) -> p h d", h=4), b, ALU.add)
                    settle()
                    u = pj[0:r, t, C_U:C_U + 256]
                    tt(u, u, Z[0:r, 1088:1344], ALU.mult).then_inc(gm_done, 1)
                    settle()

            def pooling(l):
                for g in range(4):
                    dve.wait_ge(pd_ready, at(l, 4, g + 1))
                    if g:
                        dve.wait_ge(pl_ready, at(l, 4, g))
                    V.tensor_copy(Z[0:HD, 0:TP], PS[0:HD, 5, :])
                    V.tensor_copy(Z[0:HD, TP:T], PS[0:HD, 6, 0:NS])
                    dve.drain().then_inc(pd_done, 1)

            def turn_rows(l):
                for k in range(6):
                    dve.wait_ge(ct_ready, at(l, 6, k + 1))
                    V.tensor_copy(cat[:, k, 0:TP], PS[:, 2 * (k % 2), :])
                    V.tensor_copy(cat[:, k, TP:T], PS[:, 2 * (k % 2) + 1, 0:NS])
                    dve.drain().then_inc(ct_done, 1)

            for s, n in ((gu_freed, 2), (y_added, 2), (pj_freed, 5), (tr_freed, 2), (cm_freed, 2), (kc_ready, 2),
                         (sk_freed, 2)):
                dve.sem_inc(s, n)
            dve.wait_ge(con_loaded, 32)
            dve.wait_ge(x_loaded, 16)
            dve.wait_ge(set_up, 1)
            own(dve)
            with dve.Fori(0, DEPTH) as l:
                ffn_in(l, 0)
                add_y(l, 0, compress_beside(l))
                ln(l, 0)
                rope(l)
                rows_to_cols(l)
                gv_norm(l)
                compress_prompt(l)
                sample_attention(l)
                prompt_compressed(l)
                prompt_attention(l)
                gating(l)
                pooling(l)
                turn_rows(l)
                add_y(l, 1)
                ln(l, 1)
                dve.wait_ge(stored, 16 * at(l, 11, 11))
                own(dve)
                ffn_in(l, 1)
                add_y(l, 2)
                ln(l, 2)


def constants():
    f = np.float32
    c = np.zeros((P, NCONST), f)

    def put(n, a):
        o, w = CONST[n]
        a = np.asarray(a, f).reshape(a.shape[0], -1)
        c[:a.shape[0], o:o + w] = a

    p = np.arange(P)
    inv = (10000.0 ** (-np.arange(32) / 32)).astype(f)
    pos = np.stack([t * P + p for t in range(NT)] + [PAST + p % TS], 1).astype(f)
    ang = (pos[:, :, None] * inv).astype(f)
    put("cos", np.cos(ang))
    put("sin", np.sin(ang))
    put("ident", np.eye(P))
    put("ones", np.ones((P, P)))
    q = np.stack([t * P + p for t in range(NT)], 1)
    ok = (16 * np.arange(NC_P) + 31)[None, None] <= q[:, :, None]
    put("cadd", np.where(ok, 0.0, NEG))
    r = np.arange(32)
    put("wadd", np.where(p[:, None] >= (r // 4 % 4)[None], 0.0, NEG))
    r = np.arange(256)
    k = np.arange(32)[:, None]
    put("nadd", np.where((k // 4 == r // 32) & (k % 4 <= r // 4 % 4), 0.0, NEG))
    c0, s0 = 16 * np.arange(P)[:, None], 64 * np.arange(32)[None]
    put("selmap", np.clip(np.minimum(c0 + 32, s0 + 64) - np.maximum(c0, s0), 0, None) / 32)
    s, t = p[:, None], np.arange(143)[None]
    put("band", np.stack([((s <= t) & (s > t - w)) / w - (s == t) for w in WINS], 1))
    t = np.arange(16)[None]
    put("band0", np.stack([((s <= t) & (s > t - w)) / np.minimum(w, t + 1) - (s == t) for w in WINS], 1))
    j, rr = np.arange(120)[:, None], np.arange(32)[None]
    put("bandh", np.stack([((j // 15 == rr // 4) & (j % 15 > rr % 4 + 15 - w)) / w for w in WINS], 1))
    put("bandn", np.stack([((k // 4 == rr // 4) & (k % 4 <= rr % 4) & (k % 4 > rr % 4 - w)) / w - (k == rr)
                           for w in WINS], 1))
    put("tril", s <= p[None])
    put("trils", (k // 4 == rr // 4) & (k <= rr))
    put("idx", np.tile(np.arange(30), (P, 1)))
    put("eps", np.full((P, 1), EPS))
    return c


def kernel(**inputs):
    import ml_dtypes
    import concourse.bacc as _bacc
    from concourse.bass_utils import run_bass_kernel_spmd as _run

    a = {n: np.asarray(v) for n, v in inputs.items()}
    f = np.float32
    L = DEPTH
    tok = np.concatenate([a["x_prompt"].reshape(TP, D), a["x_sample"].reshape(NS, D)])
    arr = {"x_in": tok.T.reshape(KD, P, T).transpose(1, 0, 2)}
    wi = np.zeros((L, NWI, P, 16, P), f)
    win = a["ffn_w_in"].reshape(L, 2, KD, P, 2, KF, P).transpose(0, 1, 5, 3, 4, 2, 6).reshape(L, 2, KF, P, 16, P)
    wi[:, 0:KF], wi[:, KF + 6:] = win[:, 0], win[:, 1]
    wi[:, KF] = a["cmp_w1"].reshape(L, 2, 2, 8, 2, HD, HD).transpose(0, 4, 5, 1, 3, 2, 6).reshape(L, P, 16, P)
    for b in range(32):
        wi[:, KF + 1, b, b // 2, b % 2 * 64:b % 2 * 64 + 64] = 1.0
    order = np.arange(D)
    order[:512] = np.arange(512).reshape(2, 4, HD).transpose(1, 0, 2).reshape(-1)
    wi[:, KF + 2:KF + 6] = a["w_o"][:, order].reshape(L, KD, P, 4, 2, P).transpose(0, 3, 2, 4, 1, 5).reshape(L, 4, P, 16, P)
    arr["wi"] = wi.reshape(L * NWI, P, 2048)
    wo = np.zeros((L, NWO, P, KF * P), f)
    wout = a["ffn_w_out"].reshape(L, 2, KF, P, KD, P).transpose(0, 1, 4, 3, 2, 5).reshape(L, 2, KD, P, KF * P)
    wo[:, 0:KD], wo[:, KD + NCH:] = wout[:, 0], wout[:, 1]
    wm = np.zeros((L, D, PJW), f)
    wm[:, :, :a["w_in"].shape[2]] = a["w_in"]
    wm[:, :, :512] = a["w_in"][:, :, order[:512]]
    wo[:, KD:KD + NCH] = wm.reshape(L, KD, P, NCH, CW).transpose(0, 3, 2, 1, 4).reshape(L, NCH, P, KF * P)
    arr["wo"] = wo.reshape(L * NWO, P, KF * P)
    npg = a["cache_kv_cmp"].shape[1]
    arr["cmp_t"] = a["cache_kv_cmp"].reshape(L, npg, 8, 8, 2, 2, 2, HD).transpose(0, 1, 4, 7, 5, 3, 6, 2)\
        .reshape(L * npg, P, 256)
    slc = a["cache_kv_slc"].reshape(L * npg, PAGE, 2, P)
    arr["slc_k"] = slc[:, :, 0].transpose(0, 2, 1)
    arr["slc_v"] = slc[:, :, 1]
    wst = a["state_kv_win"].reshape(L, B, 512, 2, P)
    arr["win_k"] = wst[:, :, :, 0].transpose(0, 3, 1, 2).reshape(L, P, 4096)
    arr["win_v"] = wst[:, :, :, 1].reshape(L, B * NW, P, P).transpose(0, 2, 1, 3).reshape(L, P, 4096)
    arr["win_rows"] = wst.reshape(L, B, 512, 256)
    arr["hist_rows"] = a["state_pool"]
    arr["table"] = a["page_table"].reshape(1, B * NPG).astype(np.int32)
    par = np.zeros((L, P, NPAR), f)

    def put(n, v):
        o, w = PAR[n]
        par[:, :v.shape[1], o:o + w] = v.reshape(L, v.shape[1], w)

    put("ln", np.stack([a["ln_g"], a["ln_b"]], 2).reshape(L, 3, 2, KD, P).transpose(0, 4, 1, 2, 3))
    put("gmgb", np.broadcast_to(np.concatenate([a["gm_ln_g"], a["gm_ln_b"]], 1)[:, None], (L, P, 512)))
    put("ws", a["gm_ws"].transpose(0, 3, 1, 2))
    put("gmb", a["gm_b"].transpose(0, 2, 1))
    wss = np.zeros((L, B, TS, 4, B, TS), f)
    for b in range(B):
        wss[:, b, :, :, b, :] = a["gm_ws"][:, :, :TS, :TS].transpose(0, 3, 1, 2)
    put("wss", wss.reshape(L, NS, P))
    put("gmbs", np.tile(a["gm_b"][:, :, :TS].transpose(0, 2, 1), (1, B, 1)))
    put("pw", a["pool_w"].transpose(0, 2, 1, 3))
    put("ps", a["pool_scale"].reshape(L, 4, HD).transpose(0, 2, 1))
    put("w2", a["cmp_w2"].transpose(0, 2, 1, 3))
    put("pe", a["cmp_pe"].reshape(L, 2, 2, 8, 2, HD).transpose(0, 4, 5, 1, 2, 3).reshape(L, P, 32))
    put("hist", a["state_pool"].reshape(L, B * 15, 256))
    arr["par"] = par
    arr["consts"] = constants()
    q = np.arange(P)
    arr["tri"] = np.stack([np.where(q[None] > q[:, None], NEG, 0.0), np.eye(P)], 1).astype(ml_dtypes.bfloat16)
    outs = {"o_x": (P, KD, T), "o_cmp_p": (L, TP, 256), "o_cmp_s": (L, NS, 256), "o_slc_p": (L, TP, 256),
            "o_slc_s": (L, NS, 256), "o_win_p": (L, TP, 256), "o_win_s": (L, B, 512, 256),
            "o_pool_p": (L, 15, 256), "o_pool_s": (L, B, 15, 256), "o_gv": (L, NS, 256)}
    nc = _bacc.Bacc("TRN2", target_bir_lowering=False, num_devices=1)
    arrays, aps = {}, {}
    for n, v in arr.items():
        v = np.ascontiguousarray(v)
        arrays[n + "_dram"] = v
        aps[n] = nc.dram_tensor(n + "_dram", v.shape, mybir.dt.from_np(v.dtype), kind="ExternalInput").ap()
    for n, s in outs.items():
        aps[n] = nc.dram_tensor(n + "_dram", s, F32, kind="ExternalOutput").ap()
    build(nc, **aps)
    r = _run(nc, [arrays], core_ids=[0]).results[0]
    o = {n: r[n + "_dram"] for n in outs}
    y = o["o_x"].transpose(1, 0, 2).reshape(D, T).T
    kv = lambda n, b, s: o[n].reshape(L, b, s, 2, 2, HD)
    return (y[:TP].reshape(1, TP, D), y[TP:].reshape(B, TS, D), kv("o_cmp_p", 1, TP), kv("o_cmp_s", B, TS),
            kv("o_slc_p", 1, TP), kv("o_slc_s", B, TS), kv("o_win_p", 1, TP), kv("o_win_s", B, 512),
            o["o_pool_p"].reshape(L, 1, 15, 256), o["o_pool_s"], o["o_gv"].reshape(L, B, TS, 256))
```

```python
import numpy as np
import concourse.bass as bass
from concourse import mybir
from contextlib import ExitStack

F32 = mybir.dt.float32
FR = mybir.dt.float32r
BF16 = mybir.dt.bfloat16
I32 = mybir.dt.int32
ACT = mybir.ActivationFunctionType
ALU = mybir.AluOpType
X = mybir.AxisListType.X
ds = bass.ds

P = 128
DEPTH, D, DFF = 2, 1024, 2816
TP, B, TS = 512, 8, 4
NS = B * TS
T = TP + NS
TH = T // 2
KD, KF = D // P, DFF // P
PAST, PAGE, NPG = 2048, 128, 16
HD, SCALE = 64, 64 ** -0.5
ALPHA = (2 * DEPTH) ** 0.25
EPS, NEG = 1e-5, -1e30
CW, NCH = 352, 6
PJW = CW * NCH
C_KV, C_GT, C_U, C_V, C_P = 512, 1280, 1304, 1560, 1816
NT = TP // P
ROWS = [P] * NT + [NS]
SAMPLE_AT = (0, 3, 6, 9, 14, 17, 20, 24, 27, 30, 33, 35, 37, 39, 42, 45, 48, 52, 55, 58, 62)
NPHYS = B * NPG * 5 // 4
LOT = 8
NW = 4
NC_S, NC_P = PAST // 16 - 1, TP // 16 - 1
NTOP = 13
WINS = (2, 4, 8, 16)
NWI, NWO, NCR = 50, 22, 18
CR_DMAS = 4 * NPG + 1 + 2 * 2 * NPG + 2 * 2 * NPG

CONST = {}
_at = 0
for _n, _w in (("cos", 5 * 32), ("sin", 5 * 32), ("ident", P), ("ones", P), ("cadd", 4 * 31),
               ("wadd", 32), ("nadd", 256), ("selmap", 32), ("band", 4 * 143), ("band0", 4 * 16),
               ("bandh", 4 * 32), ("bandn", 4 * 32), ("tril", P), ("trils", 32), ("idx", 30), ("eps", 1)):
    CONST[_n] = (_at, _w)
    _at += _w
NCONST = _at
PAR = {}
_at = 0
for _n, _w in (("ln", 48), ("gmgb", 512), ("ws", 512), ("gmb", 4), ("wss", 128), ("gmbs", 4), ("pw", 256),
               ("ps", 4), ("w2", 128), ("pe", 32), ("hist", 256)):
    PAR[_n] = (_at, _w)
    _at += _w
NPAR = _at


def at(l, per_layer, n):
    return l * per_layer + n


def build(nc, x_in, wi, wo, cmp_t, slc_k, slc_v, win_k, win_v, win_rows, hist_rows, table, par, consts, tri,
          o_x, o_cmp_p, o_cmp_s, o_slc_p, o_slc_s, o_win_p, o_win_s, o_pool_p, o_pool_s, o_gv):
    ctx = ExitStack()
    sb = lambda n, s, d=F32: ctx.enter_context(nc.sbuf_tensor(n, s, d))
    sem = lambda n: ctx.enter_context(nc.semaphore(n))
    with ctx:
        x = sb("x", [P, KD, T])
        N_R, N_Q, N_K, N_C = KD * T, 4 * TP, 2 * TP, 2 * 4096
        at_m = -(-nc.sbuf_base // 32) * 32
        M = sb("M", [P, N_R + N_Q + N_K + N_C + P - NS])
        R = M[:, 0:N_R]
        at_wi = -(-nc.sbuf_base // 32) * 32
        WI = sb("WI", [P, 2, 16, P])
        at_wo = -(-nc.sbuf_base // 32) * 32
        WO = sb("WO", [P, 2, KF * P])
        H = sb("H", [P, KF * T])
        qT = M[:, N_R:N_R + N_Q].rearrange("p (g t) -> p g t", g=4)
        kT = M[:, N_R + N_Q:N_R + N_Q + N_K].rearrange("p (a t) -> p a t", a=2)
        CR = M[:, N_R + N_Q + N_K:N_R + N_Q + N_K + N_C].rearrange("p (a n) -> p a n", a=2)
        XS = N_R + N_Q + N_K + N_C - 2 * KD * T
        over = nc.alloc_sbuf_tensor_at
        wi_hi = over("wi_hi", [P, 2, 16, P], FR, offset=at_m)
        wo_hi = over("wo_hi", [P, 2, KF * P], FR, offset=at_m)
        wi_lo = over("wi_lo", [P, 2, 16, P], FR, offset=at_wi)
        wo_lo = over("wo_lo", [P, 2, KF * P], FR, offset=at_wo)
        xs_flat = over("xs", [P, 2 * KD * T + P - NS], FR, offset=at_m + 4 * XS)
        xs = xs_flat[:, 0:2 * KD * T].rearrange("p (a k t) -> p a k t", a=2, k=KD)
        Qblk = sb("Qblk", [P, B, 2, TS, 4])
        kcT = sb("kcT", [P, B, NC_S])
        vc = sb("vc", [P, B, P])
        hidb = sb("hidb", [HD, 4, 2, P])
        OT = sb("OT", [P, 3, 4, NS])
        Z = sb("Z", [P, 3264])
        C = sb("C", [P, NCONST])
        PR = sb("PR", [P, NPAR])
        TRI = sb("TRI", [P, 2, P], BF16)
        peb = sb("peb", [HD, 2])
        sm = sb("sm", [P, 192])
        pt_sb = sb("pt_sb", [1, B * NPG], I32)
        PS = ctx.enter_context(nc.psum_tensor("PS", [P, 8, 512], F32))

        cat = R[:, :].rearrange("p (k t) -> p k t", k=KD)
        h = H[:, :].rearrange("p (k t) -> p k t", k=KF)
        pj = H[:, 0:5 * PJW].rearrange("p (t c) -> p t c", t=5)
        T9 = H[:, 5 * PJW:5 * PJW + 1024].rearrange("p (c h n) -> p c h n", c=2, h=2)
        kcTp = H[:, 5 * PJW + 1024:5 * PJW + 1024 + NC_P]
        vcp = H[0:32, 5 * PJW + 1056:5 * PJW + 1056 + P]
        knew = H[:, 5 * PJW + 1184:5 * PJW + 1184 + 2 * NS].rearrange("p (a n) -> p a n", a=2)
        sil = Z[:, 0:2 * T].rearrange("p (a h t) -> p a h t", a=2, h=2)
        sq = Z[:, 0:T]
        mu, rs = Z[:, 2 * T:3 * T], Z[:, 3 * T:4 * T]
        ysum, qsum = Z[:, 4 * T:5 * T], Z[:, 5 * T:6 * T]
        pbuf = Z[:, 0:1024].rearrange("p (a n) -> p a n", a=2)
        ptbuf = Z[:, 1024:2048].rearrange("p (a n) -> p a n", a=2)
        Madd = Z[:, 2048:3072].rearrange("p (c r) -> p c r", c=NPG)
        W0 = WI[:, 0, :, :].rearrange("p k n -> p (k n)")
        colx, diag, rden = W0[:, 0:256], W0[:, 256:512], W0[:, 512:768]
        snew = W0[0:NS, 768:1024]
        mtmp = W0[:, 1024:1536]
        den, nmx = sm[:, 0:64], sm[:, 64:128]
        w8 = sm[:, 128:136]
        s2 = sm[:, 136:144]
        row_max = sm[:, 190:192]
        gst = sm[:, 144:174].rearrange("p (t s) -> p t s", t=5)
        gmv = sm[:, 174:184].rearrange("p (t s) -> p t s", t=5)
        grs = sm[:, 184:189]

        pad = Z[:, 0:P - NS]

        def cst(n, rows=P):
            a, w = CONST[n]
            return C[0:rows, a:a + w]

        def prm(n, rows=P):
            a, w = PAR[n]
            return PR[0:rows, a:a + w]

        ident = cst("ident")
        ones = cst("ones")
        cos = cst("cos").rearrange("p (t d) -> p t d", t=5)
        sin = cst("sin").rearrange("p (t d) -> p t d", t=5)
        lnp = prm("ln").rearrange("p (s a k) -> p s a k", s=3, a=2)
        w1 = WI[:, 0, :, :]
        expand = WI[0:32, 1, :, :]
        w2 = prm("w2", HD).rearrange("p (c d) -> p c d", c=2)

        x_loaded, par_loaded, tab_loaded = sem("x_loaded"), sem("par_loaded"), sem("tab_loaded")
        con_loaded = sem("con_loaded")
        wi_full = [sem("wi_full0"), sem("wi_full1")]
        wo_full = [sem("wo_full0"), sem("wo_full1")]
        cr_full = [sem("cr_full0"), sem("cr_full1")]
        wi_done, wo_done, cr_freed = sem("wi_done"), sem("wo_done"), sem("cr_freed")
        sil_ready, gu_freed = sem("sil_ready"), sem("gu_freed")
        y_ready, y_added, sq_ready = sem("y_ready"), sem("y_added"), sem("sq_ready")
        sums_ready, stats_ready, var_ready, std_ready = (sem("sums_ready"), sem("stats_ready"), sem("var_ready"),
                                                         sem("std_ready"))
        xn_ready, x_ready = sem("xn_ready"), sem("x_ready")
        pj_ready, pj_freed, acts_done = sem("pj_ready"), sem("pj_freed"), sem("acts_done")
        rope_ready, gvar_ready, gstd_ready, gv_ready = (sem("rope_ready"), sem("gvar_ready"), sem("gstd_ready"),
                                                        sem("gv_ready"))
        tr_ready, tr_freed = sem("tr_ready"), sem("tr_freed")
        pe_ready, peb_ready = sem("pe_ready"), sem("peb_ready")
        cm_ready, cm_freed, hp_ready, hid_ready = sem("cm_ready"), sem("cm_freed"), sem("hp_ready"), sem("hid_ready")
        w2_ready, kc_ready = sem("w2_ready"), sem("kc_ready")
        sm_pe, sm_dve, sm_act, sm_toact = sem("sm_pe"), sem("sm_dve"), sem("sm_act"), sem("sm_toact")
        sk_ready, sk_freed = sem("sk_ready"), sem("sk_freed")
        cp_pe, cp_dve, cp_act, cp_toact = sem("cp_pe"), sem("cp_dve"), sem("cp_act"), sem("cp_toact")
        sc_ready, nm_ready, p_ready, pt_ready = sem("sc_ready"), sem("nm_ready"), sem("p_ready"), sem("pt_ready")
        ptc_ready, pv_done, o_freed = sem("ptc_ready"), sem("pv_done"), sem("o_freed")
        gm_ready, gm_done = sem("gm_ready"), sem("gm_done")
        pd_ready, pd_done, pl_ready, pl_done = sem("pd_ready"), sem("pd_done"), sem("pl_ready"), sem("pl_done")
        ct_ready, ct_done = sem("ct_ready"), sem("ct_done")
        stored, out_stored = sem("stored"), sem("out_stored")
        set_up = sem("set_up")
        wi_rounded, wi_split = sem("wi_rounded"), sem("wi_split")
        wo_rounded, wo_split = sem("wo_rounded"), sem("wo_split")
        x_split = sem("x_split")
        waited = sem("waited")

        def own(eng):
            eng.sem_inc(waited, 1)

        NST = 14

        block = ctx.enter_context(nc.Block())

        @block.sync
        def _(sp):
            def load_wi(l, s, p):
                sp.wait_ge(wi_done, at(l, NWI, s + 1))
                sp.dma_start(WI[:, p, :, :], wi[ds(l * NWI + s, 1), :, :].rearrange("o p (k n) -> p (o k) n", k=16)
                             ).then_inc(wi_full[p], 16)

            def load_wo(l, s, p):
                sp.wait_ge(wo_done, at(l, NWO, s + 1))
                sp.dma_start(WO[:, p, :], wo[ds(l * NWO + s, 1), :, :].rearrange("o p n -> p (o n)")
                             ).then_inc(wo_full[p], 16)

            def ffn_in(l, bi):
                with sp.Fori(0, KF // 2) as i:
                    for p in range(2):
                        load_wi(l, bi + 2 * i + p, p)

            def ffn_out(l, bo):
                with sp.Fori(0, KD // 2) as i:
                    for p in range(2):
                        load_wo(l, bo + 2 * i + p, p)

            def load_pages(l, first, n, src, p, width):
                with sp.Fori(0, n // LOT) as g:
                    pages = nc.values_load_multi_w_load_instructions(
                        pt_sb[0:1, ds(first + LOT * g, LOT)], engines=[mybir.EngineType.SP],
                        min_val=0, max_val=NPHYS - 1)[1]
                    for j, page in enumerate(pages):
                        sp.dma_start(CR[:, p, ds((LOT * g + j) * width, width)],
                                     src[ds(l * NPHYS + page, 1), :, :].rearrange("o p n -> p (o n)")
                                     ).then_inc(cr_full[p], 16)

            sp.dma_start(pt_sb[:, :], table).then_inc(tab_loaded, 16)
            sp.dma_start(C[:, :], consts).then_inc(con_loaded, 16)
            sp.dma_start(TRI[:, :, :], tri).then_inc(con_loaded, 16)
            sp.dma_start(x[:, :, :], x_in).then_inc(x_loaded, 16)
            sp.wait_ge(tab_loaded, 16)
            own(sp)
            with sp.Fori(0, DEPTH) as l:
                ffn_in(l, 0)
                load_wi(l, KF, 0)
                load_wi(l, KF + 1, 1)
                sp.wait_ge(wi_done, at(l, NWI, KF + 2))
                own(sp)
                with sp.Fori(0, B // 2) as i:
                    for p in range(2):
                        b = 2 * i + p
                        load_wo(l, b, p)
                        sp.wait_ge(cr_freed, at(l, NCR, b + 1))
                        own(sp)
                        load_pages(l, b * NPG, NPG, cmp_t, p, 256)
                with sp.Fori(0, NCH // 2) as i:
                    for p in range(2):
                        load_wo(l, KD + 2 * i + p, p)
                sp.wait_ge(wo_done, at(l, NWO, KD + NCH + 2))
                own(sp)
                for p, src in ((0, win_k), (1, win_v)):
                    sp.wait_ge(cr_freed, at(l, NCR, B + p + 1))
                    sp.dma_start(CR[:, p, :], src[ds(l, 1), :, :].rearrange("o p n -> p (o n)")
                                 ).then_inc(cr_full[p], 16)
                for first, src in ((B + 2, slc_k), (B + 6, slc_v)):
                    with sp.Fori(0, B // 4) as i:
                        for p in range(2):
                            sp.wait_ge(cr_freed, at(l, NCR, first + 1 + 2 * i + p))
                            own(sp)
                            load_pages(l, (2 * i + p) * 2 * NPG, 2 * NPG, src, p, 128)
                with sp.Fori(0, 2) as i:
                    for p in range(2):
                        load_wi(l, KF + 2 + 2 * i + p, p)
                ffn_in(l, KF + 6)
                ffn_out(l, KD + NCH)
            sp.wait_ge(x_ready, 24 * DEPTH + 8 + 1)
            sp.dma_start(o_x, x[:, :, :]).then_inc(out_stored, 16)
            sp.wait_ge(out_stored, 16)

        @block.gpsimd
        def _(pool):
            nc.gpsimd.memset(Qblk[:, :, :, :, :], 0.0)
            nc.gpsimd.memset(gmv[:, :, :], 1.0)
            nc.gpsimd.memset(vc[:, :, :], 0.0)
            nc.gpsimd.memset(pad, 0.0)
            pool.drain()
            nc.gpsimd.tensor_tensor(xs_flat[:, 2 * KD * T:2 * KD * T + P - NS], pad, pad, ALU.subtract)
            pool.drain().then_inc(set_up, 1)
            def low_wi(n, p):
                pool.wait_ge(wi_rounded, n)
                nc.gpsimd.tensor_tensor(wi_lo[:, p, :, :], WI[:, p, :, :], wi_hi[:, p, :, :].bitcast(F32),
                                        ALU.subtract).then_inc(wi_split, 1)

            def low_wo(n, p):
                pool.wait_ge(wo_rounded, n)
                nc.gpsimd.tensor_tensor(wo_lo[:, p, :], WO[:, p, :], wo_hi[:, p, :].bitcast(F32),
                                        ALU.subtract).then_inc(wo_split, 1)

            def low_x(n):
                for k in range(KD):
                    pool.wait_ge(x_ready, n + k)
                    nc.gpsimd.tensor_tensor(xs[:, 1, k, :], x[:, k, :], xs[:, 0, k, :].bitcast(F32),
                                            ALU.subtract).then_inc(x_split, 1)

            low_x(2)
            with pool.Fori(0, DEPTH) as l:
                pool.wait_ge(x_ready, at(l, 24, 8 + 1))
                own(pool)
                pool.dma_start(PR[:, :], par[ds(l, 1), :, :].rearrange("o p n -> p (o n)")).then_inc(par_loaded, 16)
                with pool.Fori(0, KF // 2) as i:
                    for p in range(2):
                        low_wi(at(l, 2 * KF, p + 1) + 2 * i, p)
                low_wo(at(l, NCH, 1), 0)
                low_x(at(l, 24, 8 + 2))
                low_wo(at(l, NCH, 2), 1)
                with pool.Fori(0, NCH // 2 - 1) as i:
                    for p in range(2):
                        low_wo(at(l, NCH, p + 3) + 2 * i, p)
                pool.wait_ge(pj_freed, at(l, 30, 30 + 5))
                own(pool)
                lw = lambda t, n: t[ds(l, 1)].rearrange(n)
                pool.dma_start(lw(o_pool_p, "o s n -> (o s) n"), pj[P - 15:P, NT - 1, C_P:C_P + 256]).then_inc(stored, 16)
                ops = lw(o_pool_s, "o b s n -> (o b) s n")
                pool.dma_start(ops[:, 0:11, :], lw(hist_rows, "o b s n -> (o b) s n")[:, 4:15, :]).then_inc(stored, 16)
                pool.dma_start(lw(o_pool_s, "o b s n -> (o b) s n")[:, 11:15, :],
                               pj[0:NS, NT, C_P:C_P + 256]).then_inc(stored, 16)
                ows = lw(o_win_s, "o b s n -> (o b) s n")
                pool.dma_start(ows[:, 0:508, :], lw(win_rows, "o b s n -> (o b) s n")[:, 4:512, :]).then_inc(stored, 16)
                pool.wait_ge(rope_ready, at(l, 5, 5))
                own(pool)
                for i, (op, os) in enumerate(((o_cmp_p, o_cmp_s), (o_slc_p, o_slc_s), (o_win_p, None))):
                    c0 = C_KV + 256 * i
                    pool.dma_start(op[ds(l, 1)].rearrange("o (t p) n -> p (o t) n", p=P),
                                   pj[:, 0:NT, c0:c0 + 256]).then_inc(stored, 16)
                    if os is not None:
                        pool.dma_start(lw(os, "o s n -> (o s) n"), pj[0:NS, NT, c0:c0 + 256]).then_inc(stored, 16)
                    else:
                        pool.dma_start(ows[:, 508:512, :], pj[0:NS, NT, c0:c0 + 256]).then_inc(stored, 16)
                pool.wait_ge(gv_ready, at(l, 1, 1))
                own(pool)
                pool.dma_start(lw(o_gv, "o s n -> (o s) n"), pj[0:NS, NT, C_V:C_V + 256]).then_inc(stored, 16)
                low_wi(at(l, 2 * KF, KF + 1), 0)
                low_x(at(l, 24, 16 + 2))
                low_wi(at(l, 2 * KF, KF + 2), 1)
                with pool.Fori(0, KF // 2 - 1) as i:
                    for p in range(2):
                        low_wi(at(l, 2 * KF, KF + p + 3) + 2 * i, p)
                low_x(at(l, 24, 24 + 2))
            pool.wait_ge(stored, 16 * 11 * DEPTH)

        @block.tensor
        def _(pe):
            def mm(out, lhsT, rhs, start, stop):
                return nc.tensor.matmul(out, lhsT, rhs, start=start, stop=stop, skip_group_check=True)

            def three(out, ws, xk, first, last):
                for n, (i, j) in enumerate(((0, 0), (0, 1), (1, 0))):
                    r = mm(out, ws[i], xk[j], first and n == 0, last and n == 2)
                return r

            def ffn_in(l, f, bi, x_at):
                with pe.Fori(0, KF // 2) as i:
                    for p in range(2):
                        pe.wait_ge(wi_split, at(l, 2 * KF, KF * f + p + 1) + 2 * i)
                        pe.wait_ge(gu_freed, at(l, 44, 22 * f + p + 1) + 2 * i)
                        for side in range(2):
                            for k in range(KD):
                                if p == 0 and side == 0:
                                    pe.wait_ge(x_split, at(l, 24, x_at + k + 1))
                                for a in range(2):
                                    last = three(PS[:, 4 * p + 2 * side + a, 0:TH],
                                                 [w[:, p, 8 * side + k, :] for w in (wi_hi, wi_lo)],
                                                 [xs[:, part, k, a * TH:(a + 1) * TH] for part in range(2)],
                                                 k == 0, k == KD - 1)
                        last.then_inc(wi_done, 1)

            def ffn_out(l, f, bo, y0, beside=None):
                pe.wait_ge(gu_freed, at(l, 44, 22 * (f + 1) + 2))
                own(pe)
                with pe.Fori(0, KD // 2) as i:
                    for p in range(2):
                        pe.wait_ge(wo_full[p], 16 * (at(l, NWO // 2, bo // 2 + 1) + i))
                        pe.wait_ge(y_added, at(l, 24, y0 + p + 1) + 2 * i)
                        if beside:
                            beside(i, p, 0)
                        for k in range(KF):
                            for a in range(2):
                                last = mm(PS[:, 2 * p + a, 0:TH], WO[:, p, k * P:(k + 1) * P],
                                          h[:, k, a * TH:(a + 1) * TH], k == 0, k == KF - 1)
                        last.then_inc(wo_done, 1)
                        if beside:
                            beside(i, p, 1)

            def ln_stats(l, s):
                pe.wait_ge(sums_ready, at(l, 3, s + 1))
                for i, src in enumerate((ysum, qsum)):
                    for a in range(2):
                        last = mm(PS[:, 4 + 2 * i + a, 0:TH], ones, src[:, a * TH:(a + 1) * TH], True, True)
                last.then_inc(stats_ready, 1)

            def project(l):
                with pe.Fori(0, NCH // 2) as i:
                    for p in range(2):
                        pe.wait_ge(wo_split, at(l, NCH, p + 1) + 2 * i)
                        for t in range(5):
                            pe.wait_ge(pj_freed, at(l, 30, 5 * p + t + 1) + 10 * i)
                            for k in range(KD):
                                if p == 0 and t == 0:
                                    pe.wait_ge(x_split, at(l, 24, 8 + k + 1))
                                last = three(PS[:, t, 0:CW],
                                             [xs_flat[:, o:o + P] for o in (k * T + t * P, (KD + k) * T + t * P)],
                                             [w[:, p, k * CW:(k + 1) * CW] for w in (wo_hi, wo_lo)],
                                             k == 0, k == KD - 1)
                            last.then_inc(pj_ready, 1)
                        pe.drain().then_inc(wo_done, 1)

            def rows_to_cols(l):
                pe.wait_ge(rope_ready, at(l, 5, 5))
                for u in range(10):
                    pe.wait_ge(tr_freed, at(l, 10, u + 1))
                    if u >= 8:
                        own(pe)
                    bank = PS[:, 5 + u % 2, :]
                    if u < 8:
                        for t in range(NT):
                            if u < 4:
                                src = pj[:, t, u * P:(u + 1) * P]
                            else:
                                c0 = (C_KV + 256, C_KV + 512, C_KV, C_KV + 128)[u - 4]
                                src = pj[:, t, c0:c0 + P]
                            last = nc.tensor.transpose(bank[:, t * P:(t + 1) * P], src, ident)
                    elif u == 8:
                        for g in range(4):
                            last = nc.tensor.transpose(bank[:, g * NS:(g + 1) * NS], pj[0:NS, NT, g * P:(g + 1) * P],
                                                       ident[0:NS, 0:NS])
                    else:
                        for i in range(2):
                            last = nc.tensor.transpose(bank[:, i * NS:(i + 1) * NS],
                                                       pj[0:NS, NT, C_KV + 256 * (i + 1):C_KV + 256 * (i + 1) + P],
                                                       ident[0:NS, 0:NS])
                    last.then_inc(tr_ready, 1)

            def hidden(v, prompt=False):
                for j in range(8):
                    for kv in range(2 if prompt else 1):
                        if prompt:
                            out = PS[:, 4 + v % 2, kv * 32:kv * 32 + 32]
                            src = T9[:, v, kv, :].rearrange("p (n j) -> p n j", j=8)[:, :, j]
                        else:
                            out = PS[:, 4 + v % 2, 0:256]
                            o = v % 2 * P + j * 16
                            src = CR[:, v // 2, :].rearrange("p (g n) -> p g n", g=NPG)[:, :, o:o + 16]
                        last = mm(out, w1[:, 8 * (v % 2) + j, :], src, j == 0 and kv == 0, j == 7)
                last.then_inc(cm_ready, 1)

            def compressed(base, v, n):
                c, hb = v % 2, hidb[:, 2 + v % 2, :, :]
                pe.wait_ge(hid_ready, base + v + 2)
                pe.wait_ge(kc_ready, base + v + 1)
                own(pe)
                if c == 0:
                    last = mm(PS[0:HD, 6, 0:2 * n], w2[:, 0, :], hb[:, :, 0:n], True, True)
                else:
                    for kv in range(2):
                        last = mm(PS[0:n, 7, kv * HD:(kv + 1) * HD], hb[:, kv, 0:n], w2[:, 1, :], True, True)
                last.then_inc(w2_ready, 1)

            def compress_pe(l):
                pe.wait_ge(wi_full[0], 16 * at(l, NWI // 2, KF // 2 + 1))
                pe.wait_ge(par_loaded, 16 * at(l, 1, 1))
                pe.wait_ge(gu_freed, at(l, 44, 22 + 2))
                pev = prm("pe").rearrange("p (c a j) -> p c a j", c=2, a=2)
                for c in range(2):
                    for a in range(2):
                        for j in range(8):
                            last = mm(PS[0:HD, 7, c:c + 1], w1[:, 8 * c + j, a * HD:(a + 1) * HD],
                                      pev[:, c, a, j:j + 1], (a, j) == (0, 0), (a, j) == (1, 7))
                last.then_inc(pe_ready, 1)
                pe.wait_ge(peb_ready, at(l, 1, 1))

            def compress_beside(l):
                def beside(i, p, after):
                    base = at(l, 18, 0) + 4 * i
                    if not after:
                        pe.wait_ge(cr_full[p], 16 * (at(l, CR_DMAS, NPG) + NPG * i))
                    for v in (2 * p, 2 * p + 1):
                        if after:
                            compressed(base, v, NC_S)
                        else:
                            pe.wait_ge(cm_freed, base + v + 1)
                            hidden(v)
                    if not after:
                        pe.drain().then_inc(cr_freed, 1)
                return beside

            def compress_prompt(l):
                base = at(l, 18, 16)
                pe.wait_ge(tr_freed, at(l, 10, 10 + 2))
                for v in range(2):
                    pe.wait_ge(cm_freed, base + v + 1)
                    hidden(v, True)
                for v in range(2):
                    compressed(base, v, NC_P)

            def cmp_scores(l):
                pe.wait_ge(kc_ready, at(l, 18, 18 + 2))
                for b in range(B):
                    last = mm(PS[0:NC_S, 6, b * 32:(b + 1) * 32], kcT[:, b, :], Qblk[:, b, :, :, :], b == 0, True)
                last.then_inc(sm_pe, 1)

            def cmp_turn(l):
                pe.wait_ge(sm_dve, at(l, 18, 1))
                for a in range(2):
                    last = nc.tensor.transpose(PS[:, 7, a * NC_S:(a + 1) * NC_S], R[0:NC_S, a * P:(a + 1) * P],
                                               ident[0:NC_S, 0:NC_S])
                last.then_inc(sm_pe, 1)

            def cmp_turn_back(l):
                pe.wait_ge(sm_dve, at(l, 18, 2))
                for a in range(2):
                    last = nc.tensor.transpose(PS[0:NC_S, 6, a * P:(a + 1) * P],
                                               R[:, 256 + a * NC_S:256 + (a + 1) * NC_S], ident)
                last.then_inc(sm_pe, 1)

            def cmp_output(l):
                pe.wait_ge(sm_dve, at(l, 18, 3))
                mm(PS[0:64, 7, 0:32], R[0:NC_S, 768:832], cst("selmap", NC_S), True, True)
                for b in range(B):
                    last = mm(PS[:, 5, b * 32:(b + 1) * 32], vc[0:NC_S, b, :], R[0:NC_S, 512 + b * 32:544 + b * 32],
                              b == 0, True)
                last.then_inc(sm_pe, 1)

            def turn_selection(l):
                pe.wait_ge(sm_dve, at(l, 18, 4))
                own(pe)
                nc.tensor.transpose(PS[0:32, 7, 0:64], R[0:64, 832:864], ident[0:64, 0:64]).then_inc(sm_pe, 1)

            def expand_selection(l):
                pe.wait_ge(sm_dve, at(l, 18, 5))
                pe.wait_ge(wi_full[1], 16 * at(l, NWI // 2, KF // 2 + 1))
                for c in range(NPG):
                    last = mm(PS[:, 6 + c // 8, c % 8 * 64:c % 8 * 64 + 64], expand[:, c, :], R[0:32, 864:928],
                              c % 8 == 0, True)
                last.then_inc(sm_pe, 1)

            def win_scores(l):
                pe.wait_ge(sm_dve, at(l, 18, 6))
                pe.wait_ge(cr_full[0], 16 * at(l, CR_DMAS, 4 * NPG + 1))
                for b in range(B):
                    for c in range(NW):
                        mm(PS[:, 6 + b // 4, (b % 4 * NW + c) * 32:(b % 4 * NW + c + 1) * 32],
                           CR[:, 0, b * 512 + c * P:b * 512 + (c + 1) * P], Qblk[:, b, :, :, :],
                           b % 4 == 0 and c == 0, True)
                mm(PS[0:NS, 5, 0:256], knew[:, 1, :], Qblk[:, :, :, :, :], True, True).then_inc(sm_pe, 1)
                pe.drain().then_inc(cr_freed, 1)

            def turn_maxima(l, d):
                pe.wait_ge(sm_dve, at(l, 18, d))
                for a in range(2):
                    last = nc.tensor.transpose(PS[:, 6, a * P:(a + 1) * P], colx[:, a * P:(a + 1) * P], ident)
                last.then_inc(sm_pe, 1)

            def spread_maxima(l, d):
                pe.wait_ge(sm_dve, at(l, 18, d))
                mm(PS[:, 7, 0:256], ones, diag, True, True).then_inc(sm_pe, 1)

            def denominators(l, d):
                pe.wait_ge(sm_dve, at(l, 18, d))
                mm(PS[:, 6, 0:256], ones, colx, True, True).then_inc(sm_pe, 1)

            def new_values(l, br, stop):
                c0 = C_KV + 256 * (br + 1) + P
                return mm(PS[:, 5, 0:256], pj[0:NS, NT, c0:c0 + P], snew, True, stop)

            def win_values(l):
                new_values(l, 1, False)
                pe.wait_ge(cr_full[1], 16 * at(l, CR_DMAS, 4 * NPG + 1))
                pw = R[:, 0:1024].rearrange("p (c r) -> p c r", c=NW)
                for b in range(B):
                    for c in range(NW):
                        last = mm(PS[:, 5, b * 32:(b + 1) * 32], CR[:, 1, (b * NW + c) * P:(b * NW + c + 1) * P],
                                  pw[:, c, b * 32:(b + 1) * 32], False, b == B - 1 and c == NW - 1)
                last.then_inc(sm_pe, 1)
                pe.drain().then_inc(cr_freed, 1)

            def slc_scores(l, j):
                p = j % 2
                if j == 0:
                    pe.wait_ge(sm_dve, at(l, 18, 11))
                pe.wait_ge(cr_full[p], 16 * at(l, CR_DMAS, 4 * NPG + 1 + 2 * NPG * (j // 2 + 1)))
                for q in range(2):
                    b = 2 * j + q
                    pe.wait_ge(sk_freed, at(l, 8, b + 1))
                    for c in range(NPG):
                        last = mm(PS[:, 6 + q, c * 32:(c + 1) * 32], CR[:, p, (q * NPG + c) * P:(q * NPG + c + 1) * P],
                                  Qblk[:, b, :, :, :], c == 0, True)
                    last.then_inc(sk_ready, 1)
                pe.drain().then_inc(cr_freed, 1)

            def slc_new_scores(l):
                mm(PS[0:NS, 5, 0:256], knew[:, 0, :], Qblk[:, :, :, :, :], True, True).then_inc(sm_pe, 1)

            def slc_values(l, j):
                p = j % 2
                if j == 0:
                    new_values(l, 0, False)
                pe.wait_ge(cr_full[p], 16 * at(l, CR_DMAS, 8 * NPG + 1 + 2 * NPG * (j // 2 + 1)))
                pv = R[:, 0:4096].rearrange("p (c r) -> p c r", c=NPG)
                for q in range(2):
                    r = slice((2 * j + q) * 32, (2 * j + q + 1) * 32)
                    for c in range(NPG):
                        last = mm(PS[:, 5, r], CR[:, p, (q * NPG + c) * P:(q * NPG + c + 1) * P],
                                  pv[:, c, r], False, j == 3 and q == 1 and c == NPG - 1)
                if j == 3:
                    last.then_inc(sm_pe, 1)
                pe.drain().then_inc(cr_freed, 1)

            def turn_outputs(l):
                pe.wait_ge(sm_dve, at(l, 18, 15))
                for br in range(3):
                    for g in range(4):
                        last = nc.tensor.transpose(PS[0:NS, 5 + br, g * P:(g + 1) * P], OT[:, br, g, :], ident)
                last.then_inc(sm_pe, 1)

            def give_back(l):
                pe.wait_ge(sm_dve, at(l, 18, 18))
                pe.wait_ge(o_freed, at(l, 8, 8))
                pe.drain().then_inc(wi_done, 2)

            def prompt_compressed(l):
                pe.wait_ge(kc_ready, at(l, 18, 18 + 2))
                for t in range(NT):
                    for hh in range(8):
                        g, kv = hh // 2, hh % 2
                        last = mm(PS[:, 4 * kv + t, g * NC_P:(g + 1) * NC_P],
                                  qT[kv * HD:kv * HD + HD, g, t * P:(t + 1) * P],
                                  kcTp[kv * HD:kv * HD + HD, :], g == 0, True)
                last.then_inc(cp_pe, 1)
                for t in range(NT):
                    pe.wait_ge(cp_dve, at(l, 9, 1 + 2 * t))
                    for hh in range(8):
                        o = 512 + t * 248 + (hh % 2 * 4 + hh // 2) * NC_P
                        last = nc.tensor.transpose(PS[0:NC_P, 4 + hh // 4, hh % 4 * P:(hh % 4 + 1) * P],
                                                   R[:, o:o + NC_P], ident)
                    last.then_inc(cp_pe, 1)
                    pe.wait_ge(cp_dve, at(l, 9, 2 + 2 * t))
                    for hh in range(8):
                        kv = hh % 2
                        last = mm(PS[:, 6, hh * HD:(hh + 1) * HD], R[0:NC_P, 1536 + hh * P:1536 + (hh + 1) * P],
                                  vcp[0:NC_P, kv * HD:kv * HD + HD], hh == 0, True)
                    last.then_inc(cp_pe, 1)

            def prompt_attention(l, pieces):
                def unit(u):
                    g8, hh = u // 8, u % 8
                    return g8 // 2, g8 % 2, hh % 2, hh // 2

                def scores(u):
                    t, br, kv, g = unit(u)
                    n = (t + 1) * P
                    if u >= 2:
                        pe.wait_ge(p_ready, at(l, 64, u - 1))
                    r = slice(kv * HD, kv * HD + HD)
                    mm(PS[:, u % 2, 0:n], qT[r, g, t * P:(t + 1) * P], kT[r, br, 0:n], True, False)
                    mm(PS[:, u % 2, n - P:n], TRI[:, 1, :], TRI[:, 0, :], False, True).then_inc(sc_ready, 1)

                def turn(u):
                    t, br, kv, g = unit(u)
                    pe.wait_ge(p_ready, at(l, 64, u + 1))
                    if u >= 2:
                        pe.wait_ge(ptc_ready, at(l, 64, u - 1))
                    for c in range(t + 1):
                        last = nc.tensor.transpose(PS[:, 2 + u % 2, c * P:(c + 1) * P],
                                                   pbuf[:, u % 2, c * P:(c + 1) * P], ident)
                    last.then_inc(pt_ready, 1)

                def times_v(u):
                    t, br, kv, g = unit(u)
                    g8, hh = u // 8, u % 8
                    pe.wait_ge(ptc_ready, at(l, 64, u + 1))
                    if hh == 0 and g8 >= 1:
                        pe.wait_ge(o_freed, at(l, 8, g8))
                    c0 = C_KV + 256 * (br + 1) + P + kv * HD
                    for c in range(t + 1):
                        last = mm(PS[:, 4, hh * HD:(hh + 1) * HD], ptbuf[:, u % 2, c * P:(c + 1) * P],
                                  pj[:, c, c0:c0 + HD], hh == 0 and c == 0, c == t)
                    last.then_inc(pv_done, 1)

                pe.wait_ge(cp_dve, at(l, 9, 9))
                for u in range(64 + 2):
                    if u < 64:
                        scores(u)
                    if 1 <= u <= 64:
                        turn(u - 1)
                    if u >= 2:
                        times_v(u - 2)
                    if u in pieces:
                        pieces[u]()

            def gating(l):
                pe.wait_ge(gv_ready, at(l, 1, 1))
                for t in range(5):
                    r = ROWS[t]
                    w = (prm("ws") if t < NT else prm("wss", NS)).rearrange("p (h t) -> p h t", h=4)
                    for hh in range(4):
                        last = mm(PS[0:r, t % 2, hh * HD:(hh + 1) * HD] if t < 2 else
                                  PS[0:r, (0, 1, 2, 3, 4)[t], hh * HD:(hh + 1) * HD], w[:, hh, :],
                                  pj[0:r, t, C_V + hh * HD:C_V + (hh + 1) * HD], hh == 0, True)
                    last.then_inc(gm_ready, 1)

            def pooling(l):
                band = cst("band").rearrange("p (g t) -> p g t", g=4)
                band0 = cst("band0").rearrange("p (g t) -> p g t", g=4)
                bandh = cst("bandh", 120).rearrange("p (g t) -> p g t", g=4)
                bandn = cst("bandn", NS).rearrange("p (g t) -> p g t", g=4)
                for g in range(4):
                    c0 = C_P + g * HD
                    if g >= 1:
                        pe.wait_ge(pd_done, at(l, 4, g))
                    for t in range(NT):
                        z = pj[:, t, c0:c0 + HD]
                        if t == 0:
                            mm(PS[0:HD, 5, 0:16], z, band0[:, g, :], True, False)
                            mm(PS[0:HD, 5, 16:P], z, band[:, g, 16:P], False, False)
                        else:
                            mm(PS[0:HD, 5, t * P:(t + 1) * P], z, band[:, g, 0:P], False, False)
                            mm(PS[0:HD, 5, t * P:t * P + 15], pj[:, t - 1, c0:c0 + HD], band[:, g, P:P + 15],
                               False, t == NT - 1)
                    mm(PS[0:HD, 6, 0:NS], pj[0:NS, NT, c0:c0 + HD], bandn[:, g, :], True, False)
                    mm(PS[0:HD, 6, 0:NS], prm("hist", 120)[:, g * HD:(g + 1) * HD], bandh[:, g, :], False, True)\
                        .then_inc(pd_ready, 1)
                    pe.wait_ge(pd_done, at(l, 4, g + 1))
                    if g >= 1:
                        pe.wait_ge(pl_done, at(l, 4, g))
                        own(pe)
                    pw = prm("pw", HD).rearrange("p (g e) -> p g e", g=4)
                    if g == 0:
                        pe.wait_ge(gm_done, at(l, 5, 5))
                        own(pe)
                    for a in range(2):
                        last = mm(PS[0:HD, (7, 4)[a], 0:TH], pw[:, g, :], Z[0:HD, a * TH:(a + 1) * TH], True, True)
                    last.then_inc(pl_ready, 1)

            def turn_rows(l):
                for k in range(6):
                    if k >= 2:
                        pe.wait_ge(ct_done, at(l, 6, k - 1))
                    c0 = k * P if k < 4 else C_U + (k - 4) * P
                    for t in range(NT):
                        nc.tensor.transpose(PS[:, 2 * (k % 2), t * P:(t + 1) * P], pj[:, t, c0:c0 + P], ident)
                    nc.tensor.transpose(PS[:, 2 * (k % 2) + 1, 0:NS], pj[0:NS, NT, c0:c0 + P], ident[0:NS, 0:NS])\
                        .then_inc(ct_ready, 1)

            def mixer_out(l):
                pe.wait_ge(ct_done, at(l, 6, 6))
                pe.wait_ge(pl_done, at(l, 4, 4))
                own(pe)
                with pe.Fori(0, 2) as i:
                    for p in range(2):
                        pe.wait_ge(wi_full[p], 16 * (at(l, NWI // 2, (KF + 2) // 2 + 1) + i))
                        for q in range(2):
                            pe.wait_ge(y_added, at(l, 24, 8 + 2 * p + q + 1) + 4 * i)
                            for k in range(KD):
                                for a in range(2):
                                    last = mm(PS[:, 2 * q + a, 0:TH], WI[:, p, 8 * q + k, :],
                                              cat[:, k, a * TH:(a + 1) * TH], k == 0, k == KD - 1)
                            last.then_inc(y_ready, 1)
                        pe.drain().then_inc(wi_done, 1)

            pe.sem_inc(wi_done, 2)
            pe.sem_inc(w2_ready, 2)
            pe.sem_inc(wo_done, 2)
            pe.sem_inc(cr_freed, 2)
            pe.wait_ge(con_loaded, 32)
            pe.wait_ge(x_loaded, 16)
            pe.wait_ge(set_up, 1)
            own(pe)
            with pe.Fori(0, DEPTH) as l:
                ffn_in(l, 0, 0, 0)
                compress_pe(l)
                ffn_out(l, 0, 0, 0, compress_beside(l))
                ln_stats(l, 0)
                project(l)
                rows_to_cols(l)
                compress_prompt(l)
                prompt_compressed(l)
                prompt_attention(l, {
                    SAMPLE_AT[0]: lambda: cmp_scores(l), SAMPLE_AT[1]: lambda: cmp_turn(l),
                    SAMPLE_AT[2]: lambda: cmp_turn_back(l), SAMPLE_AT[3]: lambda: cmp_output(l),
                    SAMPLE_AT[4]: lambda: turn_selection(l), SAMPLE_AT[5]: lambda: expand_selection(l),
                    SAMPLE_AT[6]: lambda: win_scores(l), SAMPLE_AT[7]: lambda: turn_maxima(l, 7),
                    SAMPLE_AT[8]: lambda: spread_maxima(l, 8),
                    SAMPLE_AT[9]: lambda: (denominators(l, 9), win_values(l)),
                    SAMPLE_AT[10]: lambda: slc_scores(l, 0), SAMPLE_AT[11]: lambda: slc_scores(l, 1),
                    SAMPLE_AT[12]: lambda: slc_scores(l, 2),
                    SAMPLE_AT[13]: lambda: (slc_scores(l, 3), slc_new_scores(l)),
                    SAMPLE_AT[14]: lambda: turn_maxima(l, 12), SAMPLE_AT[15]: lambda: spread_maxima(l, 13),
                    SAMPLE_AT[16]: lambda: (denominators(l, 14), slc_values(l, 0)),
                    SAMPLE_AT[17]: lambda: slc_values(l, 1), SAMPLE_AT[18]: lambda: slc_values(l, 2),
                    SAMPLE_AT[19]: lambda: slc_values(l, 3), SAMPLE_AT[20]: lambda: turn_outputs(l)})
                give_back(l)
                gating(l)
                pooling(l)
                turn_rows(l)
                mixer_out(l)
                ln_stats(l, 1)
                ffn_in(l, 1, KF + 6, 16)
                ffn_out(l, 1, KD + NCH, 16)
                ln_stats(l, 2)

        @block.scalar
        def _(act):
            def af(out, in_, func, **kw):
                return nc.scalar.activation(out, in_, func, **kw)

            def round_wi(l, bi, p, i):
                act.wait_ge(wi_full[p], 16 * (at(l, NWI // 2, bi // 2 + 1) + i))
                af(wi_hi[:, p, :, :], WI[:, p, :, :], ACT.Copy).then_inc(wi_rounded, 1)

            def round_wo(l, p, i):
                act.wait_ge(wo_full[p], 16 * (at(l, NWO // 2, KD // 2 + 1) + i))
                af(wo_hi[:, p, :], WO[:, p, :], ACT.Copy).then_inc(wo_rounded, 1)

            def ffn_in(l, f, bi):
                def silu(i, p):
                    act.wait_ge(wi_done, at(l, NWI, (KF + 6) * f + p + 3) + 2 * i)
                    act.wait_ge(gu_freed, at(l, 44, 22 * f + p + 1) + 2 * i)
                    af(sil[:, p, :, :], PS[:, 4 * p:4 * p + 2, 0:TH], ACT.Silu).then_inc(sil_ready, 1)

                with act.Fori(0, KF // 2 - 1) as i:
                    for p in range(2):
                        silu(i, p)
                        round_wi(l, bi, p, i + 1)
                for p in range(2):
                    silu(KF // 2 - 1, p)

            def squares(l, s, beside=None):
                with act.Fori(0, KD // 2) as i:
                    for p in range(2):
                        if beside:
                            beside(i, p)
                        act.wait_ge(y_added, at(l, 24, 8 * s + p + 3) + 2 * i)
                        af(sq, x[:, ds(2 * i + p, 1), :].rearrange("p o t -> p (o t)"), ACT.Square)\
                            .then_inc(sq_ready, 1)

            def ln(l, s):
                act.wait_ge(var_ready, at(l, 3, s + 1))
                af(rs, rs, ACT.Sqrt, bias=cst("eps")).then_inc(std_ready, 1)
                act.wait_ge(par_loaded, 16 * at(l, 1, 1))
                for k in range(KD):
                    act.wait_ge(xn_ready, at(l, 24, 8 * s + k + 1))
                    af(xs[:, 0, k, :], x[:, k, :], ACT.Identity, bias=lnp[:, s, 1, k:k + 1],
                       scale=lnp[:, s, 0, k:k + 1])
                    act.drain()
                    af(x[:, k, :], x[:, k, :], ACT.Identity, bias=lnp[:, s, 1, k:k + 1],
                       scale=lnp[:, s, 0, k:k + 1]).then_inc(x_ready, 1)

            def project(l):
                def take(i, p):
                    for t in range(5):
                        r = ROWS[t]
                        act.wait_ge(pj_ready, at(l, 30, 5 * p + t + 1) + 10 * i)
                        af(pj[0:r, t, ds(2 * CW * i + CW * p, CW)], PS[0:r, t, 0:CW], ACT.Copy)\
                            .then_inc(pj_freed, 1)

                with act.Fori(0, NCH // 2 - 1) as i:
                    for p in range(2):
                        take(i, p)
                        round_wo(l, p, i + 1)
                for p in range(2):
                    take(NCH // 2 - 1, p)
                act.drain()
                for r, ts in ((P, slice(0, NT)), (NS, slice(NT, 5))):
                    af(pj[0:r, ts, C_GT:C_GT + 24], pj[0:r, ts, C_GT:C_GT + 24], ACT.Sigmoid)
                for r, ts in ((P, slice(0, NT)), (NS, slice(NT, 5))):
                    last = af(pj[0:r, ts, C_U:C_U + 512], pj[0:r, ts, C_U:C_U + 512], ACT.Gelu_apprx_tanh)
                last.then_inc(acts_done, 1)

            def gelu(base, v, n):
                act.wait_ge(hp_ready, base + v + 1)
                act.wait_ge(w2_ready, base + v + 1)
                af(hidb[:, 2 + v % 2, :, 0:n], hidb[:, 0, :, 0:n], ACT.Gelu_apprx_tanh,
                   bias=peb[:, v % 2:v % 2 + 1]).then_inc(hid_ready, 1)

            def compress_pe(l):
                act.wait_ge(pe_ready, at(l, 1, 1))
                af(peb[:, :], PS[0:HD, 7, 0:2], ACT.Copy)
                act.drain().then_inc(peb_ready, 1)

            def compress_beside(l):
                def beside(i, p):
                    for v in (2 * p, 2 * p + 1):
                        gelu(at(l, 18, 0) + 4 * i, v, NC_S)
                return beside

            def cmp_exp(l):
                act.wait_ge(sm_toact, at(l, 4, 2))
                for a in range(2):
                    last = af(R[:, 256 + a * NC_S:256 + (a + 1) * NC_S], PS[:, 7, a * NC_S:(a + 1) * NC_S], ACT.Exp,
                              bias=s2[:, 2 + a:3 + a], scale=SCALE, accum_out=s2[:, 4 + a:5 + a])
                last.then_inc(sm_act, 1)

            def cols_exp(l, n, k):
                act.wait_ge(sm_toact, at(l, 4, k))
                af(R[:, 0:256 * n], R[:, 0:256 * n], ACT.Exp, scale=SCALE)
                af(snew, snew, ACT.Exp, scale=SCALE).then_inc(sm_act, 1)

            def prompt_compressed(l):
                act.wait_ge(sm_toact, at(l, 4, 1))
                af(R[:, 512:512 + 992], R[:, 512:512 + 992], ACT.Exp, scale=SCALE).then_inc(sm_act, 1)

            def prompt_attention(l):
                for u in range(64):
                    n = (u // 16 + 1) * P
                    act.wait_ge(nm_ready, at(l, 64, u + 1))
                    if u >= 2:
                        act.wait_ge(pt_ready, at(l, 64, u - 1))
                    af(pbuf[:, u % 2, 0:n], PS[:, u % 2, 0:n], ACT.Exp, bias=nmx[:, u:u + 1], scale=SCALE,
                       accum_out=den[:, u:u + 1]).then_inc(p_ready, 1)
                    if u == SAMPLE_AT[1] + 1:
                        cmp_exp(l)
                    if u == SAMPLE_AT[8] + 1:
                        cols_exp(l, NW, 3)
                    if u == SAMPLE_AT[15] + 1:
                        cols_exp(l, NPG, 4)

            def pooling(l):
                for g in range(4):
                    act.wait_ge(pl_ready, at(l, 4, g + 1))
                    for a in range(2):
                        last = af(cat[g % 2 * HD:g % 2 * HD + HD, 6 + g // 2, a * TH:(a + 1) * TH],
                                  PS[0:HD, (7, 4)[a], 0:TH], ACT.Copy, scale=prm("ps", HD)[:, g:g + 1])
                    last.then_inc(pl_done, 1)

            act.sem_inc(hid_ready, 1)
            act.sem_inc(x_ready, 1)
            act.wait_ge(x_loaded, 16)
            for k in range(KD):
                af(xs[:, 0, k, :], x[:, k, :], ACT.Copy).then_inc(x_ready, 1)
            with act.Fori(0, DEPTH) as l:
                round_wi(l, 0, 0, 0)
                round_wi(l, 0, 1, 0)
                ffn_in(l, 0, 0)
                compress_pe(l)
                squares(l, 0, compress_beside(l))
                round_wo(l, 0, 0)
                ln(l, 0)
                round_wo(l, 1, 0)
                project(l)
                act.wait_ge(gvar_ready, at(l, 1, 1))
                act.wait_ge(con_loaded, 32)
                af(grs, gmv[:, :, 1], ACT.Sqrt, bias=cst("eps")).then_inc(gstd_ready, 1)
                for v in range(2):
                    gelu(at(l, 18, 16), v, NC_P)
                prompt_compressed(l)
                prompt_attention(l)
                pooling(l)
                squares(l, 1)
                round_wi(l, KF + 6, 0, 0)
                ln(l, 1)
                round_wi(l, KF + 6, 1, 0)
                ffn_in(l, 1, KF + 6)
                squares(l, 2)
                ln(l, 2)

        @block.vector
        def _(dve):
            V = nc.vector

            def settle():
                dve.drain()

            def tt(out, a, b, op):
                return V.tensor_tensor(out, a, b, op)

            def ffn_in(l, f):
                with dve.Fori(0, KF // 2) as i:
                    for p in range(2):
                        dve.wait_ge(sil_ready, at(l, 44, 22 * f + p + 1) + 2 * i)
                        V.scalar_tensor_tensor(h[:, ds(2 * i + p, 1), :].rearrange("p o (a t) -> p (o a) t", a=2),
                                               sil[:, p, :, :], 0.5, PS[:, 4 * p + 2:4 * p + 4, 0:TH],
                                               ALU.mult, ALU.mult).then_inc(gu_freed, 1)

            def add_y(l, s, beside=None):
                V.memset(ysum, 0.0)
                V.memset(qsum, 0.0)
                settle()
                with dve.Fori(0, KD // 2) as i:
                    for p in range(2):
                        if beside:
                            beside(i, p, 0)
                        if s == 1:
                            dve.wait_ge(y_ready, at(l, KD, p + 1) + 2 * i)
                        else:
                            dve.wait_ge(wo_done, at(l, NWO, (KD + NCH) * (s // 2) + p + 3) + 2 * i)
                        xk = x[:, ds(2 * i + p, 1), :].rearrange("p o t -> p (o t)")
                        V.scalar_tensor_tensor(xk.rearrange("p (a t) -> p a t", a=2),
                                               xk.rearrange("p (a t) -> p a t", a=2), ALPHA,
                                               PS[:, 2 * p:2 * p + 2, 0:TH], ALU.mult, ALU.add)
                        dve.drain().then_inc(y_added, 1)
                        tt(ysum, ysum, xk, ALU.add)
                        dve.wait_ge(sq_ready, at(l, 24, 8 * s + p + 1) + 2 * i)
                        tt(qsum, qsum, sq, ALU.add)
                        if beside:
                            beside(i, p, 1)
                        settle()
                dve.sem_inc(sums_ready, 1)

            def ln(l, s):
                h2 = lambda a: a.rearrange("p (a t) -> p a t", a=2)
                dve.wait_ge(stats_ready, at(l, 3, s + 1))
                V.tensor_scalar(h2(mu), PS[:, 4:6, 0:TH], 1.0 / D, None, ALU.mult)
                settle()
                tt(rs, mu, mu, ALU.mult)
                settle()
                V.scalar_tensor_tensor(h2(rs), PS[:, 6:8, 0:TH], 1.0 / D, h2(rs), ALU.mult, ALU.subtract)\
                    .then_inc(var_ready, 1)
                dve.wait_ge(std_ready, at(l, 3, s + 1))
                V.reciprocal(rs, rs)
                for k in range(KD):
                    tt(x[:, k, :], x[:, k, :], mu, ALU.subtract)
                    settle()
                    tt(x[:, k, :], x[:, k, :], rs, ALU.mult).then_inc(xn_ready, 1)

            def rope(l):
                dve.wait_ge(pj_freed, at(l, 30, 30 + 5))
                for t in range(5):
                    r = ROWS[t]
                    ta, tb = R[0:r, 0:896], R[0:r, 896:1792]
                    q = pj[0:r, t, 0:512].rearrange("p (n a d) -> p n a d", n=8, a=2)
                    ks = [pj[0:r, t, C_KV + 256 * i:C_KV + 256 * i + P].rearrange("p (n a d) -> p n a d", n=2, a=2)
                          for i in range(3)]
                    parts = [(q, 0, 8)] + [(ks[i], 512 + P * i, 2) for i in range(3)]
                    if t:
                        settle()
                    for src, o, n in parts:
                        for tab, buf in ((cos, ta), (sin, tb)):
                            cs = tab[0:r, t, :].rearrange("p (o d) -> p o d", o=1).to_broadcast([r, 2 * n, 32])
                            tt(buf[:, o:o + n * HD].rearrange("p (m d) -> p m d", d=32),
                               src.rearrange("p n a d -> p (n a) d"), cs, ALU.mult)
                    settle()
                    for src, o, n in parts:
                        a = ta[:, o:o + n * HD].rearrange("p (n a d) -> p n a d", n=n, a=2)
                        b = tb[:, o:o + n * HD].rearrange("p (n a d) -> p n a d", n=n, a=2)
                        tt(src[:, :, 0, :], a[:, :, 0, :], b[:, :, 1, :], ALU.subtract)
                        last = tt(src[:, :, 1, :], a[:, :, 1, :], b[:, :, 0, :], ALU.add)
                    last.then_inc(rope_ready, 1)

            def gv_norm(l):
                dve.wait_ge(par_loaded, 16 * at(l, 1, 1))
                ws = prm("ws").rearrange("p (h t) -> p h t", h=4)
                wss = prm("wss", NS).rearrange("p (h t) -> p h t", h=4)
                for hh in range(4):
                    tt(ws[:, hh, :], ws[:, hh, :], cst("tril"), ALU.mult)
                    tt(wss[:, hh, :], wss[:, hh, :], cst("trils", NS), ALU.mult)
                dve.wait_ge(acts_done, at(l, 1, 1))
                for t in range(5):
                    V.bn_stats(gst[0:ROWS[t], t, :], pj[0:ROWS[t], t, C_V:C_V + 256])
                settle()
                for t in range(5):
                    V.bn_aggr(gmv[0:ROWS[t], t, :], gst[0:ROWS[t], t, :])
                settle()
                dve.sem_inc(gvar_ready, 1)
                dve.wait_ge(gstd_ready, at(l, 1, 1))
                V.reciprocal(grs, grs)
                settle()
                for t in range(5):
                    r = ROWS[t]
                    v = pj[0:r, t, C_V:C_V + 256]
                    V.tensor_scalar(v, v, gmv[0:r, t, 0:1], grs[0:r, t:t + 1], ALU.subtract, ALU.mult)
                settle()
                for op, o in ((ALU.mult, 0), (ALU.add, 256)):
                    for t in range(5):
                        r = ROWS[t]
                        v = pj[0:r, t, C_V:C_V + 256]
                        tt(v, v, prm("gmgb", r)[:, o:o + 256], op)
                    settle()
                dve.sem_inc(gv_ready, 1)

            def rows_to_cols(l):
                for u in range(10):
                    dve.wait_ge(tr_ready, at(l, 10, u + 1))
                    bank = PS[:, 5 + u % 2, :]
                    if u < 4:
                        last = V.tensor_copy(qT[:, u, :], bank)
                    elif u < 6:
                        last = V.tensor_copy(kT[:, u - 4, :], bank)
                    elif u < 8:
                        for kv in range(2):
                            for j in range(2):
                                last = V.tensor_copy(T9[j * HD:(j + 1) * HD, u - 6, kv, :],
                                                     bank[kv * HD:(kv + 1) * HD, :]
                                                     .rearrange("p (n j) -> p n j", j=2)[:, :, j])
                    elif u == 8:
                        for kv in range(2):
                            s = slice(kv * HD, (kv + 1) * HD)
                            last = V.tensor_copy(Qblk[s, :, kv, :, :],
                                                 bank[s, 0:P].rearrange("p (g b t) -> p b t g", g=4, b=B))
                    else:
                        last = V.tensor_copy(knew[:, :, :], bank[:, 0:2 * NS].rearrange("p (a n) -> p a n", a=2))
                    last.then_inc(tr_freed, 1)

            def hidden_sum(base, v, n, pages):
                dve.wait_ge(cm_ready, base + v + 1)
                dve.wait_ge(hid_ready, base + v + 1)
                for half in range(2):
                    s = PS[half * HD:(half + 1) * HD, 4 + v % 2, 0:2 * n]
                    if pages:
                        for kv in range(2):
                            V.tensor_copy(hidb[:, half, kv, 0:n].rearrange("p (g n) -> p g n", g=NPG),
                                          s.rearrange("p (g h n) -> p h g n", g=NPG, h=2)[:, kv, :, :])
                    else:
                        V.tensor_copy(hidb[:, half, :, 0:n], s.rearrange("p (h n) -> p h n", h=2))
                dve.drain().then_inc(cm_freed, 1)
                tt(hidb[:, 0, :, 0:n - 1], hidb[:, 0, :, 0:n - 1], hidb[:, 1, :, 1:n], ALU.add)\
                    .then_inc(hp_ready, 1)

            def compressed(base, v, n, b):
                dve.wait_ge(w2_ready, base + v + 3)
                if v % 2 == 0:
                    for kv in range(2):
                        s = slice(kv * HD, (kv + 1) * HD)
                        out = kcTp[s, :] if b is None else kcT[s, ds(b, 1), :].rearrange("p o n -> p (o n)")
                        last = V.tensor_copy(out, PS[0:HD, 6, kv * n:(kv + 1) * n])
                else:
                    out = vcp[0:n, :] if b is None else vc[0:n, ds(b, 1), :].rearrange("p o n -> p (o n)")
                    last = V.tensor_copy(out, PS[0:n, 7, 0:P])
                last.then_inc(kc_ready, 1)

            def compress_beside(l):
                def beside(i, p, after):
                    for v in (2 * p, 2 * p + 1):
                        if after:
                            compressed(at(l, 18, 0) + 4 * i, v, NC_S, 2 * i + p)
                        else:
                            hidden_sum(at(l, 18, 0) + 4 * i, v, P, True)
                return beside

            def compress_prompt(l):
                for v in range(2):
                    hidden_sum(at(l, 18, 16), v, 32, False)
                for v in range(2):
                    compressed(at(l, 18, 16), v, NC_P, None)

            def take_out(br, scaled):
                for kv in range(2):
                    s = slice(kv * HD, (kv + 1) * HD)
                    for b in range(1):
                        src = PS[s, 5, 0:256].rearrange("p (b h r) -> p b h r", b=B, h=2)[:, :, kv, :]
                        dst = OT[s, br, :, :].rearrange("p g (b t) -> p b t g", b=B)
                        if scaled:
                            rd = rden[s, :].rearrange("p (b h r) -> p b h r", b=B, h=2)[:, :, kv, :]
                            last = tt(dst, src.rearrange("p b (t g) -> p b t g", g=4),
                                      rd.rearrange("p b (t g) -> p b t g", g=4), ALU.mult)
                        else:
                            last = V.tensor_copy(dst, src.rearrange("p b (t g) -> p b t g", g=4))
                return last

            def col_maxima(l, n, k):
                V.tensor_reduce(colx, R[:, 0:n * 256].rearrange("p (c r) -> p r c", c=n), X, ALU.max)
                settle()
                tt(colx[0:NS, :], colx[0:NS, :], snew, ALU.max).then_inc(sm_dve, 1)

            def on_diagonal(l, k):
                dve.wait_ge(sm_pe, at(l, 17, k))
                V.tensor_reduce(s2[:, 0:2], PS[:, 6, 0:256].rearrange("p (a n) -> p a n", a=2), X, ALU.max)
                settle()
                for a in range(2):
                    last = V.tensor_scalar(diag[:, a * P:(a + 1) * P], ident, s2[:, a:a + 1], None, ALU.mult)
                last.then_inc(sm_dve, 1)

            def less_maxima(l, n, k):
                dve.wait_ge(sm_pe, at(l, 17, k))
                V.tensor_copy(rden, PS[:, 7, 0:256])
                settle()
                sr = R[:, 0:n * 256].rearrange("p (c r) -> p c r", c=n)
                tt(sr, sr, rden.rearrange("p (o r) -> p o r", o=1).to_broadcast([P, n, 256]), ALU.subtract)
                tt(snew, snew, rden[0:NS, :], ALU.subtract)
                dve.drain().then_inc(sm_toact, 1)

            def col_sums(l, n, k):
                dve.wait_ge(sm_act, at(l, 4, k))
                V.tensor_reduce(colx, R[:, 0:n * 256].rearrange("p (c r) -> p r c", c=n), X, ALU.add)
                settle()
                tt(colx[0:NS, :], colx[0:NS, :], snew, ALU.add).then_inc(sm_dve, 1)

            def reciprocals(l, k):
                dve.wait_ge(sm_pe, at(l, 17, k))
                V.reciprocal(rden, PS[:, 6, 0:256])
                settle()

            def cmp_scores(l):
                dve.wait_ge(sm_pe, at(l, 17, 1))
                V.tensor_copy(R[0:NC_S, 0:256], PS[0:NC_S, 6, 0:256]).then_inc(sm_dve, 1)

            def cmp_maxima(l):
                dve.wait_ge(sm_pe, at(l, 17, 2))
                V.tensor_reduce(s2[:, 0:2], PS[:, 7, 0:2 * NC_S].rearrange("p (a n) -> p a n", a=2), X, ALU.max)
                settle()
                V.tensor_scalar(s2[:, 2:4], s2[:, 0:2], -SCALE, None, ALU.mult).then_inc(sm_toact, 1)

            def cmp_normalise(l):
                dve.wait_ge(sm_act, at(l, 4, 2))
                V.reciprocal(s2[:, 6:8], s2[:, 4:6])
                settle()
                for a in range(2):
                    pr = R[:, 256 + a * NC_S:256 + (a + 1) * NC_S]
                    last = V.tensor_scalar(pr, pr, s2[:, 6 + a:7 + a], None, ALU.mult)
                last.then_inc(sm_dve, 1)

            def cmp_columns(l):
                dve.wait_ge(sm_pe, at(l, 17, 3))
                V.tensor_copy(R[0:NC_S, 512:768], PS[0:NC_S, 6, 0:256])
                settle()
                V.tensor_reduce(R[0:NC_S, 768:832], R[0:NC_S, 512:768].rearrange("p (r g) -> p r g", g=4), X, ALU.add)\
                    .then_inc(sm_dve, 1)

            imp, sel = R[0:64, 928:960], R[0:64, 832:864]
            g3 = R[0:64, 1024:1924].rearrange("p (j i) -> p j i", i=30)
            e3 = R[0:64, 1924:2824].rearrange("p (j i) -> p j i", i=30)
            row = lambda a: a.rearrange("p (o i) -> p o i", o=1).to_broadcast([64, 30, 30])
            col = lambda a: a.rearrange("p (j o) -> p j o", o=1).to_broadcast([64, 30, 30])

            def rank_ties(l):
                dve.wait_ge(sm_pe, at(l, 17, 4))
                take_out(0, False)
                V.tensor_copy(imp, PS[0:64, 7, 0:32])
                settle()
                tt(g3, row(imp[:, 1:31]), col(imp[:, 1:31]), ALU.is_equal)
                tt(e3, row(cst("idx", 64)), col(cst("idx", 64)), ALU.is_lt)
                settle()
                tt(e3, e3, g3, ALU.mult)
                settle()

            def rank(l):
                tt(g3, row(imp[:, 1:31]), col(imp[:, 1:31]), ALU.is_gt)
                settle()
                tt(g3, g3, e3, ALU.add)
                V.memset(sel, 1.0)
                settle()
                V.tensor_reduce(R[0:64, 960:990], g3, X, ALU.add)
                settle()
                V.tensor_scalar(sel[:, 1:31], R[0:64, 960:990], NTOP - 0.5, None, ALU.is_lt).then_inc(sm_dve, 1)

            def selection(l):
                dve.wait_ge(sm_pe, at(l, 17, 5))
                V.tensor_copy(R[0:32, 864:928], PS[0:32, 7, 0:64]).then_inc(sm_dve, 1)

            def selection_mask(l):
                dve.wait_ge(sm_pe, at(l, 17, 6))
                V.tensor_scalar(Madd.rearrange("p (a c) r -> p a (c r)", a=2), PS[:, 6:8, :], 1.0, -NEG,
                                ALU.subtract, ALU.mult)
                dve.drain().then_inc(sm_dve, 1)

            def win_scores(l):
                dve.wait_ge(sm_pe, at(l, 17, 7))
                sw = R[:, 0:1024].rearrange("p (c b r) -> p c b r", c=NW, b=B)
                for a in range(2):
                    V.tensor_copy(sw[:, :, 4 * a:4 * a + 4, :],
                                  PS[:, 6 + a, :].rearrange("p (b c r) -> p c b r", b=4, c=NW))
                tt(snew, PS[0:NS, 5, 0:256], cst("nadd", NS), ALU.add)
                settle()
                tt(sw[:, 0, :, :], sw[:, 0, :, :],
                   cst("wadd").rearrange("p (o r) -> p o r", o=1).to_broadcast([P, B, 32]), ALU.add)
                settle()
                col_maxima(l, NW, 6)

            def win_output(l):
                reciprocals(l, 10)
                dve.sem_inc(sm_dve, 1)
                dve.wait_ge(sm_pe, at(l, 17, 11))
                take_out(2, True)
                dve.drain().then_inc(sm_dve, 1)

            def slc_scores(l, j):
                for q in range(2):
                    b = 2 * j + q
                    dve.wait_ge(sk_ready, at(l, 8, b + 1))
                    mb = Madd[:, :, b * 8:b * 8 + 8].rearrange("p c (r o) -> p c r o", o=1)\
                        .to_broadcast([P, NPG, 8, 4])
                    tt(R[:, 0:4096].rearrange("p (c r g) -> p c r g", c=NPG, g=4)[:, :, b * 8:b * 8 + 8, :],
                       PS[:, 6 + q, :].rearrange("p (c r g) -> p c r g", c=NPG, g=4), mb, ALU.add)\
                        .then_inc(sk_freed, 1)

            def slc_new_scores(l):
                dve.wait_ge(sm_pe, at(l, 17, 12))
                tt(snew, PS[0:NS, 5, 0:256], cst("nadd", NS), ALU.add)
                settle()
                col_maxima(l, NPG, 11)

            def slc_output(l):
                dve.wait_ge(sm_pe, at(l, 17, 16))
                take_out(1, True)
                dve.drain().then_inc(sm_dve, 1)

            def sample_merge(l):
                dve.wait_ge(sm_pe, at(l, 17, 17))
                merge(NS, NT, lambda br: PS[0:NS, 5 + br, :].rearrange("p (g h d) -> p g h d", g=4, h=2),
                      mtmp[0:NS, :])
                dve.drain().then_inc(sm_dve, 3)

            def gate(r, t, br):
                return pj[0:r, t, C_GT:C_GT + 24].rearrange("p (h g b) -> p g h b", h=2, g=4)[:, :, :, br:br + 1]\
                    .to_broadcast([r, 4, 2, HD])

            def merge(r, t, src, tmp):
                out = pj[0:r, t, 0:512].rearrange("p (g h d) -> p g h d", g=4, h=2)
                t4 = tmp.rearrange("p (g h d) -> p g h d", g=4, h=2)
                for br in range(3):
                    tt(out if br == 0 else t4, src(br), gate(r, t, br), ALU.mult)
                    settle()
                    if br:
                        tt(out, out, t4, ALU.add)
                        settle()

            def prompt_compressed(l):
                dve.wait_ge(cp_pe, at(l, 9, 1))
                for t in range(NT):
                    for kv in range(2):
                        o = 512 + t * 248 + kv * 124
                        tt(R[:, o:o + 124].rearrange("p (h n) -> p h n", h=4),
                           PS[:, 4 * kv + t, 0:124].rearrange("p (h n) -> p h n", h=4),
                           cst("cadd")[:, t * 31:(t + 1) * 31].rearrange("p (o n) -> p o n", o=1)
                           .to_broadcast([P, 4, NC_P]), ALU.add)
                settle()
                sc = R[:, 512:512 + 992].rearrange("p (u n) -> p u n", u=32)
                m32 = Z[:, 0:32]
                mb = lambda: m32.rearrange("p (u o) -> p u o", o=1).to_broadcast([P, 32, NC_P])
                V.tensor_reduce(m32, sc, X, ALU.max)
                settle()
                tt(sc, sc, mb(), ALU.subtract)
                settle()
                dve.sem_inc(sm_toact, 1)
                dve.wait_ge(sm_act, at(l, 4, 1))
                V.tensor_reduce(m32, sc, X, ALU.add)
                settle()
                V.reciprocal(m32, m32)
                for t in range(NT):
                    s3 = R[:, 512 + t * 248:512 + (t + 1) * 248].rearrange("p (h n) -> p h n", h=8)
                    V.scalar_tensor_tensor(s3, cst("cadd")[:, t * 31:(t + 1) * 31].rearrange("p (o n) -> p o n", o=1)
                                           .to_broadcast([P, 8, NC_P]), -1.0, s3, ALU.is_ge, ALU.mult)
                settle()
                tt(sc, sc, mb(), ALU.mult).then_inc(cp_dve, 1)
                for t in range(NT):
                    dve.wait_ge(cp_pe, at(l, 9, 2 + 2 * t))
                    V.tensor_copy(R[0:NC_P, 1536:2560].rearrange("p (a n) -> p a n", a=2), PS[0:NC_P, 4:6, :])\
                        .then_inc(cp_dve, 1)
                    dve.wait_ge(cp_pe, at(l, 9, 3 + 2 * t))
                    tt(pj[:, t, 0:512].rearrange("p (g h d) -> p g h d", g=4, h=2),
                       PS[:, 6, :].rearrange("p (g h d) -> p g h d", g=4, h=2), gate(P, t, 0), ALU.mult)\
                        .then_inc(cp_dve, 1)

            def prompt_attention(l, pieces):
                def maxima(u):
                    n = (u // 16 + 1) * P
                    dve.wait_ge(sc_ready, at(l, 64, u + 1))
                    V.tensor_reduce(row_max[:, u % 2:u % 2 + 1], PS[:, u % 2, 0:n], X, ALU.max)
                    settle()
                    V.tensor_scalar(nmx[:, u:u + 1], row_max[:, u % 2:u % 2 + 1], -SCALE, None, ALU.mult)\
                        .then_inc(nm_ready, 1)

                def turned(u):
                    n = (u // 16 + 1) * P
                    dve.wait_ge(pt_ready, at(l, 64, u + 1))
                    if u >= 2:
                        dve.wait_ge(pv_done, at(l, 64, u - 1))
                    V.tensor_copy(ptbuf[:, u % 2, 0:n], PS[:, 2 + u % 2, 0:n]).then_inc(ptc_ready, 1)

                def merged(g8):
                    t, br = g8 // 2, g8 % 2
                    dve.wait_ge(p_ready, at(l, 64, 8 * g8 + 8))
                    V.reciprocal(w8, den[:, 8 * g8:8 * g8 + 8])
                    settle()
                    gt = pj[:, t, C_GT:C_GT + 24].rearrange("p (h g b) -> p g h b", h=2, g=4)[:, :, :, br + 1]
                    w42 = w8.rearrange("p (g h) -> p g h", g=4)
                    tt(w42, w42, gt, ALU.mult)
                    settle()
                    dve.wait_ge(pv_done, at(l, 64, 8 * g8 + 8))
                    tt(mtmp.rearrange("p (h d) -> p h d", h=8), PS[:, 4, :].rearrange("p (h d) -> p h d", h=8),
                       w8.rearrange("p (h o) -> p h o", o=1).to_broadcast([P, 8, HD]), ALU.mult)
                    settle()
                    if g8 < 7:
                        dve.sem_inc(o_freed, 1)
                    tt(pj[:, t, 0:512], pj[:, t, 0:512], mtmp, ALU.add)
                    settle()
                    if g8 == 7:
                        dve.sem_inc(o_freed, 1)

                for u in range(64 + 2):
                    if u < 64:
                        maxima(u)
                    if 1 <= u <= 64:
                        turned(u - 1)
                    if u >= 2 and (u - 2) % 8 == 7:
                        merged((u - 2) // 8)
                    if u in pieces:
                        pieces[u]()

            def gating(l):
                for t in range(5):
                    r = ROWS[t]
                    dve.wait_ge(gm_ready, at(l, 5, t + 1))
                    b = (prm("gmb") if t < NT else prm("gmbs", NS)).rearrange("p (h o) -> p h o", o=1)\
                        .to_broadcast([r, 4, HD])
                    tmp = Z[0:r, 1088:1344].rearrange("p (h d) -> p h d", h=4)
                    tt(tmp, PS[0:r, t, 0:256].rearrange("p (h d) -> p h d", h=4), b, ALU.add)
                    settle()
                    u = pj[0:r, t, C_U:C_U + 256]
                    tt(u, u, Z[0:r, 1088:1344], ALU.mult).then_inc(gm_done, 1)
                    settle()

            def pooling(l):
                for g in range(4):
                    dve.wait_ge(pd_ready, at(l, 4, g + 1))
                    if g:
                        dve.wait_ge(pl_ready, at(l, 4, g))
                    V.tensor_copy(Z[0:HD, 0:TP], PS[0:HD, 5, :])
                    V.tensor_copy(Z[0:HD, TP:T], PS[0:HD, 6, 0:NS])
                    dve.drain().then_inc(pd_done, 1)

            def turn_rows(l):
                for k in range(6):
                    dve.wait_ge(ct_ready, at(l, 6, k + 1))
                    V.tensor_copy(cat[:, k, 0:TP], PS[:, 2 * (k % 2), :])
                    V.tensor_copy(cat[:, k, TP:T], PS[:, 2 * (k % 2) + 1, 0:NS])
                    dve.drain().then_inc(ct_done, 1)

            for s, n in ((gu_freed, 2), (y_added, 2), (pj_freed, 5), (tr_freed, 2), (cm_freed, 2), (kc_ready, 2),
                         (sk_freed, 2)):
                dve.sem_inc(s, n)
            dve.wait_ge(con_loaded, 32)
            dve.wait_ge(x_loaded, 16)
            dve.wait_ge(set_up, 1)
            own(dve)
            with dve.Fori(0, DEPTH) as l:
                ffn_in(l, 0)
                add_y(l, 0, compress_beside(l))
                ln(l, 0)
                rope(l)
                rows_to_cols(l)
                gv_norm(l)
                compress_prompt(l)
                prompt_compressed(l)
                A = SAMPLE_AT
                prompt_attention(l, {
                    A[0] + 1: lambda: cmp_scores(l), A[1] + 1: lambda: cmp_maxima(l), A[2]: lambda: cmp_normalise(l),
                    A[2] + 1: lambda: cmp_columns(l), A[3] + 1: lambda: rank_ties(l), A[4] - 1: lambda: rank(l),
                    A[4] + 1: lambda: selection(l), A[5] + 1: lambda: selection_mask(l),
                    A[6] + 1: lambda: win_scores(l), A[7] + 1: lambda: on_diagonal(l, 8),
                    A[8] + 1: lambda: less_maxima(l, NW, 9), A[9]: lambda: col_sums(l, NW, 3),
                    A[9] + 1: lambda: win_output(l), A[10] + 1: lambda: slc_scores(l, 0),
                    A[11] + 1: lambda: slc_scores(l, 1), A[12] + 1: lambda: slc_scores(l, 2),
                    A[13] + 1: lambda: (slc_scores(l, 3), slc_new_scores(l)),
                    A[14] + 1: lambda: on_diagonal(l, 13), A[15] + 1: lambda: less_maxima(l, NPG, 14),
                    A[16]: lambda: col_sums(l, NPG, 4), A[16] + 1: lambda: reciprocals(l, 15),
                    A[19] + 1: lambda: slc_output(l), A[20] + 1: lambda: sample_merge(l)})
                gating(l)
                pooling(l)
                turn_rows(l)
                add_y(l, 1)
                ln(l, 1)
                dve.wait_ge(stored, 16 * at(l, 11, 11))
                own(dve)
                ffn_in(l, 1)
                add_y(l, 2)
                ln(l, 2)


def constants():
    f = np.float32
    c = np.zeros((P, NCONST), f)

    def put(n, a):
        o, w = CONST[n]
        a = np.asarray(a, f).reshape(a.shape[0], -1)
        c[:a.shape[0], o:o + w] = a

    p = np.arange(P)
    inv = (10000.0 ** (-np.arange(32) / 32)).astype(f)
    pos = np.stack([t * P + p for t in range(NT)] + [PAST + p % TS], 1).astype(f)
    ang = (pos[:, :, None] * inv).astype(f)
    put("cos", np.cos(ang))
    put("sin", np.sin(ang))
    put("ident", np.eye(P))
    put("ones", np.ones((P, P)))
    q = np.stack([t * P + p for t in range(NT)], 1)
    ok = (16 * np.arange(NC_P) + 31)[None, None] <= q[:, :, None]
    put("cadd", np.where(ok, 0.0, NEG))
    r = np.arange(32)
    put("wadd", np.where(p[:, None] >= (r // 4 % 4)[None], 0.0, NEG))
    r = np.arange(256)
    k = np.arange(32)[:, None]
    put("nadd", np.where((k // 4 == r // 32) & (k % 4 <= r // 4 % 4), 0.0, NEG))
    c0, s0 = 16 * np.arange(P)[:, None], 64 * np.arange(32)[None]
    put("selmap", np.clip(np.minimum(c0 + 32, s0 + 64) - np.maximum(c0, s0), 0, None) / 32)
    s, t = p[:, None], np.arange(143)[None]
    put("band", np.stack([((s <= t) & (s > t - w)) / w - (s == t) for w in WINS], 1))
    t = np.arange(16)[None]
    put("band0", np.stack([((s <= t) & (s > t - w)) / np.minimum(w, t + 1) - (s == t) for w in WINS], 1))
    j, rr = np.arange(120)[:, None], np.arange(32)[None]
    put("bandh", np.stack([((j // 15 == rr // 4) & (j % 15 > rr % 4 + 15 - w)) / w for w in WINS], 1))
    put("bandn", np.stack([((k // 4 == rr // 4) & (k % 4 <= rr % 4) & (k % 4 > rr % 4 - w)) / w - (k == rr)
                           for w in WINS], 1))
    put("tril", s <= p[None])
    put("trils", (k // 4 == rr // 4) & (k <= rr))
    put("idx", np.tile(np.arange(30), (P, 1)))
    put("eps", np.full((P, 1), EPS))
    return c


def kernel(**inputs):
    import ml_dtypes
    import concourse.bacc as _bacc
    from concourse.bass_utils import run_bass_kernel_spmd as _run

    a = {n: np.asarray(v) for n, v in inputs.items()}
    f = np.float32
    L = DEPTH
    tok = np.concatenate([a["x_prompt"].reshape(TP, D), a["x_sample"].reshape(NS, D)])
    arr = {"x_in": tok.T.reshape(KD, P, T).transpose(1, 0, 2)}
    wi = np.zeros((L, NWI, P, 16, P), f)
    win = a["ffn_w_in"].reshape(L, 2, KD, P, 2, KF, P).transpose(0, 1, 5, 3, 4, 2, 6).reshape(L, 2, KF, P, 16, P)
    wi[:, 0:KF], wi[:, KF + 6:] = win[:, 0], win[:, 1]
    wi[:, KF] = a["cmp_w1"].reshape(L, 2, 2, 8, 2, HD, HD).transpose(0, 4, 5, 1, 3, 2, 6).reshape(L, P, 16, P)
    for b in range(32):
        wi[:, KF + 1, b, b // 2, b % 2 * 64:b % 2 * 64 + 64] = 1.0
    order = np.arange(D)
    order[:512] = np.arange(512).reshape(2, 4, HD).transpose(1, 0, 2).reshape(-1)
    wi[:, KF + 2:KF + 6] = a["w_o"][:, order].reshape(L, KD, P, 4, 2, P).transpose(0, 3, 2, 4, 1, 5).reshape(L, 4, P, 16, P)
    arr["wi"] = wi.reshape(L * NWI, P, 2048)
    wo = np.zeros((L, NWO, P, KF * P), f)
    wout = a["ffn_w_out"].reshape(L, 2, KF, P, KD, P).transpose(0, 1, 4, 3, 2, 5).reshape(L, 2, KD, P, KF * P)
    wo[:, 0:KD], wo[:, KD + NCH:] = wout[:, 0], wout[:, 1]
    wm = np.zeros((L, D, PJW), f)
    wm[:, :, :a["w_in"].shape[2]] = a["w_in"]
    wm[:, :, :512] = a["w_in"][:, :, order[:512]]
    wo[:, KD:KD + NCH] = wm.reshape(L, KD, P, NCH, CW).transpose(0, 3, 2, 1, 4).reshape(L, NCH, P, KF * P)
    arr["wo"] = wo.reshape(L * NWO, P, KF * P)
    npg = a["cache_kv_cmp"].shape[1]
    arr["cmp_t"] = a["cache_kv_cmp"].reshape(L, npg, 8, 8, 2, 2, 2, HD).transpose(0, 1, 4, 7, 5, 3, 6, 2)\
        .reshape(L * npg, P, 256)
    slc = a["cache_kv_slc"].reshape(L * npg, PAGE, 2, P)
    arr["slc_k"] = slc[:, :, 0].transpose(0, 2, 1)
    arr["slc_v"] = slc[:, :, 1]
    wst = a["state_kv_win"].reshape(L, B, 512, 2, P)
    arr["win_k"] = wst[:, :, :, 0].transpose(0, 3, 1, 2).reshape(L, P, 4096)
    arr["win_v"] = wst[:, :, :, 1].reshape(L, B * NW, P, P).transpose(0, 2, 1, 3).reshape(L, P, 4096)
    arr["win_rows"] = wst.reshape(L, B, 512, 256)
    arr["hist_rows"] = a["state_pool"]
    arr["table"] = a["page_table"].reshape(1, B * NPG).astype(np.int32)
    par = np.zeros((L, P, NPAR), f)

    def put(n, v):
        o, w = PAR[n]
        par[:, :v.shape[1], o:o + w] = v.reshape(L, v.shape[1], w)

    put("ln", np.stack([a["ln_g"], a["ln_b"]], 2).reshape(L, 3, 2, KD, P).transpose(0, 4, 1, 2, 3))
    put("gmgb", np.broadcast_to(np.concatenate([a["gm_ln_g"], a["gm_ln_b"]], 1)[:, None], (L, P, 512)))
    put("ws", a["gm_ws"].transpose(0, 3, 1, 2))
    put("gmb", a["gm_b"].transpose(0, 2, 1))
    wss = np.zeros((L, B, TS, 4, B, TS), f)
    for b in range(B):
        wss[:, b, :, :, b, :] = a["gm_ws"][:, :, :TS, :TS].transpose(0, 3, 1, 2)
    put("wss", wss.reshape(L, NS, P))
    put("gmbs", np.tile(a["gm_b"][:, :, :TS].transpose(0, 2, 1), (1, B, 1)))
    put("pw", a["pool_w"].transpose(0, 2, 1, 3))
    put("ps", a["pool_scale"].reshape(L, 4, HD).transpose(0, 2, 1))
    put("w2", a["cmp_w2"].transpose(0, 2, 1, 3))
    put("pe", a["cmp_pe"].reshape(L, 2, 2, 8, 2, HD).transpose(0, 4, 5, 1, 2, 3).reshape(L, P, 32))
    put("hist", a["state_pool"].reshape(L, B * 15, 256))
    arr["par"] = par
    arr["consts"] = constants()
    q = np.arange(P)
    arr["tri"] = np.stack([np.where(q[None] > q[:, None], NEG, 0.0), np.eye(P)], 1).astype(ml_dtypes.bfloat16)
    outs = {"o_x": (P, KD, T), "o_cmp_p": (L, TP, 256), "o_cmp_s": (L, NS, 256), "o_slc_p": (L, TP, 256),
            "o_slc_s": (L, NS, 256), "o_win_p": (L, TP, 256), "o_win_s": (L, B, 512, 256),
            "o_pool_p": (L, 15, 256), "o_pool_s": (L, B, 15, 256), "o_gv": (L, NS, 256)}
    nc = _bacc.Bacc("TRN2", target_bir_lowering=False, num_devices=1)
    arrays, aps = {}, {}
    for n, v in arr.items():
        v = np.ascontiguousarray(v)
        arrays[n + "_dram"] = v
        aps[n] = nc.dram_tensor(n + "_dram", v.shape, mybir.dt.from_np(v.dtype), kind="ExternalInput").ap()
    for n, s in outs.items():
        aps[n] = nc.dram_tensor(n + "_dram", s, F32, kind="ExternalOutput").ap()
    build(nc, **aps)
    r = _run(nc, [arrays], core_ids=[0]).results[0]
    o = {n: r[n + "_dram"] for n in outs}
    y = o["o_x"].transpose(1, 0, 2).reshape(D, T).T
    kv = lambda n, b, s: o[n].reshape(L, b, s, 2, 2, HD)
    return (y[:TP].reshape(1, TP, D), y[TP:].reshape(B, TS, D), kv("o_cmp_p", 1, TP), kv("o_cmp_s", B, TS),
            kv("o_slc_p", 1, TP), kv("o_slc_s", B, TS), kv("o_win_p", 1, TP), kv("o_win_s", B, 512),
            o["o_pool_p"].reshape(L, 1, 15, 256), o["o_pool_s"], o["o_gv"].reshape(L, B, TS, 256))
```

```python
import numpy as np
import concourse.bass as bass
from concourse import mybir
from contextlib import ExitStack

F32 = mybir.dt.float32
FR = mybir.dt.float32r
BF16 = mybir.dt.bfloat16
I32 = mybir.dt.int32
ACT = mybir.ActivationFunctionType
ALU = mybir.AluOpType
X = mybir.AxisListType.X
ds = bass.ds

P = 128
DEPTH, D, DFF = 2, 1024, 2816
TP, B, TS = 512, 8, 4
NS = B * TS
T = TP + NS
TH = T // 2
KD, KF = D // P, DFF // P
PAST, PAGE, NPG = 2048, 128, 16
HD, SCALE = 64, 64 ** -0.5
ALPHA = (2 * DEPTH) ** 0.25
EPS, NEG = 1e-5, -1e30
CW, NCH = 352, 6
PJW = CW * NCH
C_KV, C_GT, C_U, C_V, C_P = 512, 1280, 1304, 1560, 1816
NT = TP // P
ROWS = [P] * NT + [NS]
AT = dict(keys_1=0, cmp_scores=1, cmp_turn=3, cmp_turn_back=5, cmp_output=7, turn_selection=11,
          expand=13, keys_2=15, keys_3=17, win_scores=18, win_maxima=20, win_spread=22, win_values=25,
          mask_0=20, mask_1=22, slc_new=27, slc_maxima=29, slc_spread=31, slc_values=42, slc_values_1=47,
          slc_values_2=52, slc_values_3=57, slc_turn=59, turn_outputs=62)
CP_STEPS = [(0, 1), (1, 1), (0, 0), (2, 1), (1, 0), (3, 1), (2, 0), (3, 0)]
NPHYS = B * NPG * 5 // 4
LOT = 8
NW = 4
NC_S, NC_P = PAST // 16 - 1, TP // 16 - 1
NTOP = 13
WINS = (2, 4, 8, 16)
NWI, NWO, NCR = 50, 22, 18
CR_DMAS = 4 * NPG + 1 + 2 * 2 * NPG + 2 * 2 * NPG

CONST = {}
_at = 0
for _n, _w in (("cos", 5 * 32), ("sin", 5 * 32), ("ident", P), ("ones", P), ("cadd", 4 * 31),
               ("wadd", 32), ("nadd", 256), ("selmap", 32), ("band", 4 * 143), ("band0", 4 * 16),
               ("bandh", 4 * 32), ("bandn", 4 * 32), ("tril", P), ("trils", 32), ("idx", 30), ("eps", 1)):
    CONST[_n] = (_at, _w)
    _at += _w
NCONST = _at
PAR = {}
_at = 0
for _n, _w in (("ln", 48), ("gmgb", 512), ("ws", 512), ("gmb", 4), ("wss", 128), ("gmbs", 4), ("pw", 256),
               ("ps", 4), ("w2", 128), ("pe", 32), ("hist", 256)):
    PAR[_n] = (_at, _w)
    _at += _w
NPAR = _at


def at(l, per_layer, n):
    return l * per_layer + n


def build(nc, x_in, wi, wo, cmp_t, slc_k, slc_v, win_k, win_v, win_rows, hist_rows, table, par, consts, tri,
          o_x, o_cmp_p, o_cmp_s, o_slc_p, o_slc_s, o_win_p, o_win_s, o_pool_p, o_pool_s, o_gv):
    ctx = ExitStack()
    sb = lambda n, s, d=F32: ctx.enter_context(nc.sbuf_tensor(n, s, d))
    sem = lambda n: ctx.enter_context(nc.semaphore(n))
    with ctx:
        x = sb("x", [P, KD, T])
        N_R, N_Q, N_K, N_C = KD * T, 4 * TP, 2 * TP, 2 * 4096
        at_m = -(-nc.sbuf_base // 32) * 32
        N_KC, N_VC, N_OT = B * NC_S, B * P, 3 * 4 * NS
        AT_KC = N_R + N_Q + N_K + N_C + P - NS
        M = sb("M", [P, AT_KC + N_KC + N_VC + N_OT])
        R = M[:, 0:N_R]
        at_wi = -(-nc.sbuf_base // 32) * 32
        WI = sb("WI", [P, 2, 16, P])
        at_wo = -(-nc.sbuf_base // 32) * 32
        WO = sb("WO", [P, 2, KF * P])
        at_h = -(-nc.sbuf_base // 32) * 32
        H = sb("H", [P, KF * T])
        qT = M[:, N_R:N_R + N_Q].rearrange("p (g t) -> p g t", g=4)
        kT = M[:, N_R + N_Q:N_R + N_Q + N_K].rearrange("p (a t) -> p a t", a=2)
        CR = M[:, N_R + N_Q + N_K:N_R + N_Q + N_K + N_C].rearrange("p (a n) -> p a n", a=2)
        XS = N_R + N_Q + N_K + N_C - 2 * KD * T
        kcT = M[:, AT_KC:AT_KC + N_KC].rearrange("p (b n) -> p b n", b=B)
        vc = M[:, AT_KC + N_KC:AT_KC + N_KC + N_VC].rearrange("p (b n) -> p b n", b=B)
        OT = M[:, AT_KC + N_KC + N_VC:].rearrange("p (r g n) -> p r g n", r=3, g=4)
        over = nc.alloc_sbuf_tensor_at
        wi_hi = over("wi_hi", [P, 2, 16, P], FR, offset=at_m)
        wo_hi = [over("wo_hi%d" % p, [P, KF * P], FR, offset=at_m + 4 * (XS - (p + 1) * KF * P)) for p in range(2)]
        KH = (2 * KD, 2 * KD + 4, KF)
        h_hi = [over("h_hi%d" % n, [P, b - a, T], FR, offset=at_m + 4 * o)
                for n, (a, b, o) in enumerate(((0, KH[0], XS), (KH[0], KH[1], AT_KC), (KH[1], KH[2], 0)))]
        h_lo = over("h_lo", [P, KF, T], FR, offset=at_h)
        wi_lo = over("wi_lo", [P, 2, 16, P], FR, offset=at_wi)
        wm_hi = over("wm_hi", [P, 2, 16, P], FR, offset=at_wo)
        wo_lo = over("wo_lo", [P, 2, KF * P], FR, offset=at_wo)
        xs_flat = over("xs", [P, 2 * KD * T + P - NS], FR, offset=at_m + 4 * XS)
        xs = xs_flat[:, 0:2 * KD * T].rearrange("p (a k t) -> p a k t", a=2, k=KD)
        Qblk = sb("Qblk", [P, B, 2, TS, 4])
        hidb = sb("hidb", [HD, 4, 2, P])
        Z = sb("Z", [P, 3264])
        C = sb("C", [P, NCONST])
        PR = sb("PR", [P, NPAR])
        TRI = sb("TRI", [P, 2, P], BF16)
        peb = sb("peb", [HD, 2])
        sm = sb("sm", [P, 192])
        pt_sb = sb("pt_sb", [1, B * NPG], I32)
        PS = ctx.enter_context(nc.psum_tensor("PS", [P, 8, 512], F32))

        cat = R[:, :].rearrange("p (k t) -> p k t", k=KD)
        h = H[:, :].rearrange("p (k t) -> p k t", k=KF)
        pj = H[:, 0:5 * PJW].rearrange("p (t c) -> p t c", t=5)
        T9 = H[:, 5 * PJW:5 * PJW + 1024].rearrange("p (c h n) -> p c h n", c=2, h=2)
        kcTp = H[:, 5 * PJW + 1024:5 * PJW + 1024 + NC_P]
        vcp = H[0:32, 5 * PJW + 1056:5 * PJW + 1056 + P]
        knew = H[:, 5 * PJW + 1184:5 * PJW + 1184 + 2 * NS].rearrange("p (a n) -> p a n", a=2)
        sil = Z[:, 0:2 * T].rearrange("p (a h t) -> p a h t", a=2, h=2)
        sq = Z[:, 0:T]
        mu, rs = Z[:, 2 * T:3 * T], Z[:, 3 * T:4 * T]
        ysum, qsum = Z[:, 4 * T:5 * T], Z[:, 5 * T:6 * T]
        WOF = WO[:, :, :].rearrange("p a n -> p (a n)")
        pbuf = WOF[:, 0:3 * TP].rearrange("p (a n) -> p a n", a=3)
        cp_rows = WOF[:, 0:992]
        cp_cols = WOF[:, 1024:3072].rearrange("p (t h n) -> p t h n", t=2, h=2)
        equal = WOF[0:64, 3584:4484]
        Rw = WOF[:, 4608:5632]
        S = Z[:, 0:1024]
        ptbuf = WOF[:, 3 * TP:7 * TP].rearrange("p (a c n) -> p a c n", a=2, c=NT)
        Madd = Z[:, 2048:3072].rearrange("p (c r) -> p c r", c=NPG)
        W0 = WI[:, 0, :, :].rearrange("p k n -> p (k n)")
        colx, diag, rden = W0[:, 0:256], W0[:, 256:512], W0[:, 512:768]
        snew = W0[0:NS, 768:1024]
        quarter_sums = [Z[:, n * 256:(n + 1) * 256] for n in range(4)]
        slc_rows = Z[0:32, 1024:2048]
        mtmp = W0[:, 1024:1536]
        den, nmx = sm[:, 0:64], sm[:, 64:128]
        w8 = sm[:, 128:136]
        s2 = sm[:, 136:144]
        row_max = sm[:, 190:192]
        gst = sm[:, 144:174].rearrange("p (t s) -> p t s", t=5)
        gmv = sm[:, 174:184].rearrange("p (t s) -> p t s", t=5)
        grs = sm[:, 184:189]

        pooled = Z[:, 0:2 * T].rearrange("p (a t) -> p a t", a=2)
        pad = Z[:, 0:P - NS]

        def cst(n, rows=P):
            a, w = CONST[n]
            return C[0:rows, a:a + w]

        def prm(n, rows=P):
            a, w = PAR[n]
            return PR[0:rows, a:a + w]

        ident = cst("ident")
        ones = cst("ones")
        cos = cst("cos").rearrange("p (t d) -> p t d", t=5)
        sin = cst("sin").rearrange("p (t d) -> p t d", t=5)
        lnp = prm("ln").rearrange("p (s a k) -> p s a k", s=3, a=2)
        w1 = WI[:, 0, :, :]
        expand = WI[0:32, 1, :, :]
        w2 = prm("w2", HD).rearrange("p (c d) -> p c d", c=2)

        x_loaded, par_loaded, tab_loaded = sem("x_loaded"), sem("par_loaded"), sem("tab_loaded")
        con_loaded = sem("con_loaded")
        wi_full = [sem("wi_full0"), sem("wi_full1")]
        wo_full = [sem("wo_full0"), sem("wo_full1")]
        cr_full = [sem("cr_full0"), sem("cr_full1")]
        wi_done, wo_done, cr_freed = sem("wi_done"), sem("wo_done"), sem("cr_freed")
        sil_ready, gu_freed = sem("sil_ready"), sem("gu_freed")
        y_ready, y_added, sq_ready = sem("y_ready"), sem("y_added"), sem("sq_ready")
        sums_ready, stats_ready, var_ready, std_ready = (sem("sums_ready"), sem("stats_ready"), sem("var_ready"),
                                                         sem("std_ready"))
        xn_ready, x_ready = sem("xn_ready"), sem("x_ready")
        pj_ready, pj_freed, acts_done = sem("pj_ready"), sem("pj_freed"), sem("acts_done")
        rope_ready, gvar_ready, gstd_ready, gv_ready = (sem("rope_ready"), sem("gvar_ready"), sem("gstd_ready"),
                                                        sem("gv_ready"))
        tr_ready, tr_freed = sem("tr_ready"), sem("tr_freed")
        pe_ready, peb_ready = sem("pe_ready"), sem("peb_ready")
        cm_ready, cm_freed, hp_ready, hid_ready = sem("cm_ready"), sem("cm_freed"), sem("hp_ready"), sem("hid_ready")
        w2_ready, kc_ready = sem("w2_ready"), sem("kc_ready")
        sm_pe, sm_dve, sm_act, sm_toact = sem("sm_pe"), sem("sm_dve"), sem("sm_act"), sem("sm_toact")
        sk_ready, sk_freed = sem("sk_ready"), sem("sk_freed")
        cp_pe, cp_dve = sem("cp_pe"), sem("cp_dve")
        sc_ready, nm_ready, p_ready, pt_ready = sem("sc_ready"), sem("nm_ready"), sem("p_ready"), sem("pt_ready")
        weighted = sem("weighted")
        ptc_ready, pv_done, o_freed = sem("ptc_ready"), sem("pv_done"), sem("o_freed")
        gm_ready, gm_done = sem("gm_ready"), sem("gm_done")
        pd_ready, pd_done, pl_ready, pl_done = sem("pd_ready"), sem("pd_done"), sem("pl_ready"), sem("pl_done")
        ct_ready, ct_done = sem("ct_ready"), sem("ct_done")
        stored, out_stored = sem("stored"), sem("out_stored")
        set_up = sem("set_up")
        wi_rounded, wi_split = sem("wi_rounded"), sem("wi_split")
        wo_rounded, wo_split = sem("wo_rounded"), sem("wo_split")
        wm_rounded, wm_split = sem("wm_rounded"), sem("wm_split")
        cat_rounded, cat_split = sem("cat_rounded"), sem("cat_split")
        h_rounded, h_split = sem("h_rounded"), sem("h_split")
        x_split, first_split = sem("x_split"), sem("first_split")
        waited = sem("waited")

        def own(eng):
            eng.sem_inc(waited, 1)


        block = ctx.enter_context(nc.Block())

        @block.sync
        def _(sp):
            def load_wi(l, s, p):
                sp.wait_ge(wi_done, at(l, NWI, s + 1))
                sp.dma_start(WI[:, p, :, :], wi[ds(l * NWI + s, 1), :, :].rearrange("o p (k n) -> p (o k) n", k=16)
                             ).then_inc(wi_full[p], 16)

            def load_wo(l, s, p):
                sp.wait_ge(wo_done, at(l, NWO, s + 1))
                sp.dma_start(WO[:, p, :], wo[ds(l * NWO + s, 1), :, :].rearrange("o p n -> p (o n)")
                             ).then_inc(wo_full[p], 16)

            def ffn_in(l, bi, first):
                with sp.Fori(first, KF // 2) as i:
                    for p in range(2):
                        load_wi(l, bi + 2 * i + p, p)

            def ffn_out(l, bo):
                with sp.Fori(0, KD // 2) as i:
                    for p in range(2):
                        load_wo(l, bo + 2 * i + p, p)

            def load_pages(l, first, n, src, p, width):
                with sp.Fori(0, n // LOT) as g:
                    pages = nc.values_load_multi_w_load_instructions(
                        pt_sb[0:1, ds(first + LOT * g, LOT)], engines=[mybir.EngineType.SP],
                        min_val=0, max_val=NPHYS - 1)[1]
                    for j, page in enumerate(pages):
                        sp.dma_start(CR[:, p, ds((LOT * g + j) * width, width)],
                                     src[ds(l * NPHYS + page, 1), :, :].rearrange("o p n -> p (o n)")
                                     ).then_inc(cr_full[p], 16)

            sp.dma_start(x[:, :, :], x_in).then_inc(x_loaded, 16)
            load_wi(0, 0, 0)
            load_wi(0, 1, 1)
            sp.dma_start(pt_sb[:, :], table).then_inc(tab_loaded, 16)
            sp.dma_start(C[:, :], consts).then_inc(con_loaded, 16)
            sp.dma_start(TRI[:, :, :], tri).then_inc(con_loaded, 16)
            sp.wait_ge(tab_loaded, 16)
            own(sp)
            with sp.Fori(0, DEPTH) as l:
                ffn_in(l, 0, 1)
                load_wi(l, KF, 0)
                load_wi(l, KF + 1, 1)
                sp.wait_ge(wi_done, at(l, NWI, KF + 2))
                own(sp)
                with sp.Fori(0, B // 2) as i:
                    for p in range(2):
                        b = 2 * i + p
                        load_wo(l, b, p)
                        sp.wait_ge(cr_freed, at(l, NCR, b + 1))
                        own(sp)
                        load_pages(l, b * NPG, NPG, cmp_t, p, 256)
                with sp.Fori(0, NCH // 2) as i:
                    for p in range(2):
                        load_wo(l, KD + 2 * i + p, p)
                sp.wait_ge(wo_done, at(l, NWO, KD + NCH + 2))
                own(sp)
                def load_pairs(first, src):
                    with sp.Fori(0, B // 4) as i:
                        for p in range(2):
                            sp.wait_ge(cr_freed, at(l, NCR, first + 1 + 2 * i + p))
                            own(sp)
                            load_pages(l, (2 * i + p) * 2 * NPG, 2 * NPG, src, p, 128)

                load_pairs(B, slc_k)
                for p, src in ((0, win_k), (1, win_v)):
                    sp.wait_ge(cr_freed, at(l, NCR, B + 4 + p + 1))
                    sp.dma_start(CR[:, p, :], src[ds(l, 1), :, :].rearrange("o p n -> p (o n)")
                                 ).then_inc(cr_full[p], 16)
                load_pairs(B + 6, slc_v)
                with sp.Fori(0, 2) as i:
                    for p in range(2):
                        load_wi(l, KF + 2 + 2 * i + p, p)
                ffn_in(l, KF + 6, 0)
                ffn_out(l, KD + NCH)
                for p in range(2):
                    load_wi(l, NWI + p, p)
            sp.wait_ge(x_ready, 24 * DEPTH + 8 + 1)
            sp.dma_start(o_x, x[:, :, :]).then_inc(out_stored, 16)
            sp.wait_ge(out_stored, 16)
            sp.wait_ge(wi_full[1], 16 * at(DEPTH, NWI // 2, 1))

        @block.gpsimd
        def _(pool):
            nc.gpsimd.memset(Qblk[:, :, :, :, :], 0.0)
            nc.gpsimd.memset(gmv[:, :, :], 1.0)
            nc.gpsimd.memset(pad, 0.0)
            pool.drain()
            nc.gpsimd.tensor_tensor(xs_flat[:, 2 * KD * T:2 * KD * T + P - NS], pad, pad, ALU.subtract)
            pool.drain().then_inc(set_up, 1)
            def low_wo(n, p):
                pool.wait_ge(wo_rounded, n)
                nc.gpsimd.tensor_tensor(wo_lo[:, p, :], WO[:, p, :], wo_hi[p][:, :].bitcast(F32),
                                        ALU.subtract).then_inc(wo_split, 1)

            def low_x(n):
                for k in range(KD):
                    pool.wait_ge(x_ready, n + k)
                    nc.gpsimd.tensor_tensor(xs[:, 1, k, :], x[:, k, :], xs[:, 0, k, :].bitcast(F32),
                                            ALU.subtract).then_inc(x_split, 1)

            def low_first(n):
                pool.wait_ge(wi_rounded, n)
                nc.gpsimd.tensor_tensor(wi_lo[:, 0, :, :], WI[:, 0, :, :], wi_hi[:, 0, :, :].bitcast(F32),
                                        ALU.subtract).then_inc(first_split, 1)

            low_first(1)
            with pool.Fori(0, DEPTH) as l:
                pool.wait_ge(x_ready, at(l, 24, 8 + 1))
                own(pool)
                pool.dma_start(PR[:, :], par[ds(l, 1), :, :].rearrange("o p n -> p (o n)")).then_inc(par_loaded, 16)
                low_wo(at(l, NCH + KD, 1), 0)
                low_x(at(l, 24, 8 + 2))
                low_wo(at(l, NCH + KD, 2), 1)
                with pool.Fori(0, NCH // 2 - 1) as i:
                    for p in range(2):
                        low_wo(at(l, NCH + KD, p + 3) + 2 * i, p)
                pool.wait_ge(pj_freed, at(l, 30, 30 + 5))
                own(pool)
                lw = lambda t, n: t[ds(l, 1)].rearrange(n)
                pool.dma_start(lw(o_pool_p, "o s n -> (o s) n"), pj[P - 15:P, NT - 1, C_P:C_P + 256]).then_inc(stored, 16)
                ops = lw(o_pool_s, "o b s n -> (o b) s n")
                pool.dma_start(ops[:, 0:11, :], lw(hist_rows, "o b s n -> (o b) s n")[:, 4:15, :]).then_inc(stored, 16)
                pool.dma_start(lw(o_pool_s, "o b s n -> (o b) s n")[:, 11:15, :],
                               pj[0:NS, NT, C_P:C_P + 256]).then_inc(stored, 16)
                ows = lw(o_win_s, "o b s n -> (o b) s n")
                pool.dma_start(ows[:, 0:508, :], lw(win_rows, "o b s n -> (o b) s n")[:, 4:512, :]).then_inc(stored, 16)
                pool.wait_ge(rope_ready, at(l, 5, 5))
                own(pool)
                for i, (op, os) in enumerate(((o_cmp_p, o_cmp_s), (o_slc_p, o_slc_s), (o_win_p, None))):
                    c0 = C_KV + 256 * i
                    pool.dma_start(op[ds(l, 1)].rearrange("o (t p) n -> p (o t) n", p=P),
                                   pj[:, 0:NT, c0:c0 + 256]).then_inc(stored, 16)
                    if os is not None:
                        pool.dma_start(lw(os, "o s n -> (o s) n"), pj[0:NS, NT, c0:c0 + 256]).then_inc(stored, 16)
                    else:
                        pool.dma_start(ows[:, 508:512, :], pj[0:NS, NT, c0:c0 + 256]).then_inc(stored, 16)
                pool.wait_ge(gv_ready, at(l, 1, 1))
                own(pool)
                pool.dma_start(lw(o_gv, "o s n -> (o s) n"), pj[0:NS, NT, C_V:C_V + 256]).then_inc(stored, 16)
                for n in range(4):
                    pool.wait_ge(wm_rounded, at(l, 4, n + 1))
                    nc.gpsimd.tensor_tensor(wi_lo[:, n % 2, :, :], WI[:, n % 2, :, :],
                                            wm_hi[:, n % 2, :, :].bitcast(F32), ALU.subtract).then_inc(wm_split, 1)
                low_first(at(l, 2 * KF, KF + 1))
                low_x(at(l, 24, 16 + 2))
                with pool.Fori(0, KD // 2) as i:
                    for p in range(2):
                        low_wo(at(l, NCH + KD, NCH + p + 1) + 2 * i, p)
                low_first(at(l, 2 * KF, 2 * KF + 1))
                low_x(at(l, 24, 24 + 2))
            pool.wait_ge(stored, 16 * 11 * DEPTH)

        @block.tensor
        def _(pe):
            def mm(out, lhsT, rhs, start, stop):
                return nc.tensor.matmul(out, lhsT, rhs, start=start, stop=stop, skip_group_check=True)

            def three(out, ws, xk, first, last):
                for n, (i, j) in enumerate(((0, 0), (0, 1), (1, 0))):
                    r = mm(out, ws[i], xk[j], first and n == 0, last and n == 2)
                return r

            def ffn_in(l, f, bi, x_at):
                def item(n, p, first=False):
                    if first:
                        pe.wait_ge(first_split, at(l, 2, f + 1))
                    else:
                        pe.wait_ge(wi_split, at(l, 2 * (KF - 1), (KF - 1) * f) + n)
                    pe.wait_ge(gu_freed, at(l, 44, 22 * f + 1) + n)
                    own(pe)
                    for k in range(KD):
                        if first:
                            pe.wait_ge(x_split, at(l, 24, x_at + k + 1))
                        for side in range(2):
                            for a in range(2):
                                last = three(PS[:, 4 * p + 2 * side + a, 0:TH],
                                             [w[:, p, 8 * side + k, :] for w in (wi_hi, wi_lo)],
                                             [xs[:, part, k, a * TH:(a + 1) * TH] for part in range(2)],
                                             k == 0, k == KD - 1)
                    last.then_inc(wi_done, 1)

                item(0, 0, True)
                item(1, 1)
                with pe.Fori(0, (KF - 2) // 4) as i:
                    for q in range(4):
                        item(4 * i + q + 2, q % 2)

            def ffn_out_3(l, bo, y0):
                def item(i, p, first=False):
                    pe.wait_ge(wo_split, at(l, NCH + KD, NCH + p + 1) + 2 * i)
                    pe.wait_ge(y_added, at(l, 24, y0 + p + 1) + 2 * i)
                    own(pe)
                    for k in range(KF):
                        n = (k >= KH[0]) + (k >= KH[1])
                        hi = h_hi[n][:, k - (0, KH[0], KH[1])[n], :]
                        if first and k % 2 == 0:
                            pe.wait_ge(h_split, at(l, KF // 2, k // 2 + 1))
                        for a in range(2):
                            last = three(PS[:, 2 * p + a, 0:TH],
                                         [w[:, k * P:(k + 1) * P] for w in (wo_hi[p], wo_lo[:, p, :])],
                                         [hi[:, a * TH:(a + 1) * TH], h_lo[:, k, a * TH:(a + 1) * TH]],
                                         k == 0, k == KF - 1)
                    last.then_inc(wo_done, 1)

                item(0, 0, True)
                item(0, 1)
                with pe.Fori(1, KD // 2) as i:
                    for p in range(2):
                        item(i, p)

            def ffn_out(l, f, bo, y0, beside):
                pe.wait_ge(gu_freed, at(l, 44, 22 * (f + 1) + 2))
                own(pe)

                def item(i, p, first=False):
                    pe.wait_ge(wo_full[p], 16 * (at(l, NWO // 2, bo // 2 + 1) + i))
                    pe.wait_ge(y_added, at(l, 24, y0 + p + 1) + 2 * i)
                    own(pe)
                    if not first:
                        beside(i, p, 0)
                    for k in range(KF):
                        for a in range(2):
                            last = mm(PS[:, 2 * p + a, 0:TH], WO[:, p, k * P:(k + 1) * P],
                                      h[:, k, a * TH:(a + 1) * TH], k == 0, k == KF - 1)
                    last.then_inc(wo_done, 1)
                    if first:
                        beside(i, p, 0)
                    beside(i, p, 1)

                item(0, 0, True)
                item(0, 1)
                with pe.Fori(1, KD // 2) as i:
                    for p in range(2):
                        item(i, p)

            def ln_stats(l, s):
                pe.wait_ge(sums_ready, at(l, 3, s + 1))
                for i, src in enumerate((ysum, qsum)):
                    for a in range(2):
                        last = mm(PS[:, 4 + 2 * i + a, 0:TH], ones, src[:, a * TH:(a + 1) * TH], True, True)
                    last.then_inc(stats_ready, 1)

            def project(l):
                def product(p, t, k):
                    return three(PS[:, t, 0:CW],
                                 [xs_flat[:, o:o + P] for o in (k * T + t * P, (KD + k) * T + t * P)],
                                 [w[:, k * CW:(k + 1) * CW] for w in (wo_hi[p], wo_lo[:, p, :])],
                                 k == 0, k == KD - 1)

                def chunk(i, p):
                    pe.wait_ge(wo_split, at(l, NCH + KD, p + 1) + 2 * i)
                    for t in range(5):
                        pe.wait_ge(pj_freed, at(l, 30, 5 * p + t + 1) + 10 * i)
                        for k in range(KD):
                            last = product(p, t, k)
                        last.then_inc(pj_ready, 1)
                    pe.drain().then_inc(wo_done, 1)

                pe.wait_ge(wo_split, at(l, NCH + KD, 1))
                pe.wait_ge(pj_freed, at(l, 30, 5))
                own(pe)
                for k in range(KD):
                    pe.wait_ge(x_split, at(l, 24, 8 + (k + 2 if k < KD - 1 else KD)))
                    for t in range(5):
                        last = product(0, t, k)
                        if k == KD - 1:
                            last.then_inc(pj_ready, 1)
                pe.drain().then_inc(wo_done, 1)
                chunk(0, 1)
                with pe.Fori(1, NCH // 2) as i:
                    for p in range(2):
                        chunk(i, p)

            def rows_to_cols(l):
                pe.wait_ge(pj_freed, at(l, 30, 30 + 5))
                pe.wait_ge(rope_ready, at(l, 5, 5))
                own(pe)
                for u in range(10):
                    pe.wait_ge(tr_freed, at(l, 10, u + 1))
                    if u >= 8:
                        own(pe)
                    bank = PS[:, 5 + u % 2, :]
                    if u < 8:
                        for t in range(NT):
                            if u < 4:
                                src = pj[:, t, u * P:(u + 1) * P]
                            else:
                                c0 = (C_KV + 256, C_KV + 512, C_KV, C_KV + 128)[u - 4]
                                src = pj[:, t, c0:c0 + P]
                            last = nc.tensor.transpose(bank[:, t * P:(t + 1) * P], src, ident)
                    elif u == 8:
                        for g in range(4):
                            last = nc.tensor.transpose(bank[:, g * NS:(g + 1) * NS], pj[0:NS, NT, g * P:(g + 1) * P],
                                                       ident[0:NS, 0:NS])
                    else:
                        for i in range(2):
                            last = nc.tensor.transpose(bank[:, i * NS:(i + 1) * NS],
                                                       pj[0:NS, NT, C_KV + 256 * (i + 1):C_KV + 256 * (i + 1) + P],
                                                       ident[0:NS, 0:NS])
                    last.then_inc(tr_ready, 1)

            def hidden(v, prompt=False):
                for j in range(8):
                    for kv in range(2 if prompt else 1):
                        if prompt:
                            out = PS[:, 4 + v % 2, kv * 32:kv * 32 + 32]
                            src = T9[:, v, kv, :].rearrange("p (n j) -> p n j", j=8)[:, :, j]
                        else:
                            out = PS[:, 4 + v % 2, 0:256]
                            o = v % 2 * P + j * 16
                            src = CR[:, v // 2, :].rearrange("p (g n) -> p g n", g=NPG)[:, :, o:o + 16]
                        last = mm(out, w1[:, 8 * (v % 2) + j, :], src, j == 0 and kv == 0, j == 7)
                last.then_inc(cm_ready, 1)

            def compressed(base, v, n):
                c, hb = v % 2, hidb[:, 2 + v % 2, :, :]
                pe.wait_ge(hid_ready, base + v + 2)
                pe.wait_ge(kc_ready, base + v + 1)
                own(pe)
                if c == 0:
                    last = mm(PS[0:HD, 6, 0:2 * n], w2[:, 0, :], hb[:, :, 0:n], True, True)
                else:
                    for kv in range(2):
                        last = mm(PS[0:n, 7, kv * HD:(kv + 1) * HD], hb[:, kv, 0:n], w2[:, 1, :], True, True)
                last.then_inc(w2_ready, 1)

            def compress_pe(l):
                pe.wait_ge(wi_full[0], 16 * at(l, NWI // 2, KF // 2 + 1))
                pe.wait_ge(par_loaded, 16 * at(l, 1, 1))
                pe.wait_ge(gu_freed, at(l, 44, 22 + 2))
                pev = prm("pe").rearrange("p (c a j) -> p c a j", c=2, a=2)
                for c in range(2):
                    for a in range(2):
                        for j in range(8):
                            last = mm(PS[0:HD, 7, c:c + 1], w1[:, 8 * c + j, a * HD:(a + 1) * HD],
                                      pev[:, c, a, j:j + 1], (a, j) == (0, 0), (a, j) == (1, 7))
                last.then_inc(pe_ready, 1)
                pe.wait_ge(peb_ready, at(l, 1, 1))

            def compress_beside(l):
                def beside(i, p, after):
                    base = at(l, 18, 0) + 4 * i
                    if not after:
                        pe.wait_ge(cr_full[p], 16 * (at(l, CR_DMAS, NPG) + NPG * i))
                    for v in (2 * p, 2 * p + 1):
                        if after:
                            compressed(base, v, NC_S)
                        else:
                            pe.wait_ge(cm_freed, base + v + 1)
                            hidden(v)
                    if not after:
                        pe.drain().then_inc(cr_freed, 1)
                return beside

            def compress_prompt(l):
                base = at(l, 18, 16)
                pe.wait_ge(tr_freed, at(l, 10, 10 + 2))
                for v in range(2):
                    pe.wait_ge(cm_freed, base + v + 1)
                    hidden(v, True)
                for v in range(2):
                    compressed(base, v, NC_P)

            def cmp_scores(l):
                pe.wait_ge(sk_freed, at(l, 8, 4 + 2))
                own(pe)
                for b in range(B):
                    last = mm(PS[0:NC_S, 6, b * 32:(b + 1) * 32], kcT[:, b, :], Qblk[:, b, :, :, :], b == 0, True)
                last.then_inc(sm_pe, 1)

            def cmp_turn(l):
                pe.wait_ge(sm_dve, at(l, 18, 1))
                for a in range(2):
                    last = nc.tensor.transpose(PS[:, 7, a * NC_S:(a + 1) * NC_S], S[0:NC_S, a * P:(a + 1) * P],
                                               ident[0:NC_S, 0:NC_S])
                last.then_inc(sm_pe, 1)

            def cmp_turn_back(l):
                pe.wait_ge(sm_dve, at(l, 18, 2))
                for a in range(2):
                    last = nc.tensor.transpose(PS[0:NC_S, 6, a * P:(a + 1) * P],
                                               S[:, 256 + a * NC_S:256 + (a + 1) * NC_S], ident)
                last.then_inc(sm_pe, 1)

            def cmp_output(l):
                pe.wait_ge(sm_dve, at(l, 18, 3))
                mm(PS[0:64, 7, 0:32], S[0:NC_S, 768:832], cst("selmap", NC_S), True, True)
                for b in range(B):
                    last = mm(PS[:, 5, b * 32:(b + 1) * 32], vc[0:NC_S, b, :], S[0:NC_S, 512 + b * 32:544 + b * 32],
                              b == 0, True)
                last.then_inc(sm_pe, 1)

            def turn_selection(l):
                pe.wait_ge(sm_dve, at(l, 18, 4))
                own(pe)
                nc.tensor.transpose(PS[0:32, 7, 0:64], S[0:64, 832:864], ident[0:64, 0:64]).then_inc(sm_pe, 1)

            def expand_selection(l):
                pe.wait_ge(sm_dve, at(l, 18, 5))
                pe.wait_ge(wi_full[1], 16 * at(l, NWI // 2, KF // 2 + 1))
                for c in range(NPG):
                    last = mm(PS[:, 6 + c // 8, c % 8 * 64:c % 8 * 64 + 64], expand[:, c, :], S[0:32, 864:928],
                              c % 8 == 0, True)
                last.then_inc(sm_pe, 1)

            def win_scores(l):
                pe.wait_ge(sk_freed, at(l, 8, 8 + 2))
                own(pe)
                pe.wait_ge(cr_full[0], 16 * at(l, CR_DMAS, 8 * NPG + 1))
                for b in range(B):
                    for c in range(NW):
                        mm(PS[:, 6 + b // 4, (b % 4 * NW + c) * 32:(b % 4 * NW + c + 1) * 32],
                           CR[:, 0, b * 512 + c * P:b * 512 + (c + 1) * P], Qblk[:, b, :, :, :],
                           b % 4 == 0 and c == 0, True)
                mm(PS[0:NS, 5, 0:256], knew[:, 1, :], Qblk[:, :, :, :, :], True, True).then_inc(sm_pe, 1)
                pe.drain().then_inc(cr_freed, 1)

            def turn_maxima(l, d):
                pe.wait_ge(sm_dve, at(l, 18, d))
                for a in range(2):
                    last = nc.tensor.transpose(PS[:, 6, a * P:(a + 1) * P], colx[:, a * P:(a + 1) * P], ident)
                last.then_inc(sm_pe, 1)

            def spread_maxima(l, d):
                pe.wait_ge(sm_dve, at(l, 18, d))
                mm(PS[:, 7, 0:256], ones, diag, True, True).then_inc(sm_pe, 1)

            def denominators(l, d, sums):
                pe.wait_ge(sm_dve, at(l, 18, d))
                for n, part in enumerate(sums):
                    last = mm(PS[:, 6, 0:256], ones, part, n == 0, n == len(sums) - 1)
                last.then_inc(sm_pe, 1)

            def win_values(l):
                c0 = C_KV + 512 + P
                mm(PS[:, 5, 0:256], pj[0:NS, NT, c0:c0 + P], snew, True, False)
                pe.wait_ge(cr_full[1], 16 * at(l, CR_DMAS, 8 * NPG + 1))
                pw = Rw.rearrange("p (c r) -> p c r", c=NW)
                for b in range(B):
                    for c in range(NW):
                        last = mm(PS[:, 5, b * 32:(b + 1) * 32], CR[:, 1, (b * NW + c) * P:(b * NW + c + 1) * P],
                                  pw[:, c, b * 32:(b + 1) * 32], False, b == B - 1 and c == NW - 1)
                last.then_inc(sm_pe, 1)
                pe.drain().then_inc(cr_freed, 1)

            def slc_scores(l, j):
                p = j % 2
                if j == 0:
                    pe.wait_ge(sm_toact, at(l, 7, 1))
                if j == 2:
                    pe.wait_ge(sm_dve, at(l, 18, 6))
                pe.wait_ge(cr_full[p], 16 * at(l, CR_DMAS, 4 * NPG + 2 * NPG * (j // 2 + 1)))
                for q in range(2):
                    b = 2 * j + q
                    pe.wait_ge(sk_freed, at(l, 8, b + 1))
                    for c in range(NPG):
                        last = mm(PS[:, 6 + q, c * 32:(c + 1) * 32], CR[:, p, (q * NPG + c) * P:(q * NPG + c + 1) * P],
                                  Qblk[:, b, :, :, :], c == 0, True)
                    last.then_inc(sk_ready, 1)
                pe.drain().then_inc(cr_freed, 1)

            def slc_new_scores(l):
                pe.wait_ge(sm_dve, at(l, 18, 11))
                mm(PS[0:NS, 5, 0:256], knew[:, 0, :], Qblk[:, :, :, :, :], True, True).then_inc(sm_pe, 1)

            def slc_values(l, j):
                p = j % 2
                out = lambda b: PS[0:32, 5 + b // 4 * 2, b % 4 * P:(b % 4 + 1) * P]
                c0 = C_KV + 256 + P
                if j == 0:
                    for b in range(B):
                        mm(out(b), snew[:, b * 32:(b + 1) * 32], pj[0:NS, NT, c0:c0 + P], b % 4 == 0, False)
                pe.wait_ge(cr_full[p], 16 * at(l, CR_DMAS, 8 * NPG + 1 + 2 * NPG * (j // 2 + 1)))
                own(pe)
                pv = R[:, 0:4096].rearrange("p (c r) -> p c r", c=NPG)
                for q in range(2):
                    b = 2 * j + q
                    for c in range(NPG):
                        last = mm(out(b), pv[:, c, b * 32:(b + 1) * 32],
                                  CR[:, p, (q * NPG + c) * P:(q * NPG + c + 1) * P], False,
                                  b % 4 == 3 and c == NPG - 1)
                if j == 3:
                    last.then_inc(sm_pe, 1)
                pe.drain().then_inc(cr_freed, 1)

            def slc_turn(l):
                pe.wait_ge(sm_dve, at(l, 18, 15))
                own(pe)
                for b in range(B):
                    last = nc.tensor.transpose(PS[:, 6, b * 32:(b + 1) * 32], slc_rows[:, b * P:(b + 1) * P],
                                               ident[0:32, 0:32])
                last.then_inc(sm_pe, 1)

            def turn_outputs(l):
                pe.wait_ge(sm_dve, at(l, 18, 16))
                for br in range(3):
                    for g in range(4):
                        last = nc.tensor.transpose(PS[0:NS, 5 + br, g * P:(g + 1) * P], OT[:, br, g, :], ident)
                last.then_inc(sm_pe, 1)

            def give_back(l):
                pe.wait_ge(sm_dve, at(l, 18, 18))
                pe.wait_ge(o_freed, at(l, 16, 16))
                pe.drain().then_inc(wi_done, 2)

            def prompt_compressed(l):
                pe.wait_ge(kc_ready, at(l, 18, 18 + 2))
                for t in range(NT):
                    for hh in range(8):
                        g, kv = hh // 2, hh % 2
                        last = mm(PS[:, 4 * kv + t, g * NC_P:(g + 1) * NC_P],
                                  qT[kv * HD:kv * HD + HD, g, t * P:(t + 1) * P],
                                  kcTp[kv * HD:kv * HD + HD, :], g == 0, True)
                last.then_inc(cp_pe, 1)
                slc_scores(l, 0)
                for t, turning in CP_STEPS:
                    if turning:
                        if t == 0:
                            pe.wait_ge(cp_dve, at(l, 9, 1))
                        for hh in range(8):
                            o = t * 248 + hh * NC_P
                            last = nc.tensor.transpose(PS[0:NC_P, 4 - t % 2 * 4 + hh // 4, hh % 4 * P:(hh % 4 + 1) * P],
                                                       cp_rows[:, o:o + NC_P], ident)
                    else:
                        pe.wait_ge(cp_dve, at(l, 9, 2 + CP_STEPS.index((t, 1))))
                        if t == 0:
                            pe.wait_ge(sk_freed, at(l, 8, 2 + 2))
                            own(pe)
                        for kv in range(2):
                            last = mm(PS[:, 6 - t % 2 * 4 + kv, :], vcp[0:NC_P, :],
                                      cp_cols[0:NC_P, t % 2, kv, :], True, True)
                    last.then_inc(cp_pe, 1)

            def prompt_attention(l, pieces):
                def unit(u):
                    return u // 16, u // 4 % 4, u // 2 % 2, u % 2

                def scores(u):
                    t, g, br, kv = unit(u)
                    n = (t + 1) * P
                    if u >= 2:
                        pe.wait_ge(p_ready, at(l, 64, u - 1))
                    r = slice(kv * HD, kv * HD + HD)
                    mm(PS[:, u % 2, 0:n], qT[r, g, t * P:(t + 1) * P], kT[r, br, 0:n], True, False)
                    mm(PS[:, u % 2, n - P:n], TRI[:, 1, :], TRI[:, 0, :], False, True).then_inc(sc_ready, 1)

                def turn(u):
                    t, g, br, kv = unit(u)
                    pe.wait_ge(weighted, at(l, 64, u + 1))
                    if u >= 2:
                        pe.wait_ge(ptc_ready, at(l, 64, u - 1))
                    for c in range(t + 1):
                        last = nc.tensor.transpose(PS[:, 2 + u % 2, c * P:(c + 1) * P],
                                                   pbuf[:, u % 3, c * P:(c + 1) * P], ident)
                    last.then_inc(pt_ready, 1)

                def times_v(w):
                    t, g, br, _ = unit(2 * w)
                    pe.wait_ge(ptc_ready, at(l, 64, 2 * w + 2))
                    if br == 0 and w >= 2:
                        pe.wait_ge(o_freed, at(l, 16, w // 2))
                    c0 = C_KV + 256 * (br + 1) + P
                    for c in range(t + 1):
                        last = mm(PS[:, 4, 0:2 * P], pj[:, c, c0:c0 + P], ptbuf[:, w % 2, c, :],
                                  br == 0 and c == 0, br == 1 and c == t)
                    last.then_inc(pv_done, 1)

                pe.wait_ge(cp_dve, at(l, 9, 9))
                for u in range(64 + 3):
                    if u < 64:
                        scores(u)
                    if 2 <= u < 66:
                        turn(u - 2)
                    if u >= 4 and u % 2 == 0:
                        times_v(u // 2 - 2)
                    if u in pieces:
                        pieces[u]()

            def gating(l):
                pe.wait_ge(gv_ready, at(l, 1, 1))
                for t in range(5):
                    r = ROWS[t]
                    w = (prm("ws") if t < NT else prm("wss", NS)).rearrange("p (h t) -> p h t", h=4)
                    for hh in range(4):
                        last = mm(PS[0:r, t % 2, hh * HD:(hh + 1) * HD] if t < 2 else
                                  PS[0:r, (0, 1, 2, 3, 4)[t], hh * HD:(hh + 1) * HD], w[:, hh, :],
                                  pj[0:r, t, C_V + hh * HD:C_V + (hh + 1) * HD], hh == 0, True)
                    last.then_inc(gm_ready, 1)

            def pooling(l):
                band = cst("band").rearrange("p (g t) -> p g t", g=4)
                band0 = cst("band0").rearrange("p (g t) -> p g t", g=4)
                bandh = cst("bandh", 120).rearrange("p (g t) -> p g t", g=4)
                bandn = cst("bandn", NS).rearrange("p (g t) -> p g t", g=4)
                def means(g):
                    c0, bank = C_P + g * HD, 5 - g % 2 * 3
                    if g == 1:
                        pe.wait_ge(gm_done, at(l, 5, 5))
                        own(pe)
                    for t in range(NT):
                        z = pj[:, t, c0:c0 + HD]
                        if t == 0:
                            mm(PS[0:HD, bank, 0:16], z, band0[:, g, :], True, False)
                            mm(PS[0:HD, bank, 16:P], z, band[:, g, 16:P], False, False)
                        else:
                            mm(PS[0:HD, bank, t * P:(t + 1) * P], z, band[:, g, 0:P], False, False)
                            mm(PS[0:HD, bank, t * P:t * P + 15], pj[:, t - 1, c0:c0 + HD], band[:, g, P:P + 15],
                               False, t == NT - 1)
                    mm(PS[0:HD, bank + 1, 0:NS], pj[0:NS, NT, c0:c0 + HD], bandn[:, g, :], True, False)
                    mm(PS[0:HD, bank + 1, 0:NS], prm("hist", 120)[:, g * HD:(g + 1) * HD], bandh[:, g, :], False,
                       True).then_inc(pd_ready, 1)

                pw = prm("pw", HD).rearrange("p (g e) -> p g e", g=4)
                means(0)
                for g in range(4):
                    if g < 3:
                        means(g + 1)
                    pe.wait_ge(pd_done, at(l, 4, g + 1))
                    if g >= 1:
                        pe.wait_ge(pl_done, at(l, 4, g))
                    own(pe)
                    for a in range(2):
                        last = mm(PS[0:HD, (7, 4)[a], 0:TH], pw[:, g, :],
                                  pooled[0:HD, g % 2, a * TH:(a + 1) * TH], True, True)
                    last.then_inc(pl_ready, 1)

            def turn_rows(l):
                for k in range(4):
                    last = nc.tensor.transpose(PS[:, 0, k * NS:(k + 1) * NS], pj[0:NS, NT, k * P:(k + 1) * P],
                                               ident[0:NS, 0:NS])
                last.then_inc(ct_ready, 1)
                for k in range(2):
                    if k:
                        pe.wait_ge(ct_done, at(l, 3, 1))
                    c0 = C_U + k * P
                    for t in range(NT):
                        nc.tensor.transpose(PS[:, 2 - 2 * k, t * P:(t + 1) * P], pj[:, t, c0:c0 + P], ident)
                    nc.tensor.transpose(PS[:, 3 - 2 * k, 0:NS], pj[0:NS, NT, c0:c0 + P], ident[0:NS, 0:NS])\
                        .then_inc(ct_ready, 1)

            def mixer_out(l):
                for n in range(KD // 2):
                    pe.wait_ge(wm_split, at(l, 4, n + 1))
                    for q in range(2):
                        pe.wait_ge(y_added, at(l, 24, 8 + 2 * n + q + 1))
                        own(pe)
                        for k in range(KD):
                            if n == 0 and q == 0:
                                pe.wait_ge(cat_split, at(l, KD, k + 1))
                            for a in range(2):
                                last = three(PS[:, 2 * q + a, 0:TH],
                                             [w[:, n % 2, 8 * q + k, :] for w in (wm_hi, wi_lo)],
                                             [xs[:, part, k, a * TH:(a + 1) * TH] for part in range(2)],
                                             k == 0, k == KD - 1)
                        last.then_inc(y_ready, 1)
                    pe.drain().then_inc(wi_done, 1)

            pe.sem_inc(wi_done, 2)
            pe.sem_inc(w2_ready, 2)
            pe.sem_inc(wo_done, 2)
            pe.sem_inc(cr_freed, 2)
            pe.wait_ge(con_loaded, 32)
            pe.wait_ge(x_loaded, 16)
            pe.wait_ge(set_up, 1)
            own(pe)
            with pe.Fori(0, DEPTH) as l:
                ffn_in(l, 0, 0, 0)
                compress_pe(l)
                ffn_out(l, 0, 0, 0, compress_beside(l))
                ln_stats(l, 0)
                project(l)
                rows_to_cols(l)
                compress_prompt(l)
                prompt_compressed(l)
                prompt_attention(l, {
                    AT["keys_1"]: lambda: slc_scores(l, 1), AT["cmp_scores"]: lambda: cmp_scores(l),
                    AT["cmp_turn"]: lambda: cmp_turn(l), AT["cmp_turn_back"]: lambda: cmp_turn_back(l),
                    AT["cmp_output"]: lambda: cmp_output(l), AT["turn_selection"]: lambda: turn_selection(l),
                    AT["expand"]: lambda: expand_selection(l),
                    AT["keys_2"]: lambda: slc_scores(l, 2), AT["keys_3"]: lambda: slc_scores(l, 3),
                    AT["win_scores"]: lambda: win_scores(l), AT["win_maxima"]: lambda: turn_maxima(l, 7),
                    AT["win_spread"]: lambda: spread_maxima(l, 8),
                    AT["win_values"]: lambda: (denominators(l, 9, [colx]), win_values(l)),
                    AT["slc_new"]: lambda: slc_new_scores(l), AT["slc_maxima"]: lambda: turn_maxima(l, 12),
                    AT["slc_spread"]: lambda: spread_maxima(l, 13),
                    AT["slc_values"]: lambda: (denominators(l, 14, quarter_sums), slc_values(l, 0)),
                    AT["slc_values_1"]: lambda: slc_values(l, 1), AT["slc_values_2"]: lambda: slc_values(l, 2),
                    AT["slc_values_3"]: lambda: slc_values(l, 3), AT["slc_turn"]: lambda: slc_turn(l),
                    AT["turn_outputs"]: lambda: turn_outputs(l)})
                give_back(l)
                gating(l)
                pooling(l)
                turn_rows(l)
                mixer_out(l)
                ln_stats(l, 1)
                ffn_in(l, 1, KF + 6, 16)
                ffn_out_3(l, KD + NCH, 16)
                ln_stats(l, 2)

        @block.scalar
        def _(act):
            def af(out, in_, func, **kw):
                return nc.scalar.activation(out, in_, func, **kw)

            def round_wi(l, bi, p, i):
                act.wait_ge(wi_full[p], 16 * (at(l, NWI // 2, bi // 2 + 1) + i))
                af(wi_hi[:, p, :, :], WI[:, p, :, :], ACT.Copy).then_inc(wi_rounded, 1)

            def round_wo(l, bo, p, i):
                act.wait_ge(wo_full[p], 16 * (at(l, NWO // 2, bo // 2 + 1) + i))
                af(wo_hi[p][:, :], WO[:, p, :], ACT.Copy).then_inc(wo_rounded, 1)

            def ffn_in(l, f, bi):
                def silu(i, p):
                    act.wait_ge(wi_done, at(l, NWI, (KF + 6) * f + p + 3) + 2 * i)
                    act.wait_ge(gu_freed, at(l, 44, 22 * f + p + 1) + 2 * i)
                    af(sil[:, p, :, :], PS[:, 4 * p:4 * p + 2, 0:TH], ACT.Silu).then_inc(sil_ready, 1)

                with act.Fori(0, KF // 2 - 1) as i:
                    for p in range(2):
                        silu(i, p)
                        round_wi(l, bi, p, i + 1)
                silu(KF // 2 - 1, 0)
                if f == 1:
                    round_wo(l, KD + NCH, 0, 0)
                silu(KF // 2 - 1, 1)

            def round_h(l):
                with act.Fori(0, KH[0] // 2) as i:
                    act.wait_ge(gu_freed, at(l, 44, KF + 2 + 2) + 2 * i)
                    af(h_hi[0][:, ds(2 * i, 2), :], h[:, ds(2 * i, 2), :], ACT.Copy).then_inc(h_rounded, 1)
                round_wo(l, KD + NCH, 1, 0)
                for j in range(2):
                    k = KH[0] + 2 * j
                    act.wait_ge(gu_freed, at(l, 44, KF + k + 2 + 2))
                    af(h_hi[1][:, 2 * j:2 * j + 2, :], h[:, k:k + 2, :], ACT.Copy).then_inc(h_rounded, 1)
                act.wait_ge(gu_freed, at(l, 44, 2 * KF + 2))
                af(h_hi[2][:, :, :], h[:, KH[1]:KF, :], ACT.Copy).then_inc(h_rounded, 1)

            def round_wm(l, n):
                act.wait_ge(wi_full[n % 2], 16 * at(l, NWI // 2, (KF + 2) // 2 + 1 + n // 2))
                af(wm_hi[:, n % 2, :, :], WI[:, n % 2, :, :], ACT.Copy).then_inc(wm_rounded, 1)

            def mixer_out(l):
                for k in range(KD):
                    act.wait_ge(ct_done, at(l, 3, min(max(k - 2, 1), 3)))
                    af(xs[:, 0, k, :], cat[:, k, :], ACT.Copy).then_inc(cat_rounded, 1)
                round_wm(l, 1)
                for k in range(KD):
                    act.wait_ge(y_added, at(l, 24, 8 + k + 3))
                    af(sq, x[:, k, :], ACT.Square).then_inc(sq_ready, 1)
                    if k in (1, 3):
                        round_wm(l, k // 2 + 2)

            def squares_3(l):
                def square(i, p):
                    act.wait_ge(y_added, at(l, 24, 16 + p + 3) + 2 * i)
                    af(sq, x[:, ds(2 * i + p, 1), :].rearrange("p o t -> p (o t)"), ACT.Square).then_inc(sq_ready, 1)

                with act.Fori(0, KD // 2 - 1) as i:
                    for p in range(2):
                        square(i, p)
                        round_wo(l, KD + NCH, p, i + 1)
                for p in range(2):
                    square(KD // 2 - 1, p)

            def squares(l, beside):
                with act.Fori(0, KD // 2) as i:
                    for p in range(2):
                        beside(i, p)
                        act.wait_ge(y_added, at(l, 24, p + 3) + 2 * i)
                        af(sq, x[:, ds(2 * i + p, 1), :].rearrange("p o t -> p (o t)"), ACT.Square)\
                            .then_inc(sq_ready, 1)

            def ln(l, s):
                act.wait_ge(var_ready, at(l, 3, s + 1))
                af(rs, rs, ACT.Sqrt, bias=cst("eps")).then_inc(std_ready, 1)
                act.wait_ge(par_loaded, 16 * at(l, 1, 1))
                for k in range(KD):
                    act.wait_ge(xn_ready, at(l, 24, 8 * s + k + 1))
                    af(xs[:, 0, k, :], x[:, k, :], ACT.Identity, bias=lnp[:, s, 1, k:k + 1],
                       scale=lnp[:, s, 0, k:k + 1])
                    act.drain()
                    af(x[:, k, :], x[:, k, :], ACT.Identity, bias=lnp[:, s, 1, k:k + 1],
                       scale=lnp[:, s, 0, k:k + 1]).then_inc(x_ready, 1)

            def project(l):
                def take(i, p):
                    for t in range(5):
                        r = ROWS[t]
                        act.wait_ge(pj_ready, at(l, 30, 5 * p + t + 1) + 10 * i)
                        af(pj[0:r, t, ds(2 * CW * i + CW * p, CW)], PS[0:r, t, 0:CW], ACT.Copy)\
                            .then_inc(pj_freed, 1)

                with act.Fori(0, NCH // 2 - 1) as i:
                    for p in range(2):
                        take(i, p)
                        round_wo(l, KD, p, i + 1)
                for p in range(2):
                    take(NCH // 2 - 1, p)
                act.drain()
                for r, ts in ((P, slice(0, NT)), (NS, slice(NT, 5))):
                    af(pj[0:r, ts, C_GT:C_GT + 24], pj[0:r, ts, C_GT:C_GT + 24], ACT.Sigmoid)
                for r, ts in ((P, slice(0, NT)), (NS, slice(NT, 5))):
                    last = af(pj[0:r, ts, C_U:C_U + 512], pj[0:r, ts, C_U:C_U + 512], ACT.Gelu_apprx_tanh)
                last.then_inc(acts_done, 1)

            def gelu(base, v, n):
                act.wait_ge(hp_ready, base + v + 1)
                act.wait_ge(w2_ready, base + v + 1)
                af(hidb[:, 2 + v % 2, :, 0:n], hidb[:, 0, :, 0:n], ACT.Gelu_apprx_tanh,
                   bias=peb[:, v % 2:v % 2 + 1]).then_inc(hid_ready, 1)

            def compress_pe(l):
                act.wait_ge(pe_ready, at(l, 1, 1))
                af(peb[:, :], PS[0:HD, 7, 0:2], ACT.Copy)
                act.drain().then_inc(peb_ready, 1)

            def compress_beside(l):
                def beside(i, p):
                    for v in (2 * p, 2 * p + 1):
                        gelu(at(l, 18, 0) + 4 * i, v, NC_S)
                return beside

            def cmp_exp(l):
                act.wait_ge(sm_toact, at(l, 7, 2))
                for a in range(2):
                    last = af(S[:, 256 + a * NC_S:256 + (a + 1) * NC_S], PS[:, 7, a * NC_S:(a + 1) * NC_S], ACT.Exp,
                              bias=s2[:, 2 + a:3 + a], scale=SCALE, accum_out=s2[:, 4 + a:5 + a])
                last.then_inc(sm_act, 1)

            def cols_exp(l, scores, k):
                act.wait_ge(sm_toact, at(l, 7, k))
                af(scores, scores, ACT.Exp, scale=SCALE)
                af(snew, snew, ACT.Exp, scale=SCALE).then_inc(sm_act, 1)

            def slc_exp(l, n):
                act.wait_ge(sm_toact, at(l, 7, 4 + n))
                if n == 0:
                    af(snew, snew, ACT.Exp, scale=SCALE)
                af(R[:, n * 1024:(n + 1) * 1024], R[:, n * 1024:(n + 1) * 1024], ACT.Exp, scale=SCALE)\
                    .then_inc(sm_act, 1)

            def key_scores(l, j):
                for q in range(2):
                    b = 2 * j + q
                    act.wait_ge(sk_ready, at(l, 8, b + 1))
                    af(R[:, 0:4096].rearrange("p (c n) -> p c n", c=NPG)[:, :, b * 32:b * 32 + 32],
                       PS[:, 6 + q, :].rearrange("p (c n) -> p c n", c=NPG), ACT.Copy).then_inc(sk_freed, 1)

            def prompt_compressed(l):
                act.wait_ge(sm_toact, at(l, 7, 1))
                af(cp_rows, cp_rows, ACT.Exp, scale=SCALE).then_inc(sm_act, 1)
                key_scores(l, 0)

            def prompt_attention(l):
                def turned(u):
                    t, w = u // 16, u // 2
                    n = (t + 1) * P
                    act.wait_ge(pt_ready, at(l, 64, u + 1))
                    if w >= 2:
                        act.wait_ge(pv_done, at(l, 32, w - 1))
                    af(ptbuf[:, w % 2, 0:t + 1, u % 2 * P:(u % 2 + 1) * P],
                       PS[:, 2 + u % 2, 0:n].rearrange("p (c n) -> p c n", n=P), ACT.Copy).then_inc(ptc_ready, 1)

                for u in range(64 + 3):
                    if u >= 3:
                        turned(u - 3)
                    if u < 64:
                        n = (u // 16 + 1) * P
                        act.wait_ge(nm_ready, at(l, 64, u + 1))
                        if u >= 3:
                            act.wait_ge(pt_ready, at(l, 64, u - 2))
                        af(pbuf[:, u % 3, 0:n], PS[:, u % 2, 0:n], ACT.Exp, bias=nmx[:, u:u + 1], scale=SCALE,
                           accum_out=den[:, u:u + 1]).then_inc(p_ready, 1)
                    for j, name in ((1, "keys_1"), (2, "keys_2"), (3, "keys_3")):
                        if u == AT[name] + 1:
                            key_scores(l, j)
                    if u == AT["cmp_turn"] + 1:
                        cmp_exp(l)
                    if u == AT["win_spread"] + 1:
                        cols_exp(l, Rw, 3)
                    if u - AT["slc_spread"] - 2 in range(4):
                        slc_exp(l, u - AT["slc_spread"] - 2)

            def pooling(l):
                for g in range(4):
                    if g == 1:
                        round_wm(l, 0)
                    act.wait_ge(pl_ready, at(l, 4, g + 1))
                    for a in range(2):
                        last = af(cat[g % 2 * HD:g % 2 * HD + HD, 6 + g // 2, a * TH:(a + 1) * TH],
                                  PS[0:HD, (7, 4)[a], 0:TH], ACT.Copy, scale=prm("ps", HD)[:, g:g + 1])
                    last.then_inc(pl_done, 1)
                act.drain()

            act.sem_inc(hid_ready, 1)
            act.sem_inc(x_ready, 1)
            act.sem_inc(sk_freed, 2)
            act.wait_ge(x_loaded, 16)
            for k in range(KD):
                af(xs[:, 0, k, :], x[:, k, :], ACT.Copy).then_inc(x_ready, 1)
            round_wi(0, 0, 0, 0)
            with act.Fori(0, DEPTH) as l:
                round_wi(l, 0, 1, 0)
                ffn_in(l, 0, 0)
                compress_pe(l)
                squares(l, compress_beside(l))
                round_wo(l, KD, 0, 0)
                ln(l, 0)
                round_wo(l, KD, 1, 0)
                project(l)
                act.wait_ge(gvar_ready, at(l, 1, 1))
                act.wait_ge(con_loaded, 32)
                af(grs, gmv[:, :, 1], ACT.Sqrt, bias=cst("eps")).then_inc(gstd_ready, 1)
                for v in range(2):
                    gelu(at(l, 18, 16), v, NC_P)
                prompt_compressed(l)
                prompt_attention(l)
                pooling(l)
                mixer_out(l)
                round_wi(l, KF + 6, 0, 0)
                ln(l, 1)
                round_wi(l, KF + 6, 1, 0)
                ffn_in(l, 1, KF + 6)
                round_h(l)
                squares_3(l)
                round_wi(l, NWI, 0, 0)
                ln(l, 2)

        @block.vector
        def _(dve):
            V = nc.vector

            def settle():
                dve.drain()

            def tt(out, a, b, op):
                return V.tensor_tensor(out, a, b, op)

            def ffn_in(l, f):
                def low_wi(n, p, done):
                    dve.wait_ge(wi_rounded, at(l, 2 * KF, KF * f + 1) + n)
                    tt(wi_lo[:, p, :, :], WI[:, p, :, :], wi_hi[:, p, :, :].bitcast(F32), ALU.subtract)\
                        .then_inc(done, 1)

                def product(i, p):
                    dve.wait_ge(sil_ready, at(l, 44, 22 * f + p + 1) + 2 * i)
                    V.scalar_tensor_tensor(h[:, ds(2 * i + p, 1), :].rearrange("p o (a t) -> p (o a) t", a=2),
                                           sil[:, p, :, :], 0.5, PS[:, 4 * p + 2:4 * p + 4, 0:TH],
                                           ALU.mult, ALU.mult).then_inc(gu_freed, 1)

                low_wi(1, 1, wi_split)
                with dve.Fori(0, KF // 2 - 1) as i:
                    for p in range(2):
                        product(i, p)
                        low_wi(2 * i + p + 2, p, wi_split)
                for p in range(2):
                    product(KF // 2 - 1, p)

            def low_h(l):
                with dve.Fori(0, KH[0] // 2) as i:
                    dve.wait_ge(h_rounded, at(l, KF // 2, 1) + i)
                    tt(h_lo[:, ds(2 * i, 2), :], h[:, ds(2 * i, 2), :], h_hi[0][:, ds(2 * i, 2), :].bitcast(F32),
                       ALU.subtract).then_inc(h_split, 1)
                for n, k in ((1, KH[0]), (1, KH[0] + 2), (2, KH[1])):
                    dve.wait_ge(h_rounded, at(l, KF // 2, k // 2 + 1))
                    o = k - KH[n - 1]
                    tt(h_lo[:, k:k + 2, :], h[:, k:k + 2, :], h_hi[n][:, o:o + 2, :].bitcast(F32), ALU.subtract)\
                        .then_inc(h_split, 1)

            def add_y(l, s, beside=None):
                V.memset(ysum, 0.0)
                V.memset(qsum, 0.0)
                settle()
                with dve.Fori(0, KD // 2) as i:
                    for p in range(2):
                        if beside:
                            beside(i, p, 0)
                        if s == 1:
                            dve.wait_ge(y_ready, at(l, KD, p + 1) + 2 * i)
                        else:
                            dve.wait_ge(wo_done, at(l, NWO, (KD + NCH) * (s // 2) + p + 3) + 2 * i)
                        xk = x[:, ds(2 * i + p, 1), :].rearrange("p o t -> p (o t)")
                        V.scalar_tensor_tensor(xk.rearrange("p (a t) -> p a t", a=2),
                                               xk.rearrange("p (a t) -> p a t", a=2), ALPHA,
                                               PS[:, 2 * p:2 * p + 2, 0:TH], ALU.mult, ALU.add)
                        dve.drain().then_inc(y_added, 1)
                        tt(ysum, ysum, xk, ALU.add)
                        dve.wait_ge(sq_ready, at(l, 24, 8 * s + p + 1) + 2 * i)
                        tt(qsum, qsum, sq, ALU.add)
                        if beside:
                            beside(i, p, 1)
                        settle()
                dve.sem_inc(sums_ready, 1)

            def ln(l, s):
                h2 = lambda a: a.rearrange("p (a t) -> p a t", a=2)
                dve.wait_ge(stats_ready, at(l, 6, 2 * s + 1))
                V.tensor_scalar(h2(mu), PS[:, 4:6, 0:TH], 1.0 / D, None, ALU.mult)
                settle()
                tt(rs, mu, mu, ALU.mult)
                settle()
                dve.wait_ge(stats_ready, at(l, 6, 2 * s + 2))
                V.scalar_tensor_tensor(h2(rs), PS[:, 6:8, 0:TH], 1.0 / D, h2(rs), ALU.mult, ALU.subtract)\
                    .then_inc(var_ready, 1)
                for k in range(2):
                    tt(x[:, k, :], x[:, k, :], mu, ALU.subtract)
                dve.wait_ge(std_ready, at(l, 3, s + 1))
                V.reciprocal(rs, rs)
                settle()
                for k in range(KD):
                    if k >= 2:
                        tt(x[:, k, :], x[:, k, :], mu, ALU.subtract)
                        settle()
                    tt(x[:, k, :], x[:, k, :], rs, ALU.mult).then_inc(xn_ready, 1)

            def rope(l):
                dve.wait_ge(pj_freed, at(l, 30, 5 * -(-C_GT // CW) + 5))
                for t in range(5):
                    r = ROWS[t]
                    ta, tb = Z[0:r, 0:896], Z[0:r, 896:1792]
                    q = pj[0:r, t, 0:512].rearrange("p (n a d) -> p n a d", n=8, a=2)
                    ks = [pj[0:r, t, C_KV + 256 * i:C_KV + 256 * i + P].rearrange("p (n a d) -> p n a d", n=2, a=2)
                          for i in range(3)]
                    parts = [(q, 0, 8)] + [(ks[i], 512 + P * i, 2) for i in range(3)]
                    if t:
                        settle()
                    for src, o, n in parts:
                        for tab, buf in ((cos, ta), (sin, tb)):
                            cs = tab[0:r, t, :].rearrange("p (o d) -> p o d", o=1).to_broadcast([r, 2 * n, 32])
                            tt(buf[:, o:o + n * HD].rearrange("p (m d) -> p m d", d=32),
                               src.rearrange("p n a d -> p (n a) d"), cs, ALU.mult)
                    settle()
                    for src, o, n in parts:
                        a = ta[:, o:o + n * HD].rearrange("p (n a d) -> p n a d", n=n, a=2)
                        b = tb[:, o:o + n * HD].rearrange("p (n a d) -> p n a d", n=n, a=2)
                        tt(src[:, :, 0, :], a[:, :, 0, :], b[:, :, 1, :], ALU.subtract)
                        last = tt(src[:, :, 1, :], a[:, :, 1, :], b[:, :, 0, :], ALU.add)
                    last.then_inc(rope_ready, 1)

            def gv_norm(l):
                dve.wait_ge(par_loaded, 16 * at(l, 1, 1))
                ws = prm("ws").rearrange("p (h t) -> p h t", h=4)
                wss = prm("wss", NS).rearrange("p (h t) -> p h t", h=4)
                for hh in range(4):
                    tt(ws[:, hh, :], ws[:, hh, :], cst("tril"), ALU.mult)
                    tt(wss[:, hh, :], wss[:, hh, :], cst("trils", NS), ALU.mult)
                dve.wait_ge(acts_done, at(l, 1, 1))
                for t in range(5):
                    V.bn_stats(gst[0:ROWS[t], t, :], pj[0:ROWS[t], t, C_V:C_V + 256])
                settle()
                for t in range(5):
                    V.bn_aggr(gmv[0:ROWS[t], t, :], gst[0:ROWS[t], t, :])
                settle()
                dve.sem_inc(gvar_ready, 1)
                dve.wait_ge(gstd_ready, at(l, 1, 1))
                V.reciprocal(grs, grs)
                settle()
                for t in range(5):
                    r = ROWS[t]
                    v = pj[0:r, t, C_V:C_V + 256]
                    V.tensor_scalar(v, v, gmv[0:r, t, 0:1], grs[0:r, t:t + 1], ALU.subtract, ALU.mult)
                settle()
                for op, o in ((ALU.mult, 0), (ALU.add, 256)):
                    for t in range(5):
                        r = ROWS[t]
                        v = pj[0:r, t, C_V:C_V + 256]
                        tt(v, v, prm("gmgb", r)[:, o:o + 256], op)
                    settle()
                dve.sem_inc(gv_ready, 1)

            def rows_to_cols(l):
                for u in range(10):
                    dve.wait_ge(tr_ready, at(l, 10, u + 1))
                    bank = PS[:, 5 + u % 2, :]
                    if u < 4:
                        last = V.tensor_copy(qT[:, u, :], bank)
                    elif u < 6:
                        last = V.tensor_copy(kT[:, u - 4, :], bank)
                    elif u < 8:
                        for kv in range(2):
                            for j in range(2):
                                last = V.tensor_copy(T9[j * HD:(j + 1) * HD, u - 6, kv, :],
                                                     bank[kv * HD:(kv + 1) * HD, :]
                                                     .rearrange("p (n j) -> p n j", j=2)[:, :, j])
                    elif u == 8:
                        for kv in range(2):
                            s = slice(kv * HD, (kv + 1) * HD)
                            last = V.tensor_copy(Qblk[s, :, kv, :, :],
                                                 bank[s, 0:P].rearrange("p (g b t) -> p b t g", g=4, b=B))
                    else:
                        last = V.tensor_copy(knew[:, :, :], bank[:, 0:2 * NS].rearrange("p (a n) -> p a n", a=2))
                    last.then_inc(tr_freed, 1)

            def hidden_sum(base, v, n, pages):
                dve.wait_ge(cm_ready, base + v + 1)
                dve.wait_ge(hid_ready, base + v + 1)
                for half in range(2):
                    s = PS[half * HD:(half + 1) * HD, 4 + v % 2, 0:2 * n]
                    if pages:
                        for kv in range(2):
                            V.tensor_copy(hidb[:, half, kv, 0:n].rearrange("p (g n) -> p g n", g=NPG),
                                          s.rearrange("p (g h n) -> p h g n", g=NPG, h=2)[:, kv, :, :])
                    else:
                        V.tensor_copy(hidb[:, half, :, 0:n], s.rearrange("p (h n) -> p h n", h=2))
                dve.drain().then_inc(cm_freed, 1)
                tt(hidb[:, 0, :, 0:n - 1], hidb[:, 0, :, 0:n - 1], hidb[:, 1, :, 1:n], ALU.add)\
                    .then_inc(hp_ready, 1)

            def compressed(base, v, n, b):
                dve.wait_ge(w2_ready, base + v + 3)
                if v % 2 == 0:
                    for kv in range(2):
                        s = slice(kv * HD, (kv + 1) * HD)
                        out = kcTp[s, :] if b is None else kcT[s, ds(b, 1), :].rearrange("p o n -> p (o n)")
                        last = V.tensor_copy(out, PS[0:HD, 6, kv * n:(kv + 1) * n])
                else:
                    out = vcp[0:n, :] if b is None else vc[0:n, ds(b, 1), :].rearrange("p o n -> p (o n)")
                    last = V.tensor_copy(out, PS[0:n, 7, 0:P])
                last.then_inc(kc_ready, 1)

            def compress_beside(l):
                def beside(i, p, after):
                    for v in (2 * p, 2 * p + 1):
                        if after:
                            compressed(at(l, 18, 0) + 4 * i, v, NC_S, 2 * i + p)
                        else:
                            hidden_sum(at(l, 18, 0) + 4 * i, v, P, True)
                return beside

            def compress_prompt(l):
                for v in range(2):
                    hidden_sum(at(l, 18, 16), v, 32, False)
                for v in range(2):
                    compressed(at(l, 18, 16), v, NC_P, None)

            def take_out(br, scaled, bank):
                for kv in range(2):
                    s = slice(kv * HD, (kv + 1) * HD)
                    for b in range(1):
                        src = PS[s, bank, 0:256].rearrange("p (b h r) -> p b h r", b=B, h=2)[:, :, kv, :]
                        dst = OT[s, br, :, :].rearrange("p g (b t) -> p b t g", b=B)
                        if scaled:
                            rd = rden[s, :].rearrange("p (b h r) -> p b h r", b=B, h=2)[:, :, kv, :]
                            last = tt(dst, src.rearrange("p b (t g) -> p b t g", g=4),
                                      rd.rearrange("p b (t g) -> p b t g", g=4), ALU.mult)
                        else:
                            last = V.tensor_copy(dst, src.rearrange("p b (t g) -> p b t g", g=4))
                return last

            def col_maxima(l, sc, n):
                V.tensor_reduce(colx, sc.rearrange("p (c r) -> p r c", c=n), X, ALU.max)
                settle()
                tt(colx[0:NS, :], colx[0:NS, :], snew, ALU.max).then_inc(sm_dve, 1)

            def on_diagonal(l, k):
                dve.wait_ge(sm_pe, at(l, 18, k))
                V.tensor_reduce(s2[:, 0:2], PS[:, 6, 0:256].rearrange("p (a n) -> p a n", a=2), X, ALU.max)
                settle()
                for a in range(2):
                    last = V.tensor_scalar(diag[:, a * P:(a + 1) * P], ident, s2[:, a:a + 1], None, ALU.mult)
                last.then_inc(sm_dve, 1)

            def less_maxima(l, sc, n, k):
                dve.wait_ge(sm_pe, at(l, 18, k))
                V.tensor_copy(rden, PS[:, 7, 0:256])
                settle()
                sr = sc.rearrange("p (c r) -> p c r", c=n)
                tt(sr, sr, rden.rearrange("p (o r) -> p o r", o=1).to_broadcast([P, n, 256]), ALU.subtract)
                tt(snew, snew, rden[0:NS, :], ALU.subtract)
                dve.drain().then_inc(sm_toact, 1)

            def col_sums(l, sc, n, k):
                dve.wait_ge(sm_act, at(l, 7, k))
                V.tensor_reduce(colx, sc.rearrange("p (c r) -> p r c", c=n), X, ALU.add)
                settle()
                tt(colx[0:NS, :], colx[0:NS, :], snew, ALU.add).then_inc(sm_dve, 1)

            def reciprocals(l, k):
                dve.wait_ge(sm_pe, at(l, 18, k))
                V.reciprocal(rden, PS[:, 6, 0:256])
                settle()

            def cmp_scores(l):
                dve.wait_ge(sm_pe, at(l, 18, 1))
                V.tensor_copy(S[0:NC_S, 0:256], PS[0:NC_S, 6, 0:256]).then_inc(sm_dve, 1)

            def cmp_maxima(l):
                dve.wait_ge(sm_pe, at(l, 18, 2))
                V.tensor_reduce(s2[:, 0:2], PS[:, 7, 0:2 * NC_S].rearrange("p (a n) -> p a n", a=2), X, ALU.max)
                settle()
                V.tensor_scalar(s2[:, 2:4], s2[:, 0:2], -SCALE, None, ALU.mult).then_inc(sm_toact, 1)

            def cmp_normalise(l):
                dve.wait_ge(sm_act, at(l, 7, 2))
                V.reciprocal(s2[:, 6:8], s2[:, 4:6])
                settle()
                for a in range(2):
                    pr = S[:, 256 + a * NC_S:256 + (a + 1) * NC_S]
                    last = V.tensor_scalar(pr, pr, s2[:, 6 + a:7 + a], None, ALU.mult)
                last.then_inc(sm_dve, 1)

            def cmp_columns(l):
                dve.wait_ge(sm_pe, at(l, 18, 3))
                V.tensor_copy(S[0:NC_S, 512:768], PS[0:NC_S, 6, 0:256])
                settle()
                V.tensor_reduce(S[0:NC_S, 768:832], S[0:NC_S, 512:768].rearrange("p (r g) -> p r g", g=4), X, ALU.add)\
                    .then_inc(sm_dve, 1)

            imp, sel = S[0:64, 928:960], S[0:64, 832:864]
            g3 = Z[0:64, 1024:1924].rearrange("p (j i) -> p j i", i=30)
            e3 = equal.rearrange("p (j i) -> p j i", i=30)
            row = lambda a: a.rearrange("p (o i) -> p o i", o=1).to_broadcast([64, 30, 30])
            col = lambda a: a.rearrange("p (j o) -> p j o", o=1).to_broadcast([64, 30, 30])

            def rank_ties(l):
                dve.wait_ge(sm_pe, at(l, 18, 4))
                take_out(0, False, 5)
                V.tensor_copy(imp, PS[0:64, 7, 0:32])
                settle()
                tt(g3, row(imp[:, 1:31]), col(imp[:, 1:31]), ALU.is_equal)
                tt(e3, row(cst("idx", 64)), col(cst("idx", 64)), ALU.is_lt)
                settle()
                tt(e3, e3, g3, ALU.mult)
                settle()

            def rank(l):
                tt(g3, row(imp[:, 1:31]), col(imp[:, 1:31]), ALU.is_gt)
                settle()
                tt(g3, g3, e3, ALU.add)
                V.memset(sel, 1.0)
                settle()
                V.tensor_reduce(S[0:64, 960:990], g3, X, ALU.add)
                settle()
                V.tensor_scalar(sel[:, 1:31], S[0:64, 960:990], NTOP - 0.5, None, ALU.is_lt).then_inc(sm_dve, 1)

            def selection(l):
                dve.wait_ge(sm_pe, at(l, 18, 5))
                V.tensor_copy(S[0:32, 864:928], PS[0:32, 7, 0:64]).then_inc(sm_dve, 1)

            def selection_mask(l):
                dve.wait_ge(sm_pe, at(l, 18, 6))
                V.tensor_scalar(Madd.rearrange("p (a c) r -> p a (c r)", a=2), PS[:, 6:8, :], 1.0, -NEG,
                                ALU.subtract, ALU.mult)
                dve.drain().then_inc(sm_dve, 1)

            def win_scores(l):
                dve.wait_ge(sm_pe, at(l, 18, 7))
                sw = Rw.rearrange("p (c b r) -> p c b r", c=NW, b=B)
                for a in range(2):
                    V.tensor_copy(sw[:, :, 4 * a:4 * a + 4, :],
                                  PS[:, 6 + a, :].rearrange("p (b c r) -> p c b r", b=4, c=NW))
                tt(snew, PS[0:NS, 5, 0:256], cst("nadd", NS), ALU.add)
                settle()
                tt(sw[:, 0, :, :], sw[:, 0, :, :],
                   cst("wadd").rearrange("p (o r) -> p o r", o=1).to_broadcast([P, B, 32]), ALU.add)
                settle()
                col_maxima(l, Rw, NW)

            def win_output(l):
                reciprocals(l, 10)
                dve.sem_inc(sm_dve, 1)
                dve.wait_ge(sm_pe, at(l, 18, 11))
                take_out(2, True, 5)
                dve.drain().then_inc(sm_dve, 1)

            def mask_keys(l, half):
                dve.wait_ge(sk_freed, at(l, 8, 8 + 2))
                own(dve)
                c0, n = half * NPG // 2, NPG // 2
                for b in range(B):
                    sc = R[:, 0:4096].rearrange("p (c r g) -> p c r g", c=NPG, g=4)[:, c0:c0 + n, b * 8:b * 8 + 8, :]
                    tt(sc, sc, Madd[:, c0:c0 + n, b * 8:b * 8 + 8].rearrange("p c (r o) -> p c r o", o=1)
                       .to_broadcast([P, n, 8, 4]), ALU.add)
                settle()

            def slc_new_scores(l):
                dve.wait_ge(sm_pe, at(l, 18, 12))
                tt(snew, PS[0:NS, 5, 0:256], cst("nadd", NS), ALU.add)
                settle()
                col_maxima(l, R[:, 0:4096], NPG)

            def slc_less_maxima(l, n):
                if n == 0:
                    dve.wait_ge(sm_pe, at(l, 18, 14))
                    V.tensor_copy(rden, PS[:, 7, 0:256])
                    settle()
                    tt(snew, snew, rden[0:NS, :], ALU.subtract)
                sr = R[:, n * 1024:(n + 1) * 1024].rearrange("p (c r) -> p c r", c=4)
                tt(sr, sr, rden.rearrange("p (o r) -> p o r", o=1).to_broadcast([P, 4, 256]), ALU.subtract)
                dve.drain().then_inc(sm_toact, 1)

            def slc_sums(l, n):
                dve.wait_ge(sm_act, at(l, 7, 4 + n))
                V.tensor_reduce(quarter_sums[n], R[:, n * 1024:(n + 1) * 1024].rearrange("p (c r) -> p r c", c=4),
                                X, ALU.add)
                if n == 0:
                    settle()
                    tt(quarter_sums[0][0:NS, :], quarter_sums[0][0:NS, :], snew, ALU.add)
                if n == 3:
                    dve.drain().then_inc(sm_dve, 1)

            def slc_copy(l):
                dve.wait_ge(sm_pe, at(l, 18, 16))
                V.tensor_copy(slc_rows[:, 0:512], PS[0:32, 5, :])
                V.tensor_copy(slc_rows[:, 512:1024], PS[0:32, 7, :])
                dve.drain().then_inc(sm_dve, 1)

            def slc_output(l):
                dve.wait_ge(sm_pe, at(l, 18, 17))
                take_out(1, True, 6)
                dve.drain().then_inc(sm_dve, 1)

            def sample_merge(l):
                dve.wait_ge(sm_pe, at(l, 18, 18))
                merge(NS, NT, lambda br: PS[0:NS, 5 + br, :].rearrange("p (g h d) -> p g h d", g=4, h=2),
                      mtmp[0:NS, :])
                dve.drain().then_inc(sm_dve, 2)

            def gates(t, br):
                return pj[:, t, C_GT:C_GT + 24].rearrange("p (h g b) -> p h g b", h=2, g=4)[:, :, :, br]

            def gate(r, t, br):
                return pj[0:r, t, C_GT:C_GT + 24].rearrange("p (h g b) -> p g h b", h=2, g=4)[:, :, :, br:br + 1]\
                    .to_broadcast([r, 4, 2, HD])

            def merge(r, t, src, tmp):
                out = pj[0:r, t, 0:512].rearrange("p (g h d) -> p g h d", g=4, h=2)
                t4 = tmp.rearrange("p (g h d) -> p g h d", g=4, h=2)
                for br in range(3):
                    tt(out if br == 0 else t4, src(br), gate(r, t, br), ALU.mult)
                    settle()
                    if br:
                        tt(out, out, t4, ALU.add)
                        settle()

            def prompt_compressed(l):
                dve.wait_ge(cp_pe, at(l, 9, 1))
                for t in range(NT):
                    for kv in range(2):
                        o = t * 248 + kv * 124
                        tt(cp_rows[:, o:o + 124].rearrange("p (h n) -> p h n", h=4),
                           PS[:, 4 * kv + t, 0:124].rearrange("p (h n) -> p h n", h=4),
                           cst("cadd")[:, t * 31:(t + 1) * 31].rearrange("p (o n) -> p o n", o=1)
                           .to_broadcast([P, 4, NC_P]), ALU.add)
                settle()
                sc = cp_rows.rearrange("p (u n) -> p u n", u=32)
                m32 = Z[:, 0:32]
                mb = lambda: m32.rearrange("p (u o) -> p u o", o=1).to_broadcast([P, 32, NC_P])
                V.tensor_reduce(m32, sc, X, ALU.max)
                settle()
                tt(sc, sc, mb(), ALU.subtract)
                settle()
                dve.sem_inc(sm_toact, 1)
                dve.wait_ge(sm_act, at(l, 7, 1))
                V.tensor_reduce(m32, sc, X, ALU.add)
                settle()
                V.reciprocal(m32, m32)
                settle()
                for t in range(NT):
                    mt = m32[:, 8 * t:8 * t + 8].rearrange("p (h g) -> p h g", h=2)
                    tt(mt, mt, gates(t, 0), ALU.mult)
                for t in range(NT):
                    st = cp_rows[:, t * 248:(t + 1) * 248].rearrange("p (h n) -> p h n", h=8)
                    V.scalar_tensor_tensor(st, cst("cadd")[:, t * 31:(t + 1) * 31].rearrange("p (o n) -> p o n", o=1)
                                           .to_broadcast([P, 8, NC_P]), -1.0, st, ALU.is_ge, ALU.mult)
                settle()
                tt(sc, sc, mb(), ALU.mult).then_inc(cp_dve, 1)
                for n, (t, turning) in enumerate(CP_STEPS):
                    dve.wait_ge(cp_pe, at(l, 9, 2 + n))
                    if turning:
                        last = V.tensor_copy(cp_cols[0:NC_P, t % 2, :, :], PS[0:NC_P, 4 - t % 2 * 4:6 - t % 2 * 4, :])
                    else:
                        for kv in range(2):
                            s = slice(kv * HD, kv * HD + HD)
                            last = V.tensor_copy(pj[s, t, 0:512], PS[s, 6 - t % 2 * 4 + kv, :])
                    last.then_inc(cp_dve, 1)

            def prompt_attention(l, pieces):
                def maxima(u):
                    n = (u // 16 + 1) * P
                    dve.wait_ge(sc_ready, at(l, 64, u + 1))
                    V.tensor_reduce(row_max[:, u % 2:u % 2 + 1], PS[:, u % 2, 0:n], X, ALU.max)
                    settle()
                    V.tensor_scalar(nmx[:, u:u + 1], row_max[:, u % 2:u % 2 + 1], -SCALE, None, ALU.mult)\
                        .then_inc(nm_ready, 1)

                def weights(u):
                    t, g, br, kv = u // 16, u // 4 % 4, u // 2 % 2, u % 2
                    n = (t + 1) * P
                    dve.wait_ge(p_ready, at(l, 64, u + 1))
                    V.reciprocal(w8[:, u % 2:u % 2 + 1], den[:, u:u + 1])
                    settle()
                    gt = C_GT + 3 * (4 * kv + g) + br + 1
                    V.tensor_scalar(pbuf[:, u % 3, 0:n], pbuf[:, u % 3, 0:n], w8[:, u % 2:u % 2 + 1],
                                    pj[:, t, gt:gt + 1], ALU.mult, ALU.mult).then_inc(weighted, 1)

                def take(i):
                    t, g = i // 4, i % 4
                    dve.wait_ge(pv_done, at(l, 32, 2 * i + 2))
                    for kv in range(2):
                        s = slice(kv * HD, kv * HD + HD)
                        o = pj[s, t, g * P:(g + 1) * P]
                        tt(o, o, PS[s, 4, kv * P:(kv + 1) * P], ALU.add)
                    dve.drain().then_inc(o_freed, 1)

                for u in range(64 + 4):
                    if u < 64:
                        maxima(u)
                    if 1 <= u <= 64:
                        weights(u - 1)
                    if u >= 7 and (u - 7) % 4 == 0:
                        take((u - 7) // 4)
                    if u in pieces:
                        pieces[u]()

            def gather_outputs(l):
                for g in range(4):
                    V.tensor_copy(cat[:, g, 0:TP].rearrange("p (t n) -> p t n", t=NT), pj[:, 0:NT, g * P:(g + 1) * P])

            def gating(l):
                for t in range(5):
                    r = ROWS[t]
                    dve.wait_ge(gm_ready, at(l, 5, t + 1))
                    b = (prm("gmb") if t < NT else prm("gmbs", NS)).rearrange("p (h o) -> p h o", o=1)\
                        .to_broadcast([r, 4, HD])
                    tmp = Z[0:r, 1088:1344].rearrange("p (h d) -> p h d", h=4)
                    tt(tmp, PS[0:r, t, 0:256].rearrange("p (h d) -> p h d", h=4), b, ALU.add)
                    settle()
                    u = pj[0:r, t, C_U:C_U + 256]
                    tt(u, u, Z[0:r, 1088:1344], ALU.mult).then_inc(gm_done, 1)
                    settle()

            def pooling(l):
                for g in range(4):
                    dve.wait_ge(pd_ready, at(l, 4, g + 1))
                    if g >= 2:
                        dve.wait_ge(pl_ready, at(l, 4, g - 1))
                    bank = 5 - g % 2 * 3
                    V.tensor_copy(pooled[0:HD, g % 2, 0:TP], PS[0:HD, bank, :])
                    V.tensor_copy(pooled[0:HD, g % 2, TP:T], PS[0:HD, bank + 1, 0:NS])
                    dve.drain().then_inc(pd_done, 1)

            def turn_rows(l):
                dve.wait_ge(ct_ready, at(l, 3, 1))
                V.tensor_copy(cat[:, 0:4, TP:T], PS[:, 0, 0:4 * NS].rearrange("p (k n) -> p k n", k=4))
                dve.drain().then_inc(ct_done, 1)
                for k in range(2):
                    dve.wait_ge(ct_ready, at(l, 3, k + 2))
                    V.tensor_copy(cat[:, 4 + k, 0:TP], PS[:, 2 - 2 * k, :])
                    V.tensor_copy(cat[:, 4 + k, TP:T], PS[:, 3 - 2 * k, 0:NS])
                    dve.drain().then_inc(ct_done, 1)

            for s, n in ((gu_freed, 2), (y_added, 2), (pj_freed, 5), (tr_freed, 2), (cm_freed, 2), (kc_ready, 2)):
                dve.sem_inc(s, n)
            dve.wait_ge(con_loaded, 32)
            dve.wait_ge(x_loaded, 16)
            dve.wait_ge(set_up, 1)
            own(dve)
            for k in range(KD):
                dve.wait_ge(x_ready, 2 + k)
                tt(xs[:, 1, k, :], x[:, k, :], xs[:, 0, k, :].bitcast(F32), ALU.subtract).then_inc(x_split, 1)
            with dve.Fori(0, DEPTH) as l:
                ffn_in(l, 0)
                add_y(l, 0, compress_beside(l))
                ln(l, 0)
                rope(l)
                rows_to_cols(l)
                gv_norm(l)
                compress_prompt(l)
                prompt_compressed(l)
                prompt_attention(l, {
                    AT["cmp_scores"] + 1: lambda: cmp_scores(l), AT["cmp_turn"] + 1: lambda: cmp_maxima(l),
                    AT["cmp_turn_back"]: lambda: cmp_normalise(l), AT["cmp_turn_back"] + 1: lambda: cmp_columns(l),
                    AT["cmp_output"] + 1: lambda: rank_ties(l), AT["turn_selection"] - 1: lambda: rank(l),
                    AT["turn_selection"] + 1: lambda: selection(l), AT["expand"] + 1: lambda: selection_mask(l),
                    AT["win_scores"] + 1: lambda: win_scores(l), AT["win_maxima"] + 1: lambda: on_diagonal(l, 8),
                    AT["win_spread"] + 1: lambda: less_maxima(l, Rw, NW, 9),
                    AT["win_values"]: lambda: col_sums(l, Rw, NW, 3), AT["win_values"] + 1: lambda: win_output(l),
                    AT["mask_0"]: lambda: mask_keys(l, 0), AT["mask_1"]: lambda: mask_keys(l, 1),
                    AT["slc_new"] + 1: lambda: slc_new_scores(l), AT["slc_maxima"] + 1: lambda: on_diagonal(l, 13),
                    AT["slc_spread"] + 1: lambda: slc_less_maxima(l, 0),
                    AT["slc_spread"] + 2: lambda: slc_less_maxima(l, 1),
                    AT["slc_spread"] + 3: lambda: (slc_less_maxima(l, 2), slc_sums(l, 0)),
                    AT["slc_spread"] + 4: lambda: (slc_less_maxima(l, 3), slc_sums(l, 1)),
                    AT["slc_spread"] + 5: lambda: slc_sums(l, 2), AT["slc_spread"] + 6: lambda: slc_sums(l, 3),
                    AT["slc_values"] + 1: lambda: reciprocals(l, 15),
                    AT["slc_values_3"] + 1: lambda: slc_copy(l), AT["slc_turn"] + 1: lambda: slc_output(l), AT["turn_outputs"] + 1: lambda: sample_merge(l)})
                gather_outputs(l)
                gating(l)
                pooling(l)
                turn_rows(l)
                for k in range(KD):
                    dve.wait_ge(cat_rounded, at(l, KD, k + 1))
                    tt(xs[:, 1, k, :], cat[:, k, :], xs[:, 0, k, :].bitcast(F32), ALU.subtract).then_inc(cat_split, 1)
                add_y(l, 1)
                ln(l, 1)
                dve.wait_ge(stored, 16 * at(l, 11, 11))
                own(dve)
                ffn_in(l, 1)
                low_h(l)
                add_y(l, 2)
                ln(l, 2)


def constants():
    f = np.float32
    c = np.zeros((P, NCONST), f)

    def put(n, a):
        o, w = CONST[n]
        a = np.asarray(a, f).reshape(a.shape[0], -1)
        c[:a.shape[0], o:o + w] = a

    p = np.arange(P)
    inv = (10000.0 ** (-np.arange(32) / 32)).astype(f)
    pos = np.stack([t * P + p for t in range(NT)] + [PAST + p % TS], 1).astype(f)
    ang = (pos[:, :, None] * inv).astype(f)
    put("cos", np.cos(ang))
    put("sin", np.sin(ang))
    put("ident", np.eye(P))
    put("ones", np.ones((P, P)))
    q = np.stack([t * P + p for t in range(NT)], 1)
    ok = (16 * np.arange(NC_P) + 31)[None, None] <= q[:, :, None]
    put("cadd", np.where(ok, 0.0, NEG))
    r = np.arange(32)
    put("wadd", np.where(p[:, None] >= (r // 4 % 4)[None], 0.0, NEG))
    r = np.arange(256)
    k = np.arange(32)[:, None]
    put("nadd", np.where((k // 4 == r // 32) & (k % 4 <= r // 4 % 4), 0.0, NEG))
    c0, s0 = 16 * np.arange(P)[:, None], 64 * np.arange(32)[None]
    put("selmap", np.clip(np.minimum(c0 + 32, s0 + 64) - np.maximum(c0, s0), 0, None) / 32)
    s, t = p[:, None], np.arange(143)[None]
    put("band", np.stack([((s <= t) & (s > t - w)) / w - (s == t) for w in WINS], 1))
    t = np.arange(16)[None]
    put("band0", np.stack([((s <= t) & (s > t - w)) / np.minimum(w, t + 1) - (s == t) for w in WINS], 1))
    j, rr = np.arange(120)[:, None], np.arange(32)[None]
    put("bandh", np.stack([((j // 15 == rr // 4) & (j % 15 > rr % 4 + 15 - w)) / w for w in WINS], 1))
    put("bandn", np.stack([((k // 4 == rr // 4) & (k % 4 <= rr % 4) & (k % 4 > rr % 4 - w)) / w - (k == rr)
                           for w in WINS], 1))
    put("tril", s <= p[None])
    put("trils", (k // 4 == rr // 4) & (k <= rr))
    put("idx", np.tile(np.arange(30), (P, 1)))
    put("eps", np.full((P, 1), EPS))
    return c


def kernel(**inputs):
    import ml_dtypes
    import concourse.bacc as _bacc
    from concourse.bass_utils import run_bass_kernel_spmd as _run

    a = {n: np.asarray(v) for n, v in inputs.items()}
    f = np.float32
    L = DEPTH
    tok = np.concatenate([a["x_prompt"].reshape(TP, D), a["x_sample"].reshape(NS, D)])
    arr = {"x_in": tok.T.reshape(KD, P, T).transpose(1, 0, 2)}
    wi = np.zeros((L, NWI, P, 16, P), f)
    win = a["ffn_w_in"].reshape(L, 2, KD, P, 2, KF, P).transpose(0, 1, 5, 3, 4, 2, 6).reshape(L, 2, KF, P, 16, P)
    wi[:, 0:KF], wi[:, KF + 6:] = win[:, 0], win[:, 1]
    wi[:, KF] = a["cmp_w1"].reshape(L, 2, 2, 8, 2, HD, HD).transpose(0, 4, 5, 1, 3, 2, 6).reshape(L, P, 16, P)
    for b in range(32):
        wi[:, KF + 1, b, b // 2, b % 2 * 64:b % 2 * 64 + 64] = 1.0
    order = np.arange(D)
    order[:512] = np.arange(512).reshape(2, 4, HD).transpose(1, 0, 2).reshape(-1)
    wi[:, KF + 2:KF + 6] = a["w_o"][:, order].reshape(L, KD, P, 4, 2, P).transpose(0, 3, 2, 4, 1, 5).reshape(L, 4, P, 16, P)
    wi = wi.reshape(L * NWI, P, 2048)
    arr["wi"] = np.concatenate([wi, wi[0:2]])
    wo = np.zeros((L, NWO, P, KF * P), f)
    wout = a["ffn_w_out"].reshape(L, 2, KF, P, KD, P).transpose(0, 1, 4, 3, 2, 5).reshape(L, 2, KD, P, KF * P)
    wo[:, 0:KD], wo[:, KD + NCH:] = wout[:, 0], wout[:, 1]
    wm = np.zeros((L, D, PJW), f)
    wm[:, :, :a["w_in"].shape[2]] = a["w_in"]
    wm[:, :, :512] = a["w_in"][:, :, order[:512]]
    wo[:, KD:KD + NCH] = wm.reshape(L, KD, P, NCH, CW).transpose(0, 3, 2, 1, 4).reshape(L, NCH, P, KF * P)
    arr["wo"] = wo.reshape(L * NWO, P, KF * P)
    npg = a["cache_kv_cmp"].shape[1]
    arr["cmp_t"] = a["cache_kv_cmp"].reshape(L, npg, 8, 8, 2, 2, 2, HD).transpose(0, 1, 4, 7, 5, 3, 6, 2)\
        .reshape(L * npg, P, 256)
    slc = a["cache_kv_slc"].reshape(L * npg, PAGE, 2, P)
    arr["slc_k"] = slc[:, :, 0].transpose(0, 2, 1)
    arr["slc_v"] = slc[:, :, 1]
    wst = a["state_kv_win"].reshape(L, B, 512, 2, P)
    arr["win_k"] = wst[:, :, :, 0].transpose(0, 3, 1, 2).reshape(L, P, 4096)
    arr["win_v"] = wst[:, :, :, 1].reshape(L, B * NW, P, P).transpose(0, 2, 1, 3).reshape(L, P, 4096)
    arr["win_rows"] = wst.reshape(L, B, 512, 256)
    arr["hist_rows"] = a["state_pool"]
    arr["table"] = a["page_table"].reshape(1, B * NPG).astype(np.int32)
    par = np.zeros((L, P, NPAR), f)

    def put(n, v):
        o, w = PAR[n]
        par[:, :v.shape[1], o:o + w] = v.reshape(L, v.shape[1], w)

    put("ln", np.stack([a["ln_g"], a["ln_b"]], 2).reshape(L, 3, 2, KD, P).transpose(0, 4, 1, 2, 3))
    put("gmgb", np.broadcast_to(np.concatenate([a["gm_ln_g"], a["gm_ln_b"]], 1)[:, None], (L, P, 512)))
    put("ws", a["gm_ws"].transpose(0, 3, 1, 2))
    put("gmb", a["gm_b"].transpose(0, 2, 1))
    wss = np.zeros((L, B, TS, 4, B, TS), f)
    for b in range(B):
        wss[:, b, :, :, b, :] = a["gm_ws"][:, :, :TS, :TS].transpose(0, 3, 1, 2)
    put("wss", wss.reshape(L, NS, P))
    put("gmbs", np.tile(a["gm_b"][:, :, :TS].transpose(0, 2, 1), (1, B, 1)))
    put("pw", a["pool_w"].transpose(0, 2, 1, 3))
    put("ps", a["pool_scale"].reshape(L, 4, HD).transpose(0, 2, 1))
    put("w2", a["cmp_w2"].transpose(0, 2, 1, 3))
    put("pe", a["cmp_pe"].reshape(L, 2, 2, 8, 2, HD).transpose(0, 4, 5, 1, 2, 3).reshape(L, P, 32))
    put("hist", a["state_pool"].reshape(L, B * 15, 256))
    arr["par"] = par
    arr["consts"] = constants()
    q = np.arange(P)
    arr["tri"] = np.stack([np.where(q[None] > q[:, None], NEG, 0.0), np.eye(P)], 1).astype(ml_dtypes.bfloat16)
    outs = {"o_x": (P, KD, T), "o_cmp_p": (L, TP, 256), "o_cmp_s": (L, NS, 256), "o_slc_p": (L, TP, 256),
            "o_slc_s": (L, NS, 256), "o_win_p": (L, TP, 256), "o_win_s": (L, B, 512, 256),
            "o_pool_p": (L, 15, 256), "o_pool_s": (L, B, 15, 256), "o_gv": (L, NS, 256)}
    nc = _bacc.Bacc("TRN2", target_bir_lowering=False, num_devices=1)
    arrays, aps = {}, {}
    for n, v in arr.items():
        v = np.ascontiguousarray(v)
        arrays[n + "_dram"] = v
        aps[n] = nc.dram_tensor(n + "_dram", v.shape, mybir.dt.from_np(v.dtype), kind="ExternalInput").ap()
    for n, s in outs.items():
        aps[n] = nc.dram_tensor(n + "_dram", s, F32, kind="ExternalOutput").ap()
    build(nc, **aps)
    r = _run(nc, [arrays], core_ids=[0]).results[0]
    o = {n: r[n + "_dram"] for n in outs}
    y = o["o_x"].transpose(1, 0, 2).reshape(D, T).T
    kv = lambda n, b, s: o[n].reshape(L, b, s, 2, 2, HD)
    return (y[:TP].reshape(1, TP, D), y[TP:].reshape(B, TS, D), kv("o_cmp_p", 1, TP), kv("o_cmp_s", B, TS),
            kv("o_slc_p", 1, TP), kv("o_slc_s", B, TS), kv("o_win_p", 1, TP), kv("o_win_s", B, 512),
            o["o_pool_p"].reshape(L, 1, 15, 256), o["o_pool_s"], o["o_gv"].reshape(L, B, TS, 256))
```
